# Optimizing a Trainium2 kernel written in Bass

```python
import jax
import jax.numpy as jnp
from jax import lax
import numpy as np

D_MODEL = 1024
BATCH = 1
SEQ = 512
DEPTH = 2

GRID_W = 64
CTX_LEN = 256
HEAD_DIM = 64
FOURIER_WIDTH = D_MODEL // 2
FOURIER_GROUPS = 4
FOURIER_GROUP_DIM = FOURIER_WIDTH // FOURIER_GROUPS
SWA_Q_HEADS = (D_MODEL // 2) // HEAD_DIM
SWA_KV_HEADS = SWA_Q_HEADS // 4
SWA_WINDOW = 128
SWA_BLOCK = 128
NA_HEADS = D_MODEL // HEAD_DIM
NA_ROWS_MAX = 8
NA_COLS = 16
N_EXPERTS = 16
EXPERT_FF = D_MODEL
EC_CAPACITY_FACTOR = 2
ROPE_BASE = 10000.0
EPS = 1e-6
N_EVEN = (DEPTH + 1) // 2
N_ODD = DEPTH // 2
EVEN_IN_WIDTH = FOURIER_WIDTH + (SWA_Q_HEADS + 2 * SWA_KV_HEADS) * HEAD_DIM
EVEN_OUT_WIDTH = FOURIER_WIDTH + SWA_Q_HEADS * HEAD_DIM
ODD_WIDTH = NA_HEADS * HEAD_DIM

kernel_name = 'hybrid_fourier_swa_natten_ecmoe_dit'

def rms_norm(x, gain):
    xf = x.astype(jnp.float32)
    y = xf * lax.rsqrt(jnp.mean(xf * xf, axis=-1, keepdims=True) + EPS)
    return (y * gain.astype(jnp.float32)).astype(x.dtype)

def modulate(h, shift, scale):
    return h * (1 + scale) + shift

def axial_rope(n_tokens):
    t = jnp.arange(n_tokens)
    row = (t // GRID_W).astype(jnp.float32)
    col = (t % GRID_W).astype(jnp.float32)
    n_freq = HEAD_DIM // 4
    inv_freq = jnp.power(ROPE_BASE, -jnp.arange(n_freq, dtype=jnp.float32) / n_freq)
    ang = jnp.concatenate([row[:, None] * inv_freq, col[:, None] * inv_freq], axis=-1)
    return jnp.cos(ang), jnp.sin(ang)

def apply_rope(x, cos, sin):
    xf = x.astype(jnp.float32)
    x1, x2 = jnp.split(xf, 2, axis=-1)
    c = cos[None, :, None, :]
    s = sin[None, :, None, :]
    return jnp.concatenate([x1 * c - x2 * s, x1 * s + x2 * c], axis=-1).astype(x.dtype)

def fourier_mix(u):
    y = jnp.fft.fft2(u.astype(jnp.float32), axes=(1, 3), norm='ortho')
    return jnp.real(y).astype(u.dtype)

def ctx_attention(q, k, v, sink):
    n_k = k.shape[1]
    s = jnp.einsum('bqhgd,bkhd->bhgqk', q, k).astype(jnp.float32) * (HEAD_DIM ** -0.5)
    if sink is not None:
        sk = jnp.broadcast_to(sink.astype(jnp.float32)[None, :, :, None, None], s.shape[:-1] + (1,))
        s = jnp.concatenate([s, sk], axis=-1)
    p = jax.nn.softmax(s, axis=-1)[..., :n_k].astype(v.dtype)
    return jnp.einsum('bhgqk,bkhd->bqhgd', p, v)

def swa_latent(q, k, v, k_ctx, v_ctx, sink):
    bsz, n, n_kv, grp, dh = q.shape
    n_ctx = k_ctx.shape[1]
    n_blk = n // SWA_BLOCK
    span = SWA_BLOCK + 2 * SWA_WINDOW
    pad = ((0, 0), (SWA_WINDOW, SWA_WINDOW), (0, 0), (0, 0))
    k_pad = jnp.pad(k, pad)
    v_pad = jnp.pad(v, pad)
    scale = HEAD_DIM ** -0.5
    sink_logit = jnp.broadcast_to(sink.astype(jnp.float32)[None, :, :, None, None],
                                  (bsz, n_kv, grp, SWA_BLOCK, 1))

    def block(i):
        q0 = i * SWA_BLOCK
        qb = lax.dynamic_slice_in_dim(q, q0, SWA_BLOCK, axis=1)
        kb = lax.dynamic_slice_in_dim(k_pad, q0, span, axis=1)
        vb = lax.dynamic_slice_in_dim(v_pad, q0, span, axis=1)
        s_ctx = jnp.einsum('bqhgd,bkhd->bhgqk', qb, k_ctx).astype(jnp.float32) * scale
        s_loc = jnp.einsum('bqhgd,bkhd->bhgqk', qb, kb).astype(jnp.float32) * scale
        q_pos = q0 + jnp.arange(SWA_BLOCK)
        k_pos = q0 - SWA_WINDOW + jnp.arange(span)
        valid = ((jnp.abs(q_pos[:, None] - k_pos[None, :]) <= SWA_WINDOW)
                 & (k_pos >= 0)[None, :] & (k_pos < n)[None, :])
        s_loc = jnp.where(valid, s_loc, -jnp.inf)
        p = jax.nn.softmax(jnp.concatenate([s_ctx, s_loc, sink_logit], axis=-1), axis=-1)
        p_ctx = p[..., :n_ctx].astype(v.dtype)
        p_loc = p[..., n_ctx:n_ctx + span].astype(v.dtype)
        return (jnp.einsum('bhgqk,bkhd->bqhgd', p_ctx, v_ctx)
                + jnp.einsum('bhgqk,bkhd->bqhgd', p_loc, vb))

    out = lax.map(block, jnp.arange(n_blk))
    return jnp.moveaxis(out, 0, 1).reshape(bsz, n, n_kv, grp, dh)

def na_latent(q, k, v, k_ctx, v_ctx, rpb):
    bsz, n, nh, dh = q.shape
    n_ctx = k_ctx.shape[1]
    rows = n // GRID_W
    kh = min(NA_ROWS_MAX, rows)
    kw = NA_COLS
    scale = HEAD_DIM ** -0.5
    q_g = q.reshape(bsz, rows, GRID_W, nh, dh)
    k_g = k.reshape(bsz, rows, GRID_W, nh, dh)
    v_g = v.reshape(bsz, rows, GRID_W, nh, dh)
    col_q = jnp.arange(GRID_W)
    col_k = jnp.arange(GRID_W)
    c_start = jnp.clip(col_q - kw // 2, 0, GRID_W - kw)
    col_valid = (col_k[None, :] >= c_start[:, None]) & (col_k[None, :] < c_start[:, None] + kw)
    dc_idx = jnp.clip(col_k[None, :] - col_q[:, None] + NA_COLS - 1, 0, 2 * NA_COLS - 2)
    rpb_f = rpb.astype(jnp.float32)

    def row_block(r):
        r_start = jnp.clip(r - kh // 2, 0, rows - kh)
        qb = lax.dynamic_index_in_dim(q_g, r, axis=1, keepdims=False)
        kb = lax.dynamic_slice_in_dim(k_g, r_start, kh, axis=1)
        vb = lax.dynamic_slice_in_dim(v_g, r_start, kh, axis=1)
        dr_idx = r_start + jnp.arange(kh) - r + NA_ROWS_MAX - 1
        bias = jnp.take(rpb_f, dr_idx, axis=1)[:, :, dc_idx]
        bias = jnp.transpose(bias, (0, 2, 1, 3))
        s_loc = jnp.einsum('bqhd,brkhd->bhqrk', qb, kb).astype(jnp.float32) * scale + bias
        s_loc = jnp.where(col_valid[:, None, :], s_loc, -jnp.inf).reshape(bsz, nh, GRID_W, kh * GRID_W)
        s_ctx = jnp.einsum('bqhd,bkhd->bhqk', qb, k_ctx).astype(jnp.float32) * scale
        p = jax.nn.softmax(jnp.concatenate([s_ctx, s_loc], axis=-1), axis=-1).astype(v.dtype)
        p_loc = p[..., n_ctx:].reshape(bsz, nh, GRID_W, kh, GRID_W)
        return (jnp.einsum('bhqk,bkhd->bqhd', p[..., :n_ctx], v_ctx)
                + jnp.einsum('bhqrk,brkhd->bqhd', p_loc, vb))

    out = lax.map(row_block, jnp.arange(rows))
    return jnp.moveaxis(out, 0, 1).reshape(bsz, n, nh, dh)

def expert_choice_ffn(h, w_router, w_gate, w_up, w_down):
    bsz, n, _ = h.shape
    cap = EC_CAPACITY_FACTOR * n // N_EXPERTS
    aff = jax.nn.softmax(jnp.einsum('bnd,de->bne', h, w_router).astype(jnp.float32), axis=-1)
    gate, idx = lax.top_k(jnp.swapaxes(aff, 1, 2), cap)
    b_idx = jnp.arange(bsz)[:, None, None]
    xs = h[b_idx, idx]
    a = jnp.einsum('becd,edf->becf', xs, w_gate)
    u = jnp.einsum('becd,edf->becf', xs, w_up)
    y = jnp.einsum('becf,efd->becd', jax.nn.silu(a) * u, w_down) * gate[..., None].astype(h.dtype)
    return jnp.zeros_like(h).at[b_idx, idx].add(y)

def split_heads(t, nh):
    return t.reshape(t.shape[0], t.shape[1], nh, HEAD_DIM)

def even_mixer(h_x, h_c, w_in, w_out, q_gain, k_gain, sink, cos, sin, ctx_out):
    bsz, n, _ = h_x.shape
    n_ctx = h_c.shape[1]
    dq = SWA_Q_HEADS * HEAD_DIM
    dkv = SWA_KV_HEADS * HEAD_DIM
    grp = SWA_Q_HEADS // SWA_KV_HEADS
    cuts = [FOURIER_WIDTH, FOURIER_WIDTH + dq, FOURIER_WIDTH + dq + dkv]
    sink_g = sink.reshape(SWA_KV_HEADS, grp)
    f_x, q_x, k_x, v_x = jnp.split(h_x @ w_in, cuts, axis=-1)
    q_x = apply_rope(rms_norm(split_heads(q_x, SWA_Q_HEADS), q_gain), cos, sin)
    k_x = apply_rope(rms_norm(split_heads(k_x, SWA_KV_HEADS), k_gain), cos, sin)
    v_x = split_heads(v_x, SWA_KV_HEADS)
    if ctx_out:
        f_c, q_c, k_c, v_c = jnp.split(h_c @ w_in, cuts, axis=-1)
    else:
        k_c, v_c = jnp.split(h_c @ w_in[:, FOURIER_WIDTH + dq:], [dkv], axis=-1)
    k_c = rms_norm(split_heads(k_c, SWA_KV_HEADS), k_gain)
    v_c = split_heads(v_c, SWA_KV_HEADS)
    a_x = swa_latent(q_x.reshape(bsz, n, SWA_KV_HEADS, grp, HEAD_DIM), k_x, v_x, k_c, v_c, sink_g)
    four_x = fourier_mix(f_x.reshape(bsz, n, FOURIER_GROUPS, FOURIER_GROUP_DIM))
    y_x = jnp.concatenate([four_x.reshape(bsz, n, FOURIER_WIDTH), a_x.reshape(bsz, n, dq)], axis=-1) @ w_out
    if not ctx_out:
        return y_x, None
    q_c = rms_norm(split_heads(q_c, SWA_Q_HEADS), q_gain).reshape(bsz, n_ctx, SWA_KV_HEADS, grp, HEAD_DIM)
    a_c = ctx_attention(q_c, k_c, v_c, sink_g)
    four_c = fourier_mix(f_c.reshape(bsz, n_ctx, FOURIER_GROUPS, FOURIER_GROUP_DIM))
    y_c = jnp.concatenate([four_c.reshape(bsz, n_ctx, FOURIER_WIDTH), a_c.reshape(bsz, n_ctx, dq)], axis=-1) @ w_out
    return y_x, y_c

def odd_mixer(h_x, h_c, w_in, w_out, q_gain, k_gain, rpb, ctx_out):
    bsz, n, _ = h_x.shape
    n_ctx = h_c.shape[1]
    q_x, k_x, v_x = jnp.split(h_x @ w_in, [ODD_WIDTH, 2 * ODD_WIDTH], axis=-1)
    q_x = rms_norm(split_heads(q_x, NA_HEADS), q_gain)
    k_x = rms_norm(split_heads(k_x, NA_HEADS), k_gain)
    v_x = split_heads(v_x, NA_HEADS)
    if ctx_out:
        q_c, k_c, v_c = jnp.split(h_c @ w_in, [ODD_WIDTH, 2 * ODD_WIDTH], axis=-1)
    else:
        k_c, v_c = jnp.split(h_c @ w_in[:, ODD_WIDTH:], [ODD_WIDTH], axis=-1)
    k_c = rms_norm(split_heads(k_c, NA_HEADS), k_gain)
    v_c = split_heads(v_c, NA_HEADS)
    a_x = na_latent(q_x, k_x, v_x, k_c, v_c, rpb)
    y_x = a_x.reshape(bsz, n, ODD_WIDTH) @ w_out
    if not ctx_out:
        return y_x, None
    q_c = rms_norm(split_heads(q_c, NA_HEADS), q_gain).reshape(bsz, n_ctx, NA_HEADS, 1, HEAD_DIM)
    a_c = ctx_attention(q_c, k_c, v_c, None)
    y_c = a_c.reshape(bsz, n_ctx, ODD_WIDTH) @ w_out
    return y_x, y_c

def setup_inputs(seed: int = 0) -> dict:
    key = jax.random.key(seed)
    ks = jax.random.split(key, 24)
    D = D_MODEL

    def nrm(k, shape, s):
        return jax.random.normal(k, shape, jnp.float32) * s

    return {
        'x': nrm(ks[0], (BATCH, SEQ, D), 1.0),
        'c': nrm(ks[1], (BATCH, D), 1.0),
        'ctx': nrm(ks[2], (BATCH, CTX_LEN, D), 1.0),
        'c_ctx': nrm(ks[3], (D,), 1.0),
        'ada_w': nrm(ks[4], (DEPTH, D, 6 * D), 0.5 * D ** -0.5),
        'ada_b': nrm(ks[5], (DEPTH, 6 * D), 0.02),
        'norm1_g': 1.0 + nrm(ks[6], (DEPTH, D), 0.05),
        'norm2_g': 1.0 + nrm(ks[7], (DEPTH, D), 0.05),
        'router_w': nrm(ks[8], (DEPTH, D, N_EXPERTS), D ** -0.5),
        'exp_w_gate': nrm(ks[9], (DEPTH, N_EXPERTS, D, EXPERT_FF), D ** -0.5),
        'exp_w_up': nrm(ks[10], (DEPTH, N_EXPERTS, D, EXPERT_FF), D ** -0.5),
        'exp_w_down': nrm(ks[11], (DEPTH, N_EXPERTS, EXPERT_FF, D), EXPERT_FF ** -0.5),
        'ev_w_in': nrm(ks[12], (N_EVEN, D, EVEN_IN_WIDTH), D ** -0.5),
        'ev_w_out': nrm(ks[13], (N_EVEN, EVEN_OUT_WIDTH, D), EVEN_OUT_WIDTH ** -0.5),
        'ev_q_gain': 1.0 + nrm(ks[14], (N_EVEN, HEAD_DIM), 0.05),
        'ev_k_gain': 1.0 + nrm(ks[15], (N_EVEN, HEAD_DIM), 0.05),
        'ev_sink': nrm(ks[16], (N_EVEN, SWA_Q_HEADS), 1.0),
        'od_w_in': nrm(ks[17], (N_ODD, D, 3 * ODD_WIDTH), D ** -0.5),
        'od_w_out': nrm(ks[18], (N_ODD, ODD_WIDTH, D), ODD_WIDTH ** -0.5),
        'od_q_gain': 1.0 + nrm(ks[19], (N_ODD, HEAD_DIM), 0.05),
        'od_k_gain': 1.0 + nrm(ks[20], (N_ODD, HEAD_DIM), 0.05),
        'od_rpb': nrm(ks[21], (N_ODD, NA_HEADS, 2 * NA_ROWS_MAX - 1, 2 * NA_COLS - 1), 0.1),
    }

def reference(x, c, ctx, c_ctx, ada_w, ada_b, norm1_g, norm2_g, router_w, exp_w_gate, exp_w_up,
              exp_w_down, ev_w_in, ev_w_out, ev_q_gain, ev_k_gain, ev_sink, od_w_in, od_w_out,
              od_q_gain, od_k_gain, od_rpb):
    n = x.shape[1]
    cos, sin = axial_rope(n)
    for layer in range(DEPTH):
        last = layer == DEPTH - 1
        j = layer // 2
        mod_x = jnp.split(jax.nn.silu(c) @ ada_w[layer] + ada_b[layer], 6, axis=-1)
        mod_c = jnp.split(jax.nn.silu(c_ctx) @ ada_w[layer] + ada_b[layer], 6, axis=-1)
        sh1, sc1, g1, sh2, sc2, g2 = [m[:, None, :] for m in mod_x]
        csh1, csc1, cg1, csh2, csc2, cg2 = mod_c
        h_x = modulate(rms_norm(x, norm1_g[layer]), sh1, sc1)
        h_c = modulate(rms_norm(ctx, norm1_g[layer]), csh1, csc1)
        if layer % 2 == 0:
            y_x, y_c = even_mixer(h_x, h_c, ev_w_in[j], ev_w_out[j], ev_q_gain[j], ev_k_gain[j],
                                  ev_sink[j], cos, sin, not last)
        else:
            y_x, y_c = odd_mixer(h_x, h_c, od_w_in[j], od_w_out[j], od_q_gain[j], od_k_gain[j],
                                 od_rpb[j], not last)
        x = x + g1 * y_x
        h_x = modulate(rms_norm(x, norm2_g[layer]), sh2, sc2)
        x = x + g2 * expert_choice_ffn(h_x, router_w[layer], exp_w_gate[layer], exp_w_up[layer],
                                       exp_w_down[layer])
        if not last:
            ctx = ctx + cg1 * y_c
            h_c = modulate(rms_norm(ctx, norm2_g[layer]), csh2, csc2)
            ctx = ctx + cg2 * expert_choice_ffn(h_c, router_w[layer], exp_w_gate[layer], exp_w_up[layer],
                                                exp_w_down[layer])
    return x


_drawn_inputs = setup_inputs


def setup_inputs(seed=0):
    import zlib

    import numpy as np

    out = dict(_drawn_inputs(seed))
    spreads = {}
    factors = {'ada_b': 3.022,
     'norm1_g': 5.443,
     'norm2_g': 3.651,
     'ev_q_gain': 8.0,
     'ev_k_gain': 8.0,
     'ev_sink': 8.0,
     'od_q_gain': 8.0,
     'od_k_gain': 8.0,
     'od_rpb': 8.0}
    for name, (base, spread) in spreads.items():
        noise = np.random.default_rng([zlib.crc32(name.encode()), seed]).standard_normal(out[name].shape)
        drawn = base * np.exp(spread * noise) if base else spread * noise
        out[name] = jnp.asarray(drawn.astype(out[name].dtype))
    for name, factor in factors.items():
        out[name] = (out[name] * factor).astype(out[name].dtype)
    return out
```

```python
from contextlib import ExitStack

import numpy as np

import concourse.bass as bass
from concourse import mybir

F32 = mybir.dt.float32
BF16 = mybir.dt.bfloat16
U32 = mybir.dt.uint32
ACT = mybir.ActivationFunctionType
ALU = mybir.AluOpType
AX = mybir.AxisListType

P = 128
D = 1024
KT = D // P
SEQ, CTX = 512, 256
XT, CT = SEQ // P, CTX // P
TT = XT + CT
TOK = SEQ + CTX
LAYERS = 2
HD = 64
GRID_W = 64
ROWS = SEQ // GRID_W
FW = D // 2
FG = FW // P
QH, KVH = 8, 2
QK0 = (QH + KVH) * HD
EV_IN = FW + QK0 + KVH * HD
NH = D // HD
NA_COLS = 16
RPB_R, RPB_C = 2 * 8 - 1, 2 * NA_COLS - 1
RPB_PAD = 48
EXPERTS = 16
CAPX, CAPC = 2 * SEQ // EXPERTS, 2 * CTX // EXPERTS
SLOT = 1024
SLOTS = 24
EPS = 1e-6
SH1, SC1, G1, SH2, SC2, G2 = range(6)

ARENA = 21504
HT_AT = 0
AB_AT = 6656
HB_AT = 10752
FT_AT, QKV_AT = 12800, 15872
QN_AT, TMP_AT, QT_AT, KT0_AT = 0, 3840, 6656, 9728
GAIN_AT = 10496
FOUR_AT = FT_AT
AT0_AT, P0_AT, PT0_AT = 0, 3072, 10496
QT1_AT, TM1_AT, KT1_AT = 6656, 10752, 12800
AT1_AT, BM1_AT, BR1_AT, P1_AT, BM1B_AT, PT1_AT = 0, 4096, 5632, 10752, 18944, 20480
GB_AT, YT_AT = 16384, 18432
ACC_AT = 0


def program(nc, x, c, ctx, c_ctx, ada_w, ada_b, norm1_g, norm2_g, router_w, exp_w_gate, exp_w_up,
            exp_w_down, ev_w_in, ev_w_out, ev_q_gain, ev_k_gain, ev_sink, od_w_in, od_w_out,
            od_q_gain, od_k_gain, rpb_pad, dft, rope, ident_in, swa_mask_in, na_mask_in,
            iota_in, out, upto=99, taps=()):
    stack = ExitStack()
    with stack:
        def sb(name, shape, dt=F32):
            return stack.enter_context(nc.sbuf_tensor(name, shape, dt))

        sems = {}

        def sem(name):
            if name not in sems:
                sems[name] = nc.alloc_semaphore(name=name)
            return sems[name]

        def view(t, col, *dims, p=0, n=P):
            row = t.shape[1] if len(t.shape) == 2 else int(np.prod(t.shape[1:]))
            return bass.AP(t, p * row + col, [[row, n], *[list(d) for d in dims]])

        resid = sb("resid", [P, TT * D])
        ring = sb("ring", [P, SLOTS * SLOT])
        arena = sb("arena", [P, ARENA])
        ident = sb("ident", [P, P])
        ident16 = sb("ident16", [P, P], BF16)
        swa_mask = sb("swa_mask", [P, 2 * P], BF16)
        router = sb("router", [P, KT * EXPERTS])
        small = sb("small", [P, 432])
        offs = sb("offs", [P, 2 * (EXPERTS + 1)], U32)
        ps = stack.enter_context(nc.psum_tensor("ps", [P, 8 * 512], F32))

        def bank(b, col=0, *dims, p=0, n=P):
            return view(ps, b * 512 + col, *(dims or ((1, 512),)), p=p, n=n)

        mods = nc.dram_tensor("mods", [LAYERS * 2, 6 * D], F32, kind="Internal").ap()
        h2x = nc.dram_tensor("h2x", [SEQ, D], F32, kind="Internal").ap()
        h2c = nc.dram_tensor("h2c", [CTX, D], F32, kind="Internal").ap()

        def mod_row(layer, stream, vec):
            return mods[2 * layer + stream, vec * D:(vec + 1) * D].partition_broadcast(P)

        def ring_load(eng, slot, cols, src, done):
            k = src.shape[0] // P
            eng.dma_start(view(ring, slot * SLOT, (cols, k), (1, cols)),
                          src.rearrange("(k p) n -> p k n", p=P)).then_inc(done, 16)

        SS, QSS, SINK, SOFT = 0, 8, 72, 96
        MISC = 300

        def ada_stage():
            HALF = 3 * SLOT
            GROUPS = 4
            steps = [(layer, k) for layer in range(LAYERS) for k in range(KT)]
            CIN, BIAS, GAIN, MOD, MASK = 0, 64, 4096, 8192, 11520
            with nc.Block() as block:
                @block.sync
                def _(sp):
                    for s, src in enumerate((c, c_ctx)):
                        sp.dma_start(view(arena, CIN + s * KT, (1, KT)),
                                     src.rearrange("(p k) -> p k", k=KT)).then_inc(sem("c_in"), 16)
                    for i, (layer, k) in enumerate(steps):
                        if i >= GROUPS:
                            sp.wait_ge(sem("ada_used"), i - GROUPS + 1)
                        sp.dma_start(view(ring, (i % GROUPS) * 6 * SLOT, (1, 6 * D)),
                                     ada_w[layer].rearrange("(p k) n -> k p n", k=KT)[k]
                                     ).then_inc(sem(f"ada_in{i % GROUPS}"), 16)
                        if i == 3:
                            for layer2 in range(LAYERS):
                                for g in range(4):
                                    sp.dma_start(view(arena, BIAS + layer2 * 1536, (512, 3), (1, 512), p=32 * g, n=2),
                                                 ada_b[layer2].rearrange("(b g n) -> g b n", g=4, n=512)[g]
                                                 .partition_broadcast(2)).then_inc(sem("bias_in"), 16)
                                    gain, at = (norm2_g, g) if g < 2 else (norm1_g, g - 2)
                                    sp.dma_start(view(arena, GAIN + layer2 * 512, (1, 512), p=32 * g, n=2),
                                                 gain[layer2, at * 512:(at + 1) * 512].partition_broadcast(2)
                                                 ).then_inc(sem("bias_in"), 16)
                    sp.dma_start(view(resid, 0, (D, XT), (1, D)),
                                 x[0].rearrange("(t p) d -> p t d", p=P)).then_inc(sem("x_in"), 16)
                    sp.dma_start(view(resid, XT * D, (D, CT), (1, D)),
                                 ctx[0].rearrange("(t p) d -> p t d", p=P)).then_inc(sem("x_in"), 16)
                    sp.dma_start(ident[:, :], ident_in).then_inc(sem("const_in"), 16)
                    sp.dma_start(view(arena, MASK, (1, 2 * P)), swa_mask_in).then_inc(sem("const_in"), 16)
                    sp.dma_start(view(small, SINK, (1, QH)), ev_sink[0].partition_broadcast(P)
                                 ).then_inc(sem("const_in"), 16)
                    sp.wait_ge(sem("ada_used"), len(steps))
                    for k in range(KT):
                        sp.dma_start(view(ring, k * EV_IN, (1, EV_IN)), ev_w_in[0, k * P:(k + 1) * P, :]
                                     ).then_inc(sem("evin_in"), 16)
                    for s in range(2):
                        sp.dma_start(view(ring, 10 * SLOT + s * 2048, (512, 4), (1, 512)),
                                     dft[s].rearrange("(t p) m -> p t m", p=P)).then_inc(sem("dft_in"), 16)
                    for k in range(4):
                        sp.dma_start(view(ring, (14 + k) * SLOT, (1, D)), ev_w_out[0, k * P:(k + 1) * P, :]
                                     ).then_inc(sem("evout_in"), 16)
                    for pr in range(4):
                        for a in range(2):
                            r0 = FW + (pr + 4 * a) * HD
                            sp.dma_start(view(ring, (18 + pr) * SLOT, (1, D), p=64 * a, n=64),
                                         ev_w_out[0, r0:r0 + HD, :]).then_inc(sem("evout_in"), 16)
                    for layer in range(LAYERS):
                        for g in range(4):
                            sp.wait_ge(sem("mod_ready"), (layer * 4 + g + 1))
                            sp.dma_start(mods[2 * layer:2 * layer + 2, :].rearrange("s (b g n) -> g s b n", g=4, n=512)[g],
                                         view(arena, MOD + layer * 1536, (512, 3), (1, 512), p=32 * g, n=2)
                                         ).then_inc(sem("mods_out"), 16)
                    sp.wait_ge(sem("mods_out"), 16 * 8)

                @block.scalar
                def _(act):
                    act.wait_ge(sem("c_in"), 32)
                    nc.scalar.activation(view(arena, CIN + 32, (1, 16)), view(arena, CIN, (1, 16)),
                                         ACT.Silu).then_inc(sem("silu_c"), 1)

                @block.tensor
                def _(pe):
                    pe.wait_ge(sem("silu_c"), 1)
                    for i, (layer, k) in enumerate(steps):
                        pe.wait_ge(sem(f"ada_in{i % GROUPS}"), 16 * (i // GROUPS + 1))
                        for b in range(3):
                            for g in range(4):
                                last = nc.tensor.matmul(
                                    bank(layer * 3 + b, 0, (1, 512), p=32 * g, n=2),
                                    view(arena, CIN + 32 + k, (KT, 2)),
                                    view(ring, (i % GROUPS) * 6 * SLOT + (b * 4 + g) * 512, (1, 512)),
                                    start=(k == 0), stop=(k == KT - 1))
                        last.then_inc(sem("ada_used"), 1)

                @block.vector
                def _(dve):
                    dve.wait_ge(sem("bias_in"), 16 * 16)
                    for layer in range(LAYERS):
                        dve.wait_ge(sem("ada_used"), KT * (layer + 1))
                        for g in range(4):
                            mod = view(arena, MOD + layer * 1536, (1, 1536), p=32 * g, n=2)
                            nc.vector.tensor_tensor(mod, bank(layer * 3, 0, (1, 1536), p=32 * g, n=2),
                                                    view(arena, BIAS + layer * 1536, (1, 1536), p=32 * g, n=2),
                                                    ALU.add).then_inc(sem("mod_sum"), 1)
                            dve.wait_ge(sem("mod_sum"), layer * 4 + g + 1)
                            part = view(arena, MOD + layer * 1536 + (1024 if g < 2 else 0), (1, 512), p=32 * g, n=2)
                            nc.vector.scalar_tensor_tensor(part, part, 1.0,
                                                           view(arena, GAIN + layer * 512, (1, 512), p=32 * g, n=2),
                                                           ALU.add, ALU.mult).then_inc(sem("mod_ready"), 1)
                    dve.wait_ge(sem("const_in"), 48)
                    nc.vector.tensor_copy(ident16[:, :], ident[:, :])
                    nc.vector.tensor_copy(swa_mask[:, :], view(arena, MASK, (1, 2 * P)))

        def norm_stage(layer, which, tiles, prefetch=None):
            n = f"{layer}{which}"
            width = 832 if (layer, which) == (1, 1) else TOK
            blocked = width == 832
            streams = 2 if tiles == TT else 1

            def hb(t):
                return view(arena, HB_AT + (t % 2) * D, (1, D))

            def res(t):
                return view(resid, t * D, (1, D))

            def ab(stream, vec):
                return view(arena, AB_AT + (2 * stream + vec) * D, (1, D))

            LG = SOFT
            AFF_T = HB_AT
            with nc.Block() as block:
                @block.sync
                def _(sp):
                    sc, sh = (SC1, SH1) if which == 1 else (SC2, SH2)
                    for s in range(streams):
                        for v, vec in enumerate((sc, sh)):
                            sp.dma_start(ab(s, v), mod_row(layer, s, vec)).then_inc(sem("ab_in" + n), 16)
                    if which == 2:
                        sp.dma_start(view(router, 0, (EXPERTS, KT), (1, EXPERTS)),
                                     router_w[layer].rearrange("(k p) e -> p k e", p=P)).then_inc(sem("rt_in" + n), 16)
                    if prefetch:
                        prefetch(sp)
                    if which == 2:
                        for t in range(tiles):
                            sp.wait_ge(sem("h_ready" + n), t + 1)
                            dst = h2x[t * P:(t + 1) * P, :] if t < XT else h2c[(t - XT) * P:(t - XT + 1) * P, :]
                            sp.dma_start(dst, hb(t)).then_inc(sem(f"h_saved{n}{t % 2}"), 16)
                        for par in range(2):
                            sp.wait_ge(sem(f"h_saved{n}{par}"), 16 * (tiles // 2))

                @block.scalar
                def _(act):
                    if (layer, which) == (0, 1):
                        act.wait_ge(sem("x_in"), 32)
                    for t in range(tiles):
                        if t >= 2:
                            act.wait_ge(sem("sq_done" + n), t - 1)
                        nc.scalar.activation(hb(t), res(t), ACT.Square,
                                             accum_out=view(small, SS + t, (1, 1))).then_inc(sem("sq_done" + n), 1)
                    act.wait_ge(sem("var_ready" + n), 1)
                    nc.scalar.activation(view(small, SS, (1, tiles)), view(small, SS, (1, tiles)), ACT.Sqrt
                                         ).then_inc(sem("std_ready" + n), 1)
                    for t in range(tiles):
                        act.wait_ge(sem("hT_ps" + n), t + 1)
                        b0 = 2 * (t % 2)
                        if blocked and t < XT:
                            for r in range(2):
                                for half in range(2):
                                    last = nc.scalar.activation(
                                        view(arena, HT_AT + 4 * half * width + (2 * t + r) * 8,
                                             (width, 4), (64, 8), (1, 8)),
                                        bank(b0 + half, r * 64, (P, 4), (8, 8), (1, 8)), ACT.Copy)
                        else:
                            at = t * P + (64 if blocked else 0)
                            last = nc.scalar.activation(view(arena, HT_AT + at, (width, KT), (1, P)),
                                                        bank(b0, 0, (P, KT), (1, P)), ACT.Copy)
                        last.then_inc(sem("hT_out" + n), 1)
                    if which == 2:
                        act.wait_ge(sem("lg_shift" + n), 1)
                        nc.scalar.activation(view(small, LG, (1, tiles * EXPERTS)), view(small, LG, (1, tiles * EXPERTS)),
                                             ACT.Exp).then_inc(sem("lg_exp" + n), 1)

                @block.vector
                def _(dve):
                    dve.wait_ge(sem("sq_done" + n), tiles)
                    s = view(small, SS, (1, tiles))
                    nc.vector.tensor_scalar(s, s, 1.0 / D, EPS, ALU.mult, ALU.add).then_inc(sem("var_ready" + n), 1)
                    dve.wait_ge(sem("std_ready" + n), 1)
                    nc.vector.reciprocal(s, s).then_inc(sem("rstd_ready" + n), 1)
                    dve.wait_ge(sem("rstd_ready" + n), 1)
                    dve.wait_ge(sem("ab_in" + n), 32 * streams)
                    for t in range(tiles):
                        stream = 0 if t < XT else 1
                        if t >= 2:
                            dve.wait_ge(sem("hT_ps" + n), t - 1)
                            if which == 2:
                                dve.wait_ge(sem(f"h_saved{n}{t % 2}"), 16 * (t // 2))
                        nc.vector.scalar_tensor_tensor(hb(t), res(t), view(small, SS + t, (1, 1)), ab(stream, 0),
                                                       ALU.mult, ALU.mult).then_inc(sem("h_scaled" + n), 1)
                        dve.wait_ge(sem("h_scaled" + n), t + 1)
                        nc.vector.tensor_tensor(hb(t), hb(t), ab(stream, 1), ALU.add).then_inc(sem("h_ready" + n), 1)
                    if blocked:
                        dve.wait_ge(sem("hT_out" + n), XT)
                        nc.vector.tensor_copy(view(arena, HT_AT + SEQ, (width, KT), (1, 64)),
                                              view(arena, HT_AT, (width, KT), (1, 64))).then_inc(sem("wrap" + n), 1)
                    if which == 2:
                        lg = view(small, LG, (EXPERTS, tiles), (1, EXPERTS))
                        mx = view(small, MISC, (1, tiles))
                        dve.wait_ge(sem("lg_ps" + n), 1)
                        nc.vector.tensor_reduce(mx, bank(4, 0, (EXPERTS, tiles), (1, EXPERTS)), AX.X, ALU.max
                                                ).then_inc(sem("lg_step" + n), 1)
                        dve.wait_ge(sem("lg_step" + n), 1)
                        nc.vector.tensor_tensor(lg, bank(4, 0, (EXPERTS, tiles), (1, EXPERTS)),
                                                view(small, MISC, (1, tiles), (0, EXPERTS)), ALU.subtract
                                                ).then_inc(sem("lg_shift" + n), 1)
                        dve.wait_ge(sem("lg_exp" + n), 1)
                        nc.vector.tensor_reduce(view(small, MISC + 8, (1, tiles)), lg, AX.X, ALU.add
                                                ).then_inc(sem("lg_step" + n), 1)
                        dve.wait_ge(sem("lg_step" + n), 2)
                        nc.vector.reciprocal(view(small, MISC + 16, (1, tiles)), view(small, MISC + 8, (1, tiles))
                                             ).then_inc(sem("lg_step" + n), 1)
                        dve.wait_ge(sem("lg_step" + n), 3)
                        nc.vector.tensor_tensor(lg, lg, view(small, MISC + 16, (1, tiles), (0, EXPERTS)), ALU.mult
                                                ).then_inc(sem("aff_ready" + n), 1)
                        dve.wait_ge(sem("affT_ps" + n), 1)
                        for par in range(2):
                            dve.wait_ge(sem(f"h_saved{n}{par}"), 16 * (tiles // 2))
                        nc.vector.tensor_copy(view(arena, AFF_T, (1, tiles * P), n=EXPERTS),
                                              bank(5, 0, (1, tiles * P), n=EXPERTS)).then_inc(sem("affT" + n), 1)

                @block.tensor
                def _(pe):
                    if (layer, which) == (0, 1):
                        pe.wait_ge(sem("const_in"), 48)
                    for t in range(tiles):
                        pe.wait_ge(sem("h_ready" + n), t + 1)
                        if t >= 2:
                            pe.wait_ge(sem("hT_out" + n), t - 1)
                        for k in range(KT):
                            last = nc.tensor.transpose(bank(2 * (t % 2), k * P, (1, P)),
                                                       view(arena, HB_AT + (t % 2) * D + k * P, (1, P)), ident[:, :])
                        last.then_inc(sem("hT_ps" + n), 1)
                    if which == 2:
                        pe.wait_ge(sem("rt_in" + n), 16)
                        for t in range(tiles):
                            pe.wait_ge(sem("hT_out" + n), t + 1)
                            for k in range(KT):
                                last = nc.tensor.matmul(bank(4, t * EXPERTS, (1, EXPERTS)),
                                                        view(arena, HT_AT + k * width + t * P, (1, P)),
                                                        view(router, k * EXPERTS, (1, EXPERTS)),
                                                        start=(k == 0), stop=(k == KT - 1))
                        last.then_inc(sem("lg_ps" + n), 1)
                        pe.wait_ge(sem("aff_ready" + n), 1)
                        for t in range(tiles):
                            last = nc.tensor.transpose(bank(5, t * P, (1, P), n=EXPERTS),
                                                       view(small, LG + t * EXPERTS, (1, EXPERTS)), ident[:, :])
                        last.then_inc(sem("affT_ps" + n), 1)

        def job_stage(n, jobs, waits, prefetch=None, vector_first=None):
            BANKS = 8

            def drained(eng, j):
                eng.wait_ge(sem(("act_out" if j % 2 == 0 else "dve_out") + n), j // 2 + 1)

            with nc.Block() as block:
                if prefetch:
                    @block.sync
                    def _(sp):
                        prefetch(sp)

                @block.tensor
                def _(pe):
                    for s, v in waits:
                        pe.wait_ge(sem(s), v)
                    for j, (mms, _) in enumerate(jobs):
                        if j >= BANKS:
                            drained(pe, j - BANKS)
                        for (at, lhsT, rhs, start, stop) in mms:
                            col, dims, p0, np_ = at
                            last = nc.tensor.matmul(bank(j % BANKS, col, *dims, p=p0, n=np_), lhsT, rhs,
                                                    start=start, stop=stop)
                        last.then_inc(sem("job_done" + n), 1)

                @block.scalar
                def _(act):
                    for j in range(0, len(jobs), 2):
                        act.wait_ge(sem("job_done" + n), j + 1)
                        for dst, col, dims in jobs[j][1]:
                            last = nc.scalar.activation(dst, bank(j % BANKS, col, *dims), ACT.Copy)
                        last.then_inc(sem("act_out" + n), 1)

                @block.vector
                def _(dve):
                    for j in range(1, len(jobs), 2):
                        dve.wait_ge(sem("job_done" + n), j + 1)
                        for dst, col, dims in jobs[j][1]:
                            last = nc.vector.tensor_copy(dst, bank(j % BANKS, col, *dims))
                        last.then_inc(sem("dve_out" + n), 1)

        def even_in_proj():
            def hT(k, t0, w):
                return view(arena, HT_AT + k * TOK + t0, (1, w))

            def w_in(k, c0, w):
                return view(ring, k * EV_IN + c0, (1, w))

            jobs = []
            for g in range(FG):
                for t0, w in ((0, SEQ), (SEQ, CTX)):
                    mms = [((0, ((1, w),), 0, P), w_in(k, g * P, P), hT(k, t0, w), k == 0, k == KT - 1)
                           for k in range(KT)]
                    jobs.append((mms, [(view(arena, FT_AT + g * TOK + t0, (1, w)), 0, ((1, w),))]))
            for t in range(TT):
                for c0, w in ((0, 512), (512, 256)):
                    mms = [((0, ((1, w),), 0, P), hT(k, t * P, P), w_in(k, FW + c0, w), k == 0, k == KT - 1)
                           for k in range(KT)]
                    if c0 == 0:
                        drain = (view(arena, QKV_AT + t * 768, (HD, 2), (2 * HD, 4), (1, HD)),
                                 0, ((4 * HD, 2), (HD, 4), (1, HD)))
                    else:
                        drain = (view(arena, QKV_AT + t * 768 + c0, (1, w)), 0, ((1, w),))
                    jobs.append((mms, [drain]))
            job_stage("ei", jobs, [("evin_in", 16 * KT)], even_gains)

        def even_gains(sp):
            for h in range(QH + KVH):
                g = ev_q_gain if h < QH else ev_k_gain
                sp.dma_start(view(arena, GAIN_AT + h * HD, (1, HD)), g[0].partition_broadcast(P)
                             ).then_inc(sem("gain_in"), 16)
            sp.dma_start(view(ring, 22 * SLOT, (P, XT), (1, P)), rope.rearrange("(t p) n -> p t n", p=P)
                         ).then_inc(sem("gain_in"), 16)

        def even_qk_fourier():
            H = QH + KVH
            UC = 0

            def qk(t):
                return view(arena, QKV_AT + t * 768, (HD, H), (1, HD))

            def qn(t):
                return view(arena, QN_AT + t * QK0, (HD, H), (1, HD))

            def tmp(t):
                return view(arena, TMP_AT + (t % 2) * QK0, (HD, H), (1, HD))

            gain = view(arena, GAIN_AT, (HD, H), (1, HD))
            rows = view(small, QSS, (H, TT), (1, H))

            with nc.Block() as block:
                @block.scalar
                def _(act):
                    for t in range(TT):
                        if t >= 2:
                            act.wait_ge(sem("qsum"), t - 1)
                        nc.scalar.activation(tmp(t), qk(t), ACT.Square).then_inc(sem("qsq"), 1)
                    act.wait_ge(sem("qvar"), 1)
                    nc.scalar.activation(rows, rows, ACT.Sqrt).then_inc(sem("qstd"), 1)
                    for t in range(TT):
                        act.wait_ge(sem("f1_ps"), t + 1)
                        norm = (SEQ * P) ** -0.5 if t < XT else (CTX * P) ** -0.5
                        b0 = 4 + 2 * (t % 2)
                        nc.scalar.activation(view(ring, UC + t * SLOT, (P, FG), (1, P)),
                                             bank(b0, 0, (2 * P, FG), (1, P)), ACT.Copy, scale=norm)
                        nc.scalar.activation(view(ring, UC + t * SLOT + 512, (P, FG), (1, P)),
                                             bank(b0, P, (2 * P, FG), (1, P)), ACT.Copy, scale=-norm
                                             ).then_inc(sem("f1_out"), 1)
                    for j in range(2 * FG):
                        act.wait_ge(sem("f2_ps"), j + 1)
                        t0, w = (0, SEQ) if j % 2 == 0 else (SEQ, CTX)
                        nc.scalar.activation(view(arena, FOUR_AT + (j // 2) * TOK + t0, (1, w)),
                                             bank(4 + j % 4, 0, (1, w)), ACT.Copy).then_inc(sem("f2_out"), 1)
                    for t in range(TT):
                        act.wait_ge(sem("qT_ps"), t + 1)
                        b0 = 2 * (t % 2)
                        nc.scalar.activation(view(arena, QT_AT + t * P, (TOK, 4), (1, P)),
                                             bank(b0, 0, (P, 4), (1, P)), ACT.Copy)
                        nc.scalar.activation(view(arena, KT0_AT + t * P, (1, P)),
                                             bank(b0 + 1, 0, (1, P)), ACT.Copy).then_inc(sem("qT_out"), 1)

                @block.vector
                def _(dve):
                    dve.wait_ge(sem("gain_in"), 16 * 11)
                    g_q = view(arena, GAIN_AT, (1, QH * HD))
                    nc.vector.tensor_scalar(g_q, g_q, HD ** -0.5, None, ALU.mult).then_inc(sem("gain_ready"), 1)
                    for t in range(TT):
                        dve.wait_ge(sem("qsq"), t + 1)
                        nc.vector.tensor_reduce(view(small, QSS + t * H, (1, H)), tmp(t), AX.X, ALU.add
                                                ).then_inc(sem("qsum"), 1)
                    dve.wait_ge(sem("qsum"), TT)
                    nc.vector.tensor_scalar(rows, rows, 1.0 / HD, EPS, ALU.mult, ALU.add).then_inc(sem("qvar"), 1)
                    dve.wait_ge(sem("qstd"), 1)
                    nc.vector.reciprocal(rows, rows).then_inc(sem("qrstd"), 1)
                    dve.wait_ge(sem("qrstd"), 1)
                    dve.wait_ge(sem("gain_ready"), 1)
                    step = 0
                    for t in range(TT):
                        nc.vector.tensor_tensor(qk(t), qk(t), view(small, QSS + t * H, (1, H), (0, HD)), ALU.mult
                                                ).then_inc(sem("qstep"), 1)
                        step += 1
                        dve.wait_ge(sem("qstep"), step)
                        if t >= XT:
                            nc.vector.tensor_tensor(qn(t), qk(t), gain, ALU.mult).then_inc(sem("qn_ready"), 1)
                            continue
                        nc.vector.tensor_tensor(qk(t), qk(t), gain, ALU.mult).then_inc(sem("qgained"), 1)
                        dve.wait_ge(sem("qgained"), t + 1)
                        nc.vector.tensor_tensor(qn(t), qk(t), view(ring, 22 * SLOT + t * P, (0, H), (1, HD)), ALU.mult
                                                ).then_inc(sem("qstep"), 1)
                        step += 1
                        dve.wait_ge(sem("qstep"), step)
                        dve.wait_ge(sem("rot"), 2 * (t + 1))
                        nc.vector.tensor_tensor(qn(t), qn(t), tmp(t), ALU.add).then_inc(sem("qn_ready"), 1)

                @block.gpsimd
                def _(pool):
                    pool.wait_ge(sem("qrstd"), 1)
                    for t in range(XT):
                        pool.wait_ge(sem("qgained"), t + 1)
                        if t >= 2:
                            pool.wait_ge(sem("qn_ready"), t - 1)
                        for half in range(2):
                            nc.gpsimd.tensor_tensor(
                                view(arena, TMP_AT + (t % 2) * QK0 + half * 32, (HD, H), (1, 32)),
                                view(arena, QKV_AT + t * 768 + (32 - half * 32), (HD, H), (1, 32)),
                                view(ring, 22 * SLOT + t * P + HD + half * 32, (0, H), (1, 32)),
                                ALU.mult).then_inc(sem("rot"), 1)

                @block.tensor
                def _(pe):
                    pe.wait_ge(sem("dft_in"), 32)
                    cos_t, sin_t = 10 * SLOT, 12 * SLOT
                    for t in range(TT):
                        if t >= 2:
                            pe.wait_ge(sem("f1_out"), t - 1)
                        for g in range(FG):
                            for s, tab in enumerate((cos_t, sin_t)):
                                last = nc.tensor.matmul(bank(4 + 2 * (t % 2), g * 2 * P + s * P, (1, P)),
                                                        view(arena, FT_AT + g * TOK + t * P, (1, P)),
                                                        view(ring, tab, (4, P)), start=True, stop=True)
                        last.then_inc(sem("f1_ps"), 1)
                    for j in range(2 * FG):
                        g, is_ctx = j // 2, j % 2
                        if j == 0:
                            pe.wait_ge(sem("f1_out"), TT)
                        if j >= 4:
                            pe.wait_ge(sem("f2_out"), j - 3)
                        tiles, w, st = ((0, 1, 2, 3), SEQ, 1) if not is_ctx else ((4, 5), CTX, 2)
                        n_mm = 2 * len(tiles)
                        i = 0
                        for s, tab in enumerate((cos_t, sin_t)):
                            for t in tiles:
                                last = nc.tensor.matmul(bank(4 + j % 4, 0, (1, w)),
                                                        view(ring, UC + t * SLOT + s * 512 + g * P, (1, P)),
                                                        view(ring, tab + (t - tiles[0]) * 512, (st, w)),
                                                        start=(i == 0), stop=(i == n_mm - 1))
                                i += 1
                        last.then_inc(sem("f2_ps"), 1)
                    for t in range(TT):
                        pe.wait_ge(sem("qn_ready"), t + 1)
                        if t >= 2:
                            pe.wait_ge(sem("qT_out"), t - 1)
                        for pr in range(5):
                            last = nc.tensor.transpose(bank(2 * (t % 2), pr * P, (1, P)),
                                                       view(arena, QN_AT + t * QK0 + pr * P, (1, P)), ident[:, :])
                        last.then_inc(sem("qT_ps"), 1)

        def attention(layer):
            n = f"a{layer}"
            if layer == 0:
                units = [(pr, t) for t in range(TT) for pr in range(4)]
                p_at, pt_at = P0_AT, PT0_AT
                p_w = 640
            else:
                units = [(pr, t) for pr in range(NH // 2) for t in range(XT)]
                p_at, pt_at = P1_AT, PT1_AT
                p_w = 512
            n_p = 2 if layer == 0 else 2

            def chunks(t):
                if layer == 1:
                    return [(SEQ, None), (SEQ + P, None), (((t - 1) % XT) * P, None), (t * P, None)]
                keys = [(SEQ, None), (SEQ + P, None)]
                if t < XT:
                    keys.append((t * P, None))
                    if t > 0:
                        keys.append(((t - 1) * P, 0))
                    if t < XT - 1:
                        keys.append(((t + 1) * P, 1))
                return keys

            def sc_bank(u, a):
                return 2 * a if layer == 0 else 2 * (u % 2) + a

            def probs(u, a, col=0, *dims):
                return view(arena, p_at + ((u % n_p) * 2 + a) * p_w + col, *(dims or ((1, P),)))

            def pt(a, col, w):
                return view(arena, pt_at + a * p_w + col, (1, w))

            def v_tile(key, pr, a):
                if layer == 0:
                    return view(arena, QKV_AT + (key // P) * 768 + QK0 + a * HD, (1, HD))
                return view(ring, (key // P) * SLOT + (2 * pr + a) * HD, (1, HD))

            def qT(pr, t, a):
                at, w = (QT_AT, TOK) if layer == 0 else (QT1_AT, SEQ)
                return view(arena, at + pr * w + t * P, (1, P), p=64 * a, n=64)

            def kT(pr, key, w, a):
                at = KT0_AT if layer == 0 else KT1_AT + pr * TOK
                return view(arena, at + key, (1, w), p=64 * a, n=64)

            ST = SOFT

            def st(u, what, a=0, w=1):
                return view(small, ST + (u % 2) * 16 + what * 2 + a, (1, w))

            MX, NEG, SUM, ES, REC, SHS = 0, 1, 2, 3, 4, 5
            O_BANKS = (7,) if layer == 0 else (6, 7)

            with nc.Block() as block:
                if layer == 1:
                    @block.sync
                    def _(sp):
                        for h in range(NH):
                            if h >= 2:
                                sp.wait_ge(sem("bm_read"), h - 1)
                            sp.dma_start(view(arena, BR1_AT + (h % 2) * 384, (1, 384)), rpb_pad[h]
                                         ).then_inc(sem(f"br_in{h % 2}"), 16)

                    @block.gpsimd
                    def _(pool):
                        pool.wait_ge(sem("na_mask_in"), 16)
                        for h in range(NH):
                            pr, a = h // 2, h % 2
                            pool.wait_ge(sem(f"br_in{h % 2}"), 16 * (h // 2 + 1))
                            if pr >= 2:
                                pool.wait_ge(sem("biased"), 8 * (pr - 1))
                            for v in range(3):
                                last = nc.gpsimd.tensor_tensor(
                                    view(arena, bm_at(pr) + (a * 3 + v) * 256, (64, 4), (8, 8), (1, 8)),
                                    view(arena, BR1_AT + (h % 2) * 384, (8, 4), (RPB_PAD, 8), (1, 8)),
                                    view(ring, 6 * SLOT + v * 256, (64, 4), (8, 8), (1, 8)), ALU.add)
                            last.then_inc(sem("bm_read"), 1)

                @block.tensor
                def _(pe):
                    def scores(u):
                        pr, t = units[u]
                        if layer == 0 and u >= 1:
                            pe.wait_ge(sem("exp_done" + n), 2 * u)
                        if layer == 1 and u >= 2:
                            pe.wait_ge(sem("exp_done" + n), 2 * (u - 1))
                        keys = chunks(t)
                        segs = []
                        for i, (key, mask) in enumerate(keys):
                            if (segs and segs[-1][1] + segs[-1][2] == key and i * P % 512
                                    and segs[-1][3] is None and mask is None):
                                segs[-1][2] += P
                            else:
                                segs.append([i * P, key, P, mask])
                        for col, key, w, mask in segs:
                            for a in range(2):
                                last = nc.tensor.matmul(bank(sc_bank(u, a), col, (1, w)), qT(pr, t, a),
                                                        kT(pr, key, w, a), start=True, stop=mask is None,
                                                        skip_group_check=True)
                            if mask is not None:
                                for a in range(2):
                                    last = nc.tensor.matmul(bank(sc_bank(u, a), col, (1, w)), ident16[:, :],
                                                            view(swa_mask, mask * P, (1, P)), start=False, stop=True,
                                                            skip_group_check=True)
                        last.then_inc(sem("scores" + n), 1)

                    scores(0)
                    for u, (pr, t) in enumerate(units):
                        if u + 1 < len(units):
                            scores(u + 1)
                        nk = len(chunks(t))
                        for a in range(2):
                            pe.wait_ge(sem("p_ready" + n), 2 * u + a + 1)
                            if u >= 1 and a == 0:
                                pe.wait_ge(sem("pt_act" + n), u)
                                pe.wait_ge(sem("pt_dve" + n), u)
                            for i in range(nk):
                                at = (4 + a, i * P) if i < 4 else (6, a * P)
                                last = nc.tensor.transpose(bank(at[0], at[1], (1, P)), probs(u, a, i * P), ident[:, :])
                            last.then_inc(sem("pt_ps" + n), 1)
                        pe.wait_ge(sem("pt_act" + n), u + 1)
                        pe.wait_ge(sem("pt_dve" + n), u + 1)
                        if u >= len(O_BANKS):
                            pe.wait_ge(sem("o_out" + n), u + 1 - len(O_BANKS))
                        for i, (key, _) in enumerate(chunks(t)):
                            for a in range(2):
                                last = nc.tensor.matmul(bank(O_BANKS[u % len(O_BANKS)], 0, (1, P), p=64 * a, n=64),
                                                        v_tile(key, pr, a), pt(a, i * P, P),
                                                        start=(i == 0), stop=(i == nk - 1))
                        last.then_inc(sem("o_ps" + n), 1)

                @block.vector
                def _(dve):
                    steps = [0]

                    def stepped(ins):
                        steps[0] += 1
                        ins.then_inc(sem("dstep" + n), 1)
                        dve.wait_ge(sem("dstep" + n), steps[0])

                    def pt_out(u):
                        w = len(chunks(units[u][1])) * P
                        dve.wait_ge(sem("pt_ps" + n), 2 * u + 2)
                        if u >= 1:
                            dve.wait_ge(sem("o_ps" + n), u)
                        nc.vector.tensor_copy(pt(1, 0, min(w, 512)), bank(5, 0, (1, min(w, 512)))
                                              ).then_inc(sem("pt_dve" + n), 1)

                    for u, (pr, t) in enumerate(units):
                        w = len(chunks(t)) * P
                        dve.wait_ge(sem("scores" + n), u + 1)
                        if layer == 1:
                            if t == 0:
                                dve.wait_ge(sem("bm_read"), 2 * pr + 2)
                            v = 0 if t == 0 else 2 if t == XT - 1 else 1
                            for a in range(2):
                                s = bank(sc_bank(u, a), 256, (1, 256))
                                nc.vector.tensor_tensor(s, s, view(arena, bm_at(pr) + (a * 3 + v) * 256, (1, 256)),
                                                        ALU.add).then_inc(sem("biased"), 1)
                            dve.wait_ge(sem("biased"), 2 * u + 2)
                        for a in range(2):
                            last = nc.vector.tensor_reduce(st(u, MX, a), bank(sc_bank(u, a), 0, (1, w)), AX.X, ALU.max)
                            stepped(last)
                        if layer == 0:
                            sk = view(small, SINK + pr, (4, 2))
                            stepped(nc.vector.tensor_tensor(st(u, MX, 0, 2), st(u, MX, 0, 2), sk, ALU.max))
                            stepped(nc.vector.tensor_tensor(st(u, SHS, 0, 2), sk, st(u, MX, 0, 2), ALU.subtract))
                        nc.vector.tensor_scalar(st(u, NEG, 0, 2), st(u, MX, 0, 2), -1.0, None, ALU.mult
                                                ).then_inc(sem("neg" + n), 1)
                        if u >= 1:
                            pt_out(u - 1)
                        dve.wait_ge(sem("exp_done" + n), 2 * u + 2)
                        if layer == 0:
                            dve.wait_ge(sem("es" + n), u + 1)
                            stepped(nc.vector.tensor_tensor(st(u, SUM, 0, 2), st(u, SUM, 0, 2), st(u, ES, 0, 2),
                                                            ALU.add))
                        stepped(nc.vector.reciprocal(st(u, REC, 0, 2), st(u, SUM, 0, 2)))
                        for a in range(2):
                            pp = probs(u, a, 0, (1, w))
                            nc.vector.tensor_scalar(pp, pp, st(u, REC, a), None, ALU.mult
                                                    ).then_inc(sem("p_ready" + n), 1)
                    pt_out(len(units) - 1)

                @block.scalar
                def _(act):
                    def tail(u):
                        pr, t = units[u]
                        w = len(chunks(t)) * P
                        act.wait_ge(sem("pt_ps" + n), 2 * u + (2 if w > 512 else 1))
                        if u >= 1:
                            act.wait_ge(sem("o_ps" + n), u)
                        last = nc.scalar.activation(pt(0, 0, min(w, 512)), bank(4, 0, (1, min(w, 512))), ACT.Copy)
                        if w > 512:
                            last = nc.scalar.activation(view(arena, pt_at + 512, (p_w, 2), (1, P)),
                                                        bank(6, 0, (P, 2), (1, P)), ACT.Copy)
                        last.then_inc(sem("pt_act" + n), 1)

                    def out_copy(u):
                        pr, t = units[u]
                        act.wait_ge(sem("o_ps" + n), u + 1)
                        if layer == 0:
                            nc.scalar.activation(view(arena, AT0_AT + pr * TOK + t * P, (1, P)),
                                                 bank(O_BANKS[u % len(O_BANKS)], 0, (1, P)), ACT.Copy).then_inc(sem("o_out" + n), 1)
                        else:
                            nc.scalar.activation(view(arena, AT1_AT + pr * SEQ + t * 16, (8, 2), (64, 8), (1, 8)),
                                                 bank(O_BANKS[u % len(O_BANKS)], 0, (64, 2), (8, 8), (1, 8)), ACT.Copy
                                                 ).then_inc(sem("o_out" + n), 1)

                    for u, (pr, t) in enumerate(units):
                        w = len(chunks(t)) * P
                        act.wait_ge(sem("neg" + n), u + 1)
                        if u >= 2:
                            act.wait_ge(sem("pt_ps" + n), 2 * (u - 1))
                        for a in range(2):
                            nc.scalar.activation(probs(u, a, 0, (1, w)), bank(sc_bank(u, a), 0, (1, w)), ACT.Exp,
                                                 bias=st(u, NEG, a), accum_out=st(u, SUM, a)
                                                 ).then_inc(sem("exp_done" + n), 1)
                        if layer == 0:
                            nc.scalar.activation(st(u, ES, 0, 2), st(u, SHS, 0, 2), ACT.Exp).then_inc(sem("es" + n), 1)
                        if u >= 2:
                            out_copy(u - 2)
                        if u >= 1:
                            tail(u - 1)
                    out_copy(len(units) - 2)
                    tail(len(units) - 1)
                    out_copy(len(units) - 1)

        def bm_at(pr):
            return BM1_AT if pr % 2 == 0 else BM1B_AT

        def out_proj(layer, prefetch=None):
            n = f"o{layer}"
            tiles = TT if layer == 0 else XT
            w_slot = 14 if layer == 0 else 8

            def lhsT(k, t):
                if layer == 0:
                    at = FOUR_AT + k * TOK if k < 4 else AT0_AT + (k - 4) * TOK
                    return view(arena, at + t * P, (1, P))
                return view(arena, AT1_AT + k * SEQ + t * P, (1, P))

            jobs = [(t, h) for t in range(tiles) for h in range(2)]
            with nc.Block() as block:
                @block.sync
                def _(sp):
                    for s in range(2 if tiles == TT else 1):
                        sp.dma_start(view(arena, GB_AT + s * D, (1, D)), mod_row(layer, s, G1)
                                     ).then_inc(sem("g_in" + n), 16)
                    if prefetch:
                        prefetch(sp)

                @block.tensor
                def _(pe):
                    pe.wait_ge(sem("evout_in" if layer == 0 else "odout_in"), 16 * (12 if layer == 0 else 8))
                    for j, (t, h) in enumerate(jobs):
                        if j >= 8:
                            pe.wait_ge(sem("gated" + n), j - 7)
                        for k in range(KT):
                            last = nc.tensor.matmul(bank(j % 8), lhsT(k, t),
                                                    view(ring, (w_slot + k) * SLOT + h * 512, (1, 512)),
                                                    start=(k == 0), stop=(k == KT - 1))
                        last.then_inc(sem("y_ps" + n), 1)

                @block.vector
                def _(dve):
                    dve.wait_ge(sem("g_in" + n), 32 if tiles == TT else 16)
                    for j, (t, h) in enumerate(jobs):
                        dve.wait_ge(sem("y_ps" + n), j + 1)
                        if j >= 4:
                            dve.wait_ge(sem("added" + n), j - 3)
                        nc.vector.tensor_tensor(view(arena, YT_AT + (j % 4) * 512, (1, 512)), bank(j % 8),
                                                view(arena, GB_AT + (0 if t < XT else D) + h * 512, (1, 512)),
                                                ALU.mult).then_inc(sem("gated" + n), 1)

                @block.gpsimd
                def _(pool):
                    for j, (t, h) in enumerate(jobs):
                        pool.wait_ge(sem("gated" + n), j + 1)
                        r = view(resid, t * D + h * 512, (1, 512))
                        nc.gpsimd.tensor_tensor(r, r, view(arena, YT_AT + (j % 4) * 512, (1, 512)), ALU.add
                                                ).then_inc(sem("added" + n), 1)

        IOTA = 12800
        META = IOTA + SEQ
        MT = META + 68
        IDX = MT + 768
        CUR = IDX + 384
        GX = CUR + 8
        XS = GX + 1536
        SX = XS + 1536
        HU = 6144
        SU = HU + 768
        HXT = SU + 768
        YB = HXT + 768
        AFFW = HB_AT
        assert SX + 1536 <= ARENA and YB + 1536 <= HB_AT

        def top_k(layer):
            n = f"t{layer}"
            streams = [(0, SEQ, CAPX)] + ([(SEQ, CTX, CAPC)] if layer == 0 else [])
            with nc.Block() as block:
                @block.sync
                def _(sp):
                    sp.dma_start(view(arena, IOTA, (1, SEQ)), iota_in.partition_broadcast(P)
                                 ).then_inc(sem("iota_in" + n), 16)
                    sp.wait_ge(sem("iota_in" + n), 16)

                @block.vector
                def _(dve):
                    step = [0]

                    def stepped(ins):
                        step[0] += 1
                        ins.then_inc(sem("tk" + n), 1)
                        dve.wait_ge(sem("tk" + n), step[0])

                    E = EXPERTS
                    stepped(nc.vector.memset(view(arena, MT, (1, 768), n=E), 0.0))
                    for s, (t0, w, cap) in enumerate(streams):
                        aff = view(arena, AFFW + t0, (1, w), n=E)
                        reps = P // cap
                        for r in range(cap // 8):
                            val = view(arena, IDX + s * 64 + r * 8, (1, 8), n=E)
                            idx = view(arena, IDX + 192 + s * 64 + r * 8, (1, 8), n=E)
                            stepped(nc.vector.max(val, aff))
                            stepped(nc.vector.max_index(idx.bitcast(U32), val, aff))
                            stepped(nc.vector.match_replace(aff, val, aff, -1.0))
                        raw = view(arena, IDX + 192 + s * 64, (1, cap), n=E)
                        num = view(arena, IDX + 320, (1, cap), n=E)
                        stepped(nc.vector.tensor_copy(num, raw.bitcast(U32)))
                        val = view(arena, IDX + s * 64, (1, cap), n=E)
                        for q in range(reps):
                            stepped(nc.vector.tensor_copy(view(arena, MT + s * P + q * cap, (1, cap), n=E), num))
                            stepped(nc.vector.tensor_copy(view(arena, MT + (2 + s) * P + q * cap, (1, cap), n=E), val))
                            stepped(nc.vector.tensor_scalar(view(arena, MT + (4 + s) * P + q * cap, (1, cap), n=E),
                                                            num, float(reps), float(q), ALU.mult, ALU.add))
                    dve.wait_ge(sem("mt_ps" + n), 1)
                    stepped(nc.vector.tensor_copy(view(arena, META, (4, E), (1, 4)),
                                                  bank(0, 0, (1, E), (E, 4))))
                    stepped(nc.vector.tensor_copy(view(arena, META + 4 * E, (1, 4)), view(arena, META + 4 * E - 4, (1, 4))))
                    stepped(nc.vector.tensor_copy(view(offs, 0, (2, E), (1, 2)), bank(0, 4 * E, (1, E), (E, 2))))
                    stepped(nc.vector.tensor_copy(view(offs, 2 * E, (1, 2)), view(offs, 2 * E - 2, (1, 2))))

                @block.tensor
                def _(pe):
                    n_steps = 1 + sum(3 * (cap // 8) + 1 + 3 * (P // cap) for _, _, cap in streams)
                    pe.wait_ge(sem("tk" + n), n_steps)
                    for j in range(6):
                        last = nc.tensor.transpose(bank(0, j * EXPERTS, (1, EXPERTS)),
                                                   view(arena, MT + j * P, (1, P), n=EXPERTS),
                                                   ident[0:EXPERTS, 0:EXPERTS])
                    last.then_inc(sem("mt_ps" + n), 1)

        WCH = SLOTS // 2

        def expert_src(layer, e, ch):
            w = (exp_w_gate, exp_w_up, exp_w_down)[ch // 4]
            r0 = (ch % 4) * 2 * P
            if isinstance(e, int):
                return w[layer, e, r0:r0 + 2 * P, :].rearrange("(k p) n -> p k n", p=P)
            return w[layer, bass.ds(e, 1), r0:r0 + 2 * P, :].rearrange("e (k p) n -> p (e k) n", p=P)

        def ring_chunk(ch):
            return view(ring, ch * 2 * SLOT, (SLOT, 2), (1, SLOT))

        def load_first(layer, chunks):
            def go(sp):
                for ch in chunks:
                    sp.dma_start(ring_chunk(ch), expert_src(layer, 0, ch)).then_inc(sem(f"w{layer}_{ch}"), 16)
            return go

        def mixture(layer, early):
            n = f"m{layer}"
            has_c = layer == 0
            NC = 2 if has_c else 1
            SA = XT + (CT if has_c else 0)

            def buf(at, par, s):
                return view(arena, at + par * 768 + (512 if s else 0), (1, 256 if s else 512))

            def cur(par, what):
                return view(arena, CUR + par * 4 + what, (1, 1))

            with nc.Block() as block:
                @block.sync
                def _(sp):
                    for ch in range(WCH):
                        if ch not in early:
                            sp.dma_start(ring_chunk(ch), expert_src(layer, 0, ch)).then_inc(sem(f"w{layer}_{ch}"), 16)
                    with nc.sync.Fori(0, EXPERTS - 1) as i:
                        for ch in range(WCH):
                            if ch in (7, 11):
                                used, freed = sem(("gu_ps" if ch == 7 else "y_ps") + n), i + 1
                            else:
                                used, freed = sem("w_used" + n), i * 10 + (ch + 1 if ch < 7 else ch)
                            freed = nc.sync.snap(freed)
                            src = expert_src(layer, nc.sync.snap(i + 1), ch)
                            sp.wait_ge(used, freed)
                            sp.dma_start(ring_chunk(ch), src).then_inc(sem(f"w{layer}_{ch}"), 16)

                def gather(e):
                    par = e % 2
                    off = view(offs, e * 2, (1, 1))
                    nc.gpsimd.indirect_dma_start(buf(GX, par, 0), None, h2x.rearrange("t (h d) -> (t h) d", h=2),
                                                 bass.IndirectOffsetOnAxis(ap=off, axis=0)
                                                 ).then_inc(sem(f"gx{par}" + n), 16)
                    if has_c:
                        off = view(offs, e * 2 + 1, (1, 1))
                        nc.gpsimd.indirect_dma_start(buf(GX, par, 1), None, h2c.rearrange("t (q d) -> (t q) d", q=4),
                                                     bass.IndirectOffsetOnAxis(ap=off, axis=0)
                                                     ).then_inc(sem(f"gc{par}" + n), 16)

                @block.gpsimd
                def _(pool):
                    for e in range(EXPERTS + 1):
                        if e >= 2:
                            pool.wait_ge(sem("xs_ps" + n), e - 1)
                        gather(e)

                @block.tensor
                def _(pe):
                    def turn(par):
                        for j in range(4):
                            last = nc.tensor.transpose(bank(7, j * P, (1, P)), view(arena, GX + par * 768 + j * P, (1, P)),
                                                       ident[:, :])
                        if has_c:
                            for j in range(2):
                                last = nc.tensor.transpose(bank(2, j * P, (1, P)),
                                                           view(arena, GX + par * 768 + 512 + j * P, (1, P)), ident[:, :])
                        last.then_inc(sem("xs_ps" + n), 1)

                    def xs(par, k):
                        return view(arena, XS + par * 768 + (k % 4) * P + (k // 4) * 64, (1, 64))

                    def xsc(par, k):
                        return view(arena, XS + par * 768 + 512 + (k % 2) * P + (k // 2) * 32, (1, 32))

                    def hx(k):
                        return view(arena, HXT + (k % 4) * P + (k // 4) * 64, (1, 64))

                    def hc(k):
                        return view(arena, HXT + 512 + (k % 2) * P + (k // 2) * 32, (1, 32))

                    def dense(ch, k, lx, lc, bx, bc, cc):
                        w0 = (ch * 2 + k % 2) * SLOT
                        for half in range(2):
                            last = nc.tensor.matmul(bank(bx, 0, (1, 512), p=64 * half, n=64), lx,
                                                    view(ring, w0 + half * 512, (1, 512)),
                                                    start=(k == 0), stop=(k == KT - 1))
                        if has_c:
                            for q in range(4):
                                last = nc.tensor.matmul(bank(bc, cc, (1, 256), p=32 * q, n=32), lc,
                                                        view(ring, w0 + q * 256, (1, 256)),
                                                        start=(k == 0), stop=(k == KT - 1))
                        return last

                    def scatter(e1, par):
                        pe.wait_ge(sem("s_ready" + n), e1)
                        pe.wait_ge(sem("y_out" + n), e1)
                        for tt in range(XT):
                            if tt >= 2:
                                pe.wait_ge(sem("sc_add" + n), (e1 - 1) * SA + (tt - 1))
                            for half in range(2):
                                last = nc.tensor.matmul(
                                    bank(3 + 2 * (tt % 2) + half),
                                    view(arena, SX + par * 768 + tt * P, (1, P), p=64 * half, n=64),
                                    view(arena, YB + par * 768, (1, 512), p=64 * half, n=64), start=True, stop=True)
                            last.then_inc(sem("sc_ps" + n), 1)
                        if has_c:
                            for tt in range(CT):
                                pe.wait_ge(sem("sc_add" + n), (e1 - 1) * SA + (4 + tt))
                                for q in range(4):
                                    last = nc.tensor.matmul(
                                        bank(3 + q, 0, (1, 256)),
                                        view(arena, SX + par * 768 + 512 + tt * P, (1, P), p=32 * q, n=32),
                                        view(arena, YB + par * 768 + 512, (1, 256), p=32 * q, n=32),
                                        start=True, stop=True)
                                last.then_inc(sem("sc_ps" + n), 1)

                    pe.wait_ge(sem("gx0" + n), 16)
                    if has_c:
                        pe.wait_ge(sem("gc0" + n), 16)
                    turn(0)
                    with nc.tensor.Fori(0, EXPERTS // 2) as i:
                        for par in range(2):
                            e = i * 2 + par
                            pe.wait_ge(sem("xs_out" + n), e * NC + NC)
                            for m in range(2):
                                for ch in range(4 * m, 4 * m + 4):
                                    pe.wait_ge(sem(f"w{layer}_{ch}"), e * 16 + 16)
                                    for k in (2 * (ch % 4), 2 * (ch % 4) + 1):
                                        last = dense(ch, k, xs(par, k), xsc(par, k), m, 2, 256 * m)
                                    if ch < 7:
                                        last.then_inc(sem("w_used" + n), 1)
                            last.then_inc(sem("gu_ps" + n), 1)
                            scatter(e + 1, 1 - par)
                            pe.wait_ge(sem("h_ready" + n), e * NC + NC)
                            for j in range(4):
                                last = nc.tensor.transpose(bank(0, j * P, (1, P)), view(arena, HU + j * P, (1, P)),
                                                           ident[:, :])
                            if has_c:
                                for j in range(2):
                                    last = nc.tensor.transpose(bank(1, j * P, (1, P)),
                                                               view(arena, HU + 512 + j * P, (1, P)), ident[:, :])
                            last.then_inc(sem("hT_ps" + n), 1)
                            pe.wait_ge(sem(f"gx{1 - par}" + n), i * 16 + (16 if par == 0 else 32))
                            if has_c:
                                pe.wait_ge(sem(f"gc{1 - par}" + n), i * 16 + (16 if par == 0 else 32))
                            turn(1 - par)
                            pe.wait_ge(sem("hT_out" + n), e * NC + NC)
                            pe.wait_ge(sem("sc_add" + n), e * SA + SA)
                            for ch in range(8, 12):
                                pe.wait_ge(sem(f"w{layer}_{ch}"), e * 16 + 16)
                                for k in (2 * (ch % 4), 2 * (ch % 4) + 1):
                                    last = dense(ch, k, hx(k), hc(k), 3, 4, 0)
                                if ch < 11:
                                    last.then_inc(sem("w_used" + n), 1)
                            last.then_inc(sem("y_ps" + n), 1)
                    scatter(EXPERTS + 1, 1)

                @block.scalar
                def _(act):
                    def xs_out(par, e1):
                        act.wait_ge(sem("xs_ps" + n), e1)
                        nc.scalar.activation(buf(XS, par, 0), bank(7), ACT.Copy).then_inc(sem("xs_out" + n), 1)
                        if has_c:
                            nc.scalar.activation(buf(XS, par, 1), bank(2, 0, (1, 256)), ACT.Copy
                                                 ).then_inc(sem("xs_out" + n), 1)

                    xs_out(0, 1)
                    with nc.scalar.Fori(0, EXPERTS // 2) as i:
                        for par in range(2):
                            e = i * 2 + par
                            act.wait_ge(sem("gu_ps" + n), e + 1)
                            nc.scalar.activation(view(arena, SU, (1, 512)), bank(0), ACT.Silu).then_inc(sem("silu" + n), 1)
                            if has_c:
                                nc.scalar.activation(view(arena, SU + 512, (1, 256)), bank(2, 0, (1, 256)), ACT.Silu
                                                     ).then_inc(sem("silu" + n), 1)
                            act.wait_ge(sem("hT_ps" + n), e + 1)
                            nc.scalar.activation(view(arena, HXT, (1, 512)), bank(0), ACT.Copy).then_inc(sem("hT_out" + n), 1)
                            if has_c:
                                nc.scalar.activation(view(arena, HXT + 512, (1, 256)), bank(1, 0, (1, 256)), ACT.Copy
                                                     ).then_inc(sem("hT_out" + n), 1)
                            xs_out(1 - par, e + 2)
                            act.wait_ge(sem("y_ps" + n), e + 1)
                            last = nc.scalar.activation(buf(YB, par, 0), bank(3), ACT.Copy, scale=cur(par, 2))
                            if has_c:
                                last = nc.scalar.activation(buf(YB, par, 1), bank(4, 0, (1, 256)), ACT.Copy,
                                                            scale=cur(par, 3))
                            last.then_inc(sem("y_out" + n), 1)

                @block.vector
                def _(dve):
                    def meta(e, par):
                        nc.vector.tensor_copy(view(arena, CUR + par * 4, (1, 4)), arena[:, bass.ds(e * 4 + META, 4)]
                                              ).then_inc(sem("cur" + n), 1)

                    def adds(e1):
                        for tt in range(XT):
                            dve.wait_ge(sem("sc_ps" + n), (e1 - 1) * SA + (tt + 1))
                            a = view(arena, ACC_AT + tt * D, (512, 2), (1, 512))
                            nc.vector.tensor_tensor(a, a, bank(3 + 2 * (tt % 2), 0, (512, 2), (1, 512)), ALU.add
                                                    ).then_inc(sem("sc_add" + n), 1)
                        if has_c:
                            for tt in range(CT):
                                dve.wait_ge(sem("sc_ps" + n), (e1 - 1) * SA + (XT + tt + 1))
                                a = view(arena, ACC_AT + (XT + tt) * D, (256, 4), (1, 256))
                                nc.vector.tensor_tensor(a, a, bank(3, 0, (512, 4), (1, 256)), ALU.add
                                                        ).then_inc(sem("sc_add" + n), 1)

                    nc.vector.memset(view(arena, SX + 768, (1, 768)), 0.0)
                    nc.vector.memset(view(arena, YB + 768, (1, 768)), 0.0).then_inc(sem("y_out" + n), 1)
                    nc.vector.memset(view(arena, ACC_AT, (1, 6144)), 0.0).then_inc(sem("s_ready" + n), 1)
                    dve.wait_ge(sem("s_ready" + n), 1)
                    meta(0, 0)
                    with nc.vector.Fori(0, EXPERTS // 2) as i:
                        for par in range(2):
                            e = i * 2 + par
                            dve.wait_ge(sem("cur" + n), e + 1)
                            for s in range(NC):
                                last = nc.vector.tensor_scalar(buf(SX, par, s), view(arena, IOTA, (1, 256 if s else 512)),
                                                               cur(par, s), None, ALU.is_equal)
                            last.then_inc(sem("s_ready" + n), 1)
                            dve.wait_ge(sem("silu" + n), e * NC + 1)
                            meta(nc.vector.snap(e + 1), 1 - par)
                            nc.vector.tensor_tensor(view(arena, HU, (1, 512)), view(arena, SU, (1, 512)), bank(1), ALU.mult
                                                    ).then_inc(sem("h_ready" + n), 1)
                            if has_c:
                                dve.wait_ge(sem("silu" + n), e * NC + 2)
                                nc.vector.tensor_tensor(view(arena, HU + 512, (1, 256)), view(arena, SU + 512, (1, 256)),
                                                        bank(2, 256, (1, 256)), ALU.mult).then_inc(sem("h_ready" + n), 1)
                            adds(e + 1)
                    adds(EXPERTS + 1)

        def ffn_residual(layer, prefetch=None):
            n = f"f{layer}"
            tiles = TT if layer == 0 else XT
            with nc.Block() as block:
                @block.sync
                def _(sp):
                    for s in range(2 if tiles == TT else 1):
                        sp.dma_start(view(arena, 16384 + s * D, (1, D)), mod_row(layer, s, G2)
                                     ).then_inc(sem("g_in" + n), 16)
                    if prefetch:
                        prefetch(sp)
                    if layer == 1:
                        for t in range(XT):
                            sp.wait_ge(sem("added" + n), t + 1)
                            sp.dma_start(out[0, t * P:(t + 1) * P, :], view(resid, t * D, (1, D))
                                         ).then_inc(sem("out_done"), 16)
                        sp.wait_ge(sem("out_done"), 16 * XT)

                @block.vector
                def _(dve):
                    dve.wait_ge(sem("g_in" + n), 32 if tiles == TT else 16)
                    for t in range(tiles):
                        a = view(arena, ACC_AT + t * D, (1, D))
                        nc.vector.tensor_tensor(a, a, view(arena, 16384 + (0 if t < XT else D), (1, D)), ALU.mult
                                                ).then_inc(sem("gated" + n), 1)
                        dve.wait_ge(sem("gated" + n), t + 1)
                        r = view(resid, t * D, (1, D))
                        nc.vector.tensor_tensor(r, r, a, ALU.add).then_inc(sem("added" + n), 1)

        def load_odd(sp):
            for cb in range(6):
                for k4 in range(2):
                    sp.dma_start(view(ring, cb * 4 * SLOT + k4 * 2048, (512, 4), (1, 512)),
                                 od_w_in[0, k4 * 512:(k4 + 1) * 512, cb * 512:(cb + 1) * 512]
                                 .rearrange("(k p) n -> p k n", p=P)).then_inc(sem(f"odin{cb}"), 16)

        def odd_in_proj():
            W1 = 832
            qk_jobs = [(cb, t) for cb in range(4) for t in range(XT if cb < 2 else TT)]
            v_jobs = [(cb, t) for cb in (4, 5) for t in range(TT)]
            jobs = qk_jobs + v_jobs
            NQ = len(qk_jobs)

            def hT_cols(cb, t):
                if t >= XT:
                    return 576 + (t - XT) * P
                return t * P if cb < 2 else t * P + 64

            def tm(j):
                return view(arena, TM1_AT + (j % 4) * 512, (HD, 8), (1, HD))

            def tmf(j):
                return view(arena, TM1_AT + (j % 4) * 512, (1, 512))

            RS = SOFT
            GQ = 0

            with nc.Block() as block:
                @block.sync
                def _(sp):
                    for s, g in enumerate((od_q_gain, od_k_gain)):
                        sp.dma_start(view(small, MISC + s * HD, (1, HD)), g[0].partition_broadcast(P)
                                     ).then_inc(sem("odgain_in"), 16)
                    sp.wait_ge(sem("od_ps"), 2 * XT + TT)
                    sp.dma_start(view(ring, 6 * SLOT, (1, 768)), na_mask_in).then_inc(sem("na_mask_in"), 16)
                    sp.wait_ge(sem("od_ps"), NQ)
                    for k in range(KT):
                        sp.dma_start(view(ring, (8 + k) * SLOT, (1, D)), od_w_out[0, k * P:(k + 1) * P, :]
                                     ).then_inc(sem("odout_in"), 16)

                @block.tensor
                def _(pe):
                    def project(j):
                        cb, t = jobs[j]
                        pe.wait_ge(sem(f"odin{cb}"), 32)
                        if j >= 4:
                            if j - 4 < NQ:
                                pe.wait_ge(sem("tm_in"), j - 3)
                            else:
                                pe.wait_ge(sem("v_out"), j - 4 - NQ + 1)
                        for k in range(KT):
                            last = nc.tensor.matmul(bank(j % 4), view(arena, HT_AT + k * W1 + hT_cols(cb, t), (1, P)),
                                                    view(ring, cb * 4 * SLOT + k * 512, (1, 512)),
                                                    start=(k == 0), stop=(k == KT - 1))
                        last.then_inc(sem("od_ps"), 1)

                    def turn(j):
                        pe.wait_ge(sem("qk_ready"), j + 1)
                        if j >= 2:
                            pe.wait_ge(sem("odT_out"), j - 1)
                        for i in range(4):
                            last = nc.tensor.transpose(bank(4 + j % 2, i * P, (1, P)),
                                                       view(arena, TM1_AT + (j % 4) * 512 + i * P, (1, P)), ident[:, :])
                        last.then_inc(sem("odT_ps"), 1)

                    for j in range(len(jobs)):
                        project(j)
                        if 2 <= j < NQ + 2:
                            turn(j - 2)

                @block.scalar
                def _(act):
                    def turned(j):
                        cb, t = jobs[j]
                        act.wait_ge(sem("odT_ps"), j + 1)
                        if cb < 2:
                            dst = view(arena, QT1_AT + cb * 4 * SEQ + t * P, (SEQ, 4), (1, P))
                        else:
                            dst = view(arena, KT1_AT + (cb - 2) * 4 * TOK + t * P, (TOK, 4), (1, P))
                        nc.scalar.activation(dst, bank(4 + j % 2, 0, (P, 4), (1, P)), ACT.Copy
                                             ).then_inc(sem("odT_out"), 1)

                    for j in range(len(jobs)):
                        act.wait_ge(sem("od_ps"), j + 1)
                        cb, t = jobs[j]
                        if j < NQ:
                            if j >= 4:
                                act.wait_ge(sem("odT_ps"), j - 3)
                            nc.scalar.activation(tmf(j), bank(j % 4), ACT.Copy).then_inc(sem("tm_in"), 1)
                            if j >= 2:
                                act.wait_ge(sem("odsum"), j - 1)
                            act.wait_ge(sem("tm_in"), j + 1)
                            nc.scalar.activation(view(arena, PT1_AT - 512 + (j % 2) * 512, (1, 512)), tmf(j),
                                                 ACT.Square).then_inc(sem("odsq"), 1)
                            if j >= 1:
                                act.wait_ge(sem("odvar"), j)
                                s = view(small, RS + ((j - 1) % 4) * 8, (1, 8))
                                nc.scalar.activation(s, s, ACT.Sqrt).then_inc(sem("odstd"), 1)
                        else:
                            if j == NQ:
                                act.wait_ge(sem("odvar"), NQ)
                                s = view(small, RS + ((NQ - 1) % 4) * 8, (1, 8))
                                nc.scalar.activation(s, s, ACT.Sqrt).then_inc(sem("odstd"), 1)
                            nc.scalar.activation(view(ring, t * SLOT + (cb - 4) * 512, (1, 512)), bank(j % 4), ACT.Copy
                                                 ).then_inc(sem("v_out"), 1)
                        if 2 <= j < NQ + 2:
                            turned(j - 2)

                @block.vector
                def _(dve):
                    dve.wait_ge(sem("odgain_in"), 32)
                    gq = view(small, MISC, (1, HD))
                    nc.vector.tensor_scalar(gq, gq, HD ** -0.5, None, ALU.mult).then_inc(sem("odgain"), 1)
                    dve.wait_ge(sem("odgain"), 1)

                    def finish(j):
                        s = view(small, RS + (j % 4) * 8, (1, 8))
                        dve.wait_ge(sem("odstd"), j + 1)
                        nc.vector.reciprocal(s, s).then_inc(sem("odrstd"), 1)
                        dve.wait_ge(sem("odrstd"), j + 1)
                        nc.vector.tensor_tensor(tm(j), tm(j), view(small, RS + (j % 4) * 8, (1, 8), (0, HD)), ALU.mult
                                                ).then_inc(sem("odmul"), 1)
                        dve.wait_ge(sem("odmul"), j + 1)
                        g = view(small, MISC + (0 if jobs[j][0] < 2 else HD), (0, 8), (1, HD))
                        nc.vector.tensor_tensor(tm(j), tm(j), g, ALU.mult).then_inc(sem("qk_ready"), 1)

                    for j in range(NQ):
                        s = view(small, RS + (j % 4) * 8, (1, 8))
                        dve.wait_ge(sem("odsq"), j + 1)
                        nc.vector.tensor_reduce(s, view(arena, PT1_AT - 512 + (j % 2) * 512, (HD, 8), (1, HD)), AX.X,
                                                ALU.add).then_inc(sem("odsum"), 1)
                        dve.wait_ge(sem("odsum"), j + 1)
                        nc.vector.tensor_scalar(s, s, 1.0 / HD, EPS, ALU.mult, ALU.add).then_inc(sem("odvar"), 1)
                        if j >= 1:
                            finish(j - 1)
                    finish(NQ - 1)

        stages = [
            lambda: ada_stage(),
            lambda: norm_stage(0, 1, TT),
            lambda: even_in_proj(),
            lambda: even_qk_fourier(),
            lambda: attention(0),
            lambda: out_proj(0, load_first(0, range(0, 5))),
            lambda: norm_stage(0, 2, TT, load_first(0, range(5, 12))),
            lambda: top_k(0),
            lambda: mixture(0, range(0, 12)),
            lambda: ffn_residual(0, load_odd),
            lambda: norm_stage(1, 1, TT),
            lambda: odd_in_proj(),
            lambda: attention(1),
            lambda: out_proj(1, load_first(1, range(8, 12))),
            lambda: norm_stage(1, 2, XT, load_first(1, range(0, 8))),
            lambda: top_k(1),
            lambda: mixture(1, range(0, 12)),
            lambda: ffn_residual(1),
        ]
        for number, stage in enumerate(stages[:upto]):
            if number == 9:
                nc.clear_and_free_semaphores([sems.pop(name) for name in list(sems)])
                nc.all_engine_barrier()
            stage()
        if taps:
            named = {"resid": resid, "arena": arena, "ring": ring, "small": small, "mods": mods, "h2x": h2x, "offs": offs}
            with nc.Block() as block:
                @block.sync
                def _(sp):
                    for i, (name, dst, col, w, parts) in enumerate(taps):
                        t = named[name]
                        src = t if name in ("mods", "h2x") else view(t, col, (1, w), n=parts)
                        sp.dma_start(dst, src).then_inc(sem("tapped"), 16)
                    sp.wait_ge(sem("tapped"), 16 * len(taps))


def shape_constants():
    n = np.arange(SEQ)
    ang = 2.0 * np.pi * ((n[:, None] * n[None, :]) % SEQ) / SEQ
    dft = np.stack([np.cos(ang), np.sin(ang)]).astype(np.float32)
    inv = np.power(np.float32(10000.0), -np.arange(16, dtype=np.float32) / np.float32(16)).astype(np.float32)
    row, col = (n // GRID_W).astype(np.float32), (n % GRID_W).astype(np.float32)
    a = np.concatenate([row[:, None] * inv, col[:, None] * inv], axis=-1)
    co, si = np.cos(a).astype(np.float32), np.sin(a).astype(np.float32)
    rope = np.concatenate([co, co, -si, si], axis=1).astype(np.float32)
    i, j = np.arange(P)[:, None], np.arange(P)[None, :]
    swa = np.concatenate([np.where(j >= i, 0.0, -1e30), np.where(j <= i, 0.0, -1e30)], axis=1).astype(np.float32)
    na = np.zeros((P, 3, 256), np.float32)
    p, key = np.arange(P), np.arange(256)
    for v, t in enumerate((0, 1, 3)):
        cq = 16 * t + 8 * (p // 64) + p % 8
        ck = 16 * t - 8 + 8 * (key // 64) + key % 8
        start = np.clip(cq - NA_COLS // 2, 0, GRID_W - NA_COLS)
        ok = (ck[None, :] >= start[:, None]) & (ck[None, :] < start[:, None] + NA_COLS)
        na[:, v] = np.where(ok, 0.0, -1e30)
    return {"dft": dft, "rope": rope, "ident": np.eye(P, dtype=np.float32),  "swa_mask": swa, "na_mask": na.reshape(P, 768), "iota": np.arange(SEQ, dtype=np.float32)}


def layout(inputs):
    a = {k: np.ascontiguousarray(np.asarray(v)) for k, v in inputs.items()}
    a["c"] = a["c"].reshape(D)
    rpb = a.pop("od_rpb")[0]
    wide = np.zeros((NH, RPB_R, RPB_PAD), rpb.dtype)
    wide[:, :, 8:8 + RPB_C] = rpb
    flat = np.concatenate([wide.reshape(NH, -1), np.zeros((NH, RPB_PAD), rpb.dtype)], axis=1)
    p = np.arange(P)
    start = (7 - (p // 8) % 8) * RPB_PAD + 15 - (8 * (p // 64) + p % 8)
    a["rpb_pad"] = np.stack([flat[:, s:s + 8 * RPB_PAD] for s in start], axis=1)
    a.update(shape_constants())
    return a


_INS = ["x", "c", "ctx", "c_ctx", "ada_w", "ada_b", "norm1_g", "norm2_g", "router_w", "exp_w_gate", "exp_w_up",
        "exp_w_down", "ev_w_in", "ev_w_out", "ev_q_gain", "ev_k_gain", "ev_sink", "od_w_in", "od_w_out",
        "od_q_gain", "od_k_gain", "rpb_pad", "dft", "rope", "ident", "swa_mask", "na_mask", "iota"]


def kernel(**inputs):
    import concourse.bacc as bacc
    from concourse.bass_utils import run_bass_kernel_spmd

    a = layout(inputs)
    nc = bacc.Bacc("TRN2", target_bir_lowering=False, num_devices=1)
    arrays, args = {}, []
    for name in _INS:
        arrays[f"in_{name}"] = np.ascontiguousarray(a[name])
        args.append(nc.dram_tensor(f"in_{name}", a[name].shape, mybir.dt.from_np(a[name].dtype),
                                   kind="ExternalInput").ap())
    args.append(nc.dram_tensor("out_x", (1, SEQ, D), F32, kind="ExternalOutput").ap())
    program(nc, *args)
    r = run_bass_kernel_spmd(nc, [arrays], core_ids=[0])
    return r.results[0]["out_x"]
```

```python
from contextlib import ExitStack

import numpy as np

import concourse.bass as bass
from concourse import mybir

F32 = mybir.dt.float32
BF16 = mybir.dt.bfloat16
U32 = mybir.dt.uint32
ACT = mybir.ActivationFunctionType
ALU = mybir.AluOpType
AX = mybir.AxisListType

P = 128
D = 1024
KT = D // P
SEQ, CTX = 512, 256
XT, CT = SEQ // P, CTX // P
TT = XT + CT
TOK = SEQ + CTX
LAYERS = 2
HD = 64
GRID_W = 64
ROWS = SEQ // GRID_W
FW = D // 2
FG = FW // P
QH, KVH = 8, 2
QK0 = (QH + KVH) * HD
EV_IN = FW + QK0 + KVH * HD
NH = D // HD
NA_COLS = 16
RPB_R, RPB_C = 2 * 8 - 1, 2 * NA_COLS - 1
RPB_PAD = 48
EXPERTS = 16
CAPX, CAPC = 2 * SEQ // EXPERTS, 2 * CTX // EXPERTS
SLOT = 1024
SLOTS = 24
EPS = 1e-6
SH1, SC1, G1, SH2, SC2, G2 = range(6)

ARENA = 21504
HT_AT = 0
AB_AT = 6656
HB_AT = 10752
FT_AT, QKV_AT = 12800, 15872
QN_AT, TMP_AT, QT_AT, KT0_AT = 0, 3840, 6656, 9728
GAIN_AT = 10496
FOUR_AT = FT_AT
AT0_AT, P0_AT, PT0_AT = 0, 3072, 10496
QT1_AT, TM1_AT, KT1_AT = 6656, 10752, 12800
AT1_AT, BM1_AT, BR1_AT, P1_AT, BM1B_AT, PT1_AT = 0, 4096, 5632, 10752, 18944, 20480
GB_AT, YT_AT = 16384, 18432
G2_AT = 0


def program(nc, x, c, ctx, c_ctx, ada_w, ada_b, norm1_g, norm2_g, router_w, exp_w_gate, exp_w_up,
            exp_w_down, ev_w_in, ev_w_out, ev_q_gain, ev_k_gain, ev_sink, od_w_in, od_w_out,
            od_q_gain, od_k_gain, rpb_pad, dft, rope, ident_in, swa_mask_in, na_mask_in,
            iota_in, out, upto=99, taps=()):
    stack = ExitStack()
    with stack:
        def sb(name, shape, dt=F32):
            return stack.enter_context(nc.sbuf_tensor(name, shape, dt))

        sems = {}

        def sem(name):
            if name not in sems:
                sems[name] = nc.alloc_semaphore(name=name)
            return sems[name]

        def view(t, col, *dims, p=0, n=P):
            row = t.shape[1] if len(t.shape) == 2 else int(np.prod(t.shape[1:]))
            return bass.AP(t, p * row + col, [[row, n], *[list(d) for d in dims]])

        resid = sb("resid", [P, TT * D])
        ring = sb("ring", [P, SLOTS * SLOT])
        arena = sb("arena", [P, ARENA])
        ident = sb("ident", [P, P])
        ident16 = sb("ident16", [P, P], BF16)
        swa_mask = sb("swa_mask", [P, 2 * P], BF16)
        router = sb("router", [P, KT * EXPERTS])
        small = sb("small", [P, 432])
        offs = sb("offs", [P, 2 * (EXPERTS + 1)], U32)
        ps = stack.enter_context(nc.psum_tensor("ps", [P, 8 * 512], F32))

        def bank(b, col=0, *dims, p=0, n=P):
            return view(ps, b * 512 + col, *(dims or ((1, 512),)), p=p, n=n)

        mods = nc.dram_tensor("mods", [LAYERS * 2, 6 * D], F32, kind="Internal").ap()
        h2x = nc.dram_tensor("h2x", [SEQ, D], F32, kind="Internal").ap()
        h2c = nc.dram_tensor("h2c", [CTX, D], F32, kind="Internal").ap()

        def mod_row(layer, stream, vec):
            return mods[2 * layer + stream, vec * D:(vec + 1) * D].partition_broadcast(P)

        def ring_load(eng, slot, cols, src, done):
            k = src.shape[0] // P
            eng.dma_start(view(ring, slot * SLOT, (cols, k), (1, cols)),
                          src.rearrange("(k p) n -> p k n", p=P)).then_inc(done, 16)

        SS, QSS, SINK, SOFT = 0, 8, 72, 96
        MISC = 300

        SILU = 0

        def ada_load(sp, layer, k, group):
            sp.dma_start(view(ring, group * 6 * SLOT, (1, 6 * D)),
                         ada_w[layer].rearrange("(p k) n -> k p n", k=KT)[k]
                         ).then_inc(sem(f"ada{layer}_in{group}"), 16)

        def ada_bias_load(sp, layer, bias, gain):
            for g in range(4):
                sp.dma_start(view(arena, bias, (512, 3), (1, 512), p=32 * g, n=2),
                             ada_b[layer].rearrange("(b g n) -> g b n", g=4, n=512)[g]
                             .partition_broadcast(2)).then_inc(sem(f"bias{layer}_in"), 16)
                src, at = (norm2_g, g) if g < 2 else (norm1_g, g - 2)
                sp.dma_start(view(arena, gain, (1, 512), p=32 * g, n=2),
                             src[layer, at * 512:(at + 1) * 512].partition_broadcast(2)
                             ).then_inc(sem(f"bias{layer}_in"), 16)

        def ada_product(pe, layer, k, groups, bank0):
            pe.wait_ge(sem(f"ada{layer}_in{k % groups}"), 16 * (k // groups + 1))
            for b in range(3):
                for g in range(4):
                    last = nc.tensor.matmul(bank(bank0 + b, 0, (1, 512), p=32 * g, n=2),
                                            view(router, SILU + k, (KT, 2)),
                                            view(ring, (k % groups) * 6 * SLOT + (b * 4 + g) * 512, (1, 512)),
                                            start=(k == 0), stop=(k == KT - 1))
            last.then_inc(sem(f"ada{layer}_used"), 1)

        def ada_sums(dve, layer, bias, gain, bank0):
            dve.wait_ge(sem(f"bias{layer}_in"), 16 * 8)
            dve.wait_ge(sem(f"ada{layer}_used"), KT)
            for g in range(4):
                mod = view(arena, bias, (1, 1536), p=32 * g, n=2)
                nc.vector.tensor_tensor(mod, bank(bank0, 0, (1, 1536), p=32 * g, n=2), mod, ALU.add
                                        ).then_inc(sem(f"mod_sum{layer}"), 1)
                dve.wait_ge(sem(f"mod_sum{layer}"), g + 1)
                part = view(arena, bias + (1024 if g < 2 else 0), (1, 512), p=32 * g, n=2)
                nc.vector.scalar_tensor_tensor(part, part, 1.0, view(arena, gain, (1, 512), p=32 * g, n=2),
                                               ALU.add, ALU.mult).then_inc(sem(f"mod_ready{layer}"), 1)

        def ada_save(sp, layer, bias):
            for g in range(4):
                sp.wait_ge(sem(f"mod_ready{layer}"), g + 1)
                sp.dma_start(mods[2 * layer:2 * layer + 2, :].rearrange("s (b g n) -> g s b n", g=4, n=512)[g],
                             view(arena, bias, (512, 3), (1, 512), p=32 * g, n=2)
                             ).then_inc(sem(f"mods{layer}_out"), 16)

        def ada_stage():
            GROUPS = 4
            CIN, BIAS, GAIN, MASK = 0, 64, 4096, 11520
            with nc.Block() as block:
                @block.sync
                def _(sp):
                    for s, src in enumerate((c, c_ctx)):
                        sp.dma_start(view(arena, CIN + s * KT, (1, KT)),
                                     src.rearrange("(p k) -> p k", k=KT)).then_inc(sem("c_in"), 16)
                    for k in range(KT):
                        if k >= GROUPS:
                            sp.wait_ge(sem("ada0_used"), k - GROUPS + 1)
                        ada_load(sp, 0, k, k % GROUPS)
                        if k == 3:
                            ada_bias_load(sp, 0, BIAS, GAIN)
                    sp.dma_start(view(resid, 0, (D, XT), (1, D)),
                                 x[0].rearrange("(t p) d -> p t d", p=P)).then_inc(sem("x_in"), 16)
                    sp.dma_start(view(resid, XT * D, (D, CT), (1, D)),
                                 ctx[0].rearrange("(t p) d -> p t d", p=P)).then_inc(sem("x_in"), 16)
                    sp.dma_start(ident[:, :], ident_in).then_inc(sem("const_in"), 16)
                    sp.dma_start(view(arena, MASK, (1, 2 * P)), swa_mask_in).then_inc(sem("const_in"), 16)
                    sp.dma_start(view(small, SINK, (1, QH)), ev_sink[0].partition_broadcast(P)
                                 ).then_inc(sem("const_in"), 16)
                    ada_save(sp, 0, BIAS)
                    sp.wait_ge(sem("mods0_out"), 16 * 4)

                @block.scalar
                def _(act):
                    act.wait_ge(sem("c_in"), 32)
                    nc.scalar.activation(view(router, SILU, (1, 2 * KT)), view(arena, CIN, (1, 2 * KT)),
                                         ACT.Silu).then_inc(sem("silu_c"), 1)

                @block.tensor
                def _(pe):
                    pe.wait_ge(sem("silu_c"), 1)
                    for k in range(KT):
                        ada_product(pe, 0, k, GROUPS, 0)

                @block.vector
                def _(dve):
                    ada_sums(dve, 0, BIAS, GAIN, 0)
                    dve.wait_ge(sem("const_in"), 48)
                    nc.vector.tensor_copy(ident16[:, :], ident[:, :])
                    nc.vector.tensor_copy(swa_mask[:, :], view(arena, MASK, (1, 2 * P)))

        def load_even(sp):
            for k in range(KT):
                sp.dma_start(view(ring, k * EV_IN, (1, EV_IN)), ev_w_in[0, k * P:(k + 1) * P, :]
                             ).then_inc(sem("evin_in"), 16)
            for s in range(2):
                sp.dma_start(view(ring, 10 * SLOT + s * 2048, (512, 4), (1, 512)),
                             dft[s].rearrange("(t p) m -> p t m", p=P)).then_inc(sem("dft_in"), 16)
            for k in range(4):
                sp.dma_start(view(ring, (14 + k) * SLOT, (1, D)), ev_w_out[0, k * P:(k + 1) * P, :]
                             ).then_inc(sem("evout_in"), 16)
            for pr in range(4):
                for a in range(2):
                    r0 = FW + (pr + 4 * a) * HD
                    sp.dma_start(view(ring, (18 + pr) * SLOT, (1, D), p=64 * a, n=64),
                                 ev_w_out[0, r0:r0 + HD, :]).then_inc(sem("evout_in"), 16)

        def ab_at(stream, vec):
            return view(arena, AB_AT + (2 * stream + vec) * D, (1, D))

        def load_modulation(sp, layer, which):
            for s in range(1 if (layer, which) == (1, 2) else 2):
                for v, vec in enumerate((SC1, SH1) if which == 1 else (SC2, SH2)):
                    sp.dma_start(ab_at(s, v), mod_row(layer, s, vec)).then_inc(sem(f"ab_in{layer}{which}"), 16)

        def square_sum(act, n, t):
            if t >= 2:
                act.wait_ge(sem("sq_done" + n), t - 1)
            nc.scalar.activation(view(arena, HB_AT + (t % 2) * D, (1, D)), view(resid, t * D, (1, D)), ACT.Square,
                                 accum_out=view(small, SS + t, (1, 1))).then_inc(sem("sq_done" + n), 1)

        def norm_stage(layer, which, tiles, prefetch=None):
            n = f"{layer}{which}"
            width = 832 if (layer, which) == (1, 1) else TOK
            blocked = width == 832
            streams = 2 if tiles == TT else 1

            def hb(t):
                return view(arena, HB_AT + (t % 2) * D, (1, D))

            def res(t):
                return view(resid, t * D, (1, D))

            LG = SOFT
            LGT = HB_AT + 2 * D
            AFF_T = HB_AT
            with nc.Block() as block:
                @block.sync
                def _(sp):
                    if n == "01":
                        load_modulation(sp, layer, which)
                    if which == 2:
                        sp.dma_start(view(router, 0, (EXPERTS, KT), (1, EXPERTS)),
                                     router_w[layer].rearrange("(k p) e -> p k e", p=P)).then_inc(sem("rt_in" + n), 16)
                    if which == 2:
                        for t in range(tiles):
                            sp.wait_ge(sem("h_ready" + n), t + 1)
                            dst = h2x[t * P:(t + 1) * P, :] if t < XT else h2c[(t - XT) * P:(t - XT + 1) * P, :]
                            sp.dma_start(dst, hb(t)).then_inc(sem(f"h_saved{n}{t % 2}"), 16)
                    if prefetch:
                        prefetch(sp)
                    if which == 2:
                        for par in range(2):
                            sp.wait_ge(sem(f"h_saved{n}{par}"), 16 * (tiles // 2))

                @block.scalar
                def _(act):
                    if n == "01":
                        act.wait_ge(sem("x_in"), 32)
                        for t in range(tiles):
                            square_sum(act, n, t)
                    act.wait_ge(sem("var_ready" + n), 1)
                    nc.scalar.activation(view(small, SS, (1, tiles)), view(small, SS, (1, tiles)), ACT.Sqrt
                                         ).then_inc(sem("std_ready" + n), 1)
                    for t in range(tiles):
                        act.wait_ge(sem("hT_ps" + n), t + 1)
                        b0 = 2 * (t % 2)
                        if blocked and t < XT:
                            for r in range(2):
                                for half in range(2):
                                    last = nc.scalar.activation(
                                        view(arena, HT_AT + 4 * half * width + (2 * t + r) * 8,
                                             (width, 4), (64, 8), (1, 8)),
                                        bank(b0 + half, r * 64, (P, 4), (8, 8), (1, 8)), ACT.Copy)
                        else:
                            at = t * P + (64 if blocked else 0)
                            last = nc.scalar.activation(view(arena, HT_AT + at, (width, KT), (1, P)),
                                                        bank(b0, 0, (P, KT), (1, P)), ACT.Copy)
                        last.then_inc(sem("hT_out" + n), 1)
                    if which == 2:
                        act.wait_ge(sem("lg_shift" + n), 1)
                        nc.scalar.activation(view(small, LG, (1, tiles * EXPERTS)), view(small, LG, (1, tiles * EXPERTS)),
                                             ACT.Exp).then_inc(sem("lg_exp" + n), 1)

                @block.vector
                def _(dve):
                    dve.wait_ge(sem("sq_done" + n), tiles)
                    s = view(small, SS, (1, tiles))
                    nc.vector.tensor_scalar(s, s, 1.0 / D, EPS, ALU.mult, ALU.add).then_inc(sem("var_ready" + n), 1)
                    dve.wait_ge(sem("std_ready" + n), 1)
                    nc.vector.reciprocal(s, s).then_inc(sem("rstd_ready" + n), 1)
                    dve.wait_ge(sem("rstd_ready" + n), 1)
                    dve.wait_ge(sem("ab_in" + n), 32 * streams)
                    for t in range(tiles):
                        stream = 0 if t < XT else 1
                        if t >= 2:
                            dve.wait_ge(sem("hT_ps" + n), t - 1)
                            if which == 2:
                                dve.wait_ge(sem(f"h_saved{n}{t % 2}"), 16 * (t // 2))
                        nc.vector.scalar_tensor_tensor(hb(t), res(t), view(small, SS + t, (1, 1)), ab_at(stream, 0),
                                                       ALU.mult, ALU.mult).then_inc(sem("h_scaled" + n), 1)
                        dve.wait_ge(sem("h_scaled" + n), t + 1)
                        nc.vector.tensor_tensor(hb(t), hb(t), ab_at(stream, 1), ALU.add).then_inc(sem("h_ready" + n), 1)
                    if blocked:
                        dve.wait_ge(sem("hT_out" + n), XT)
                        nc.vector.tensor_copy(view(arena, HT_AT + SEQ, (width, KT), (1, 64)),
                                              view(arena, HT_AT, (width, KT), (1, 64))).then_inc(sem("wrap" + n), 1)
                    if which == 2:
                        lg = view(small, LG, (EXPERTS, tiles), (1, EXPERTS))
                        mx = view(small, MISC, (1, tiles))
                        dve.wait_ge(sem("lgT_ps" + n), 1)
                        nc.vector.tensor_copy(view(arena, LGT, (1, tiles * P), n=EXPERTS),
                                              bank(4, 0, (1, tiles * P), n=EXPERTS)).then_inc(sem("lgT_out" + n), 1)
                        dve.wait_ge(sem("lg_ps" + n), 1)
                        nc.vector.tensor_reduce(mx, bank(7, 0, (EXPERTS, tiles), (1, EXPERTS)), AX.X, ALU.max
                                                ).then_inc(sem("lg_step" + n), 1)
                        dve.wait_ge(sem("lg_step" + n), 1)
                        nc.vector.tensor_tensor(lg, bank(7, 0, (EXPERTS, tiles), (1, EXPERTS)),
                                                view(small, MISC, (1, tiles), (0, EXPERTS)), ALU.subtract
                                                ).then_inc(sem("lg_shift" + n), 1)
                        dve.wait_ge(sem("lg_exp" + n), 1)
                        nc.vector.tensor_reduce(view(small, MISC + 8, (1, tiles)), lg, AX.X, ALU.add
                                                ).then_inc(sem("lg_step" + n), 1)
                        dve.wait_ge(sem("lg_step" + n), 2)
                        nc.vector.reciprocal(view(small, MISC + 16, (1, tiles)), view(small, MISC + 8, (1, tiles))
                                             ).then_inc(sem("lg_step" + n), 1)
                        dve.wait_ge(sem("lg_step" + n), 3)
                        nc.vector.tensor_tensor(lg, lg, view(small, MISC + 16, (1, tiles), (0, EXPERTS)), ALU.mult
                                                ).then_inc(sem("aff_ready" + n), 1)
                        dve.wait_ge(sem("affT_ps" + n), 1)
                        for par in range(2):
                            dve.wait_ge(sem(f"h_saved{n}{par}"), 16 * (tiles // 2))
                        nc.vector.tensor_copy(view(arena, AFF_T, (1, tiles * P), n=EXPERTS),
                                              bank(5, 0, (1, tiles * P), n=EXPERTS)).then_inc(sem("affT" + n), 1)

                @block.tensor
                def _(pe):
                    def logits(t):
                        pe.wait_ge(sem("hT_out" + n), t + 1)
                        for k in range(KT):
                            last = nc.tensor.matmul(bank(4, t * P, (1, P), n=EXPERTS),
                                                    view(router, k * EXPERTS, (1, EXPERTS)),
                                                    view(arena, HT_AT + k * width + t * P, (1, P)),
                                                    start=(k == 0), stop=(k == KT - 1))
                        return last

                    if (layer, which) == (0, 1):
                        pe.wait_ge(sem("const_in"), 48)
                    for t in range(tiles):
                        if t == 0 and which == 2:
                            pe.wait_ge(sem("rt_in" + n), 16)
                        pe.wait_ge(sem("h_ready" + n), t + 1)
                        if t >= 2:
                            pe.wait_ge(sem("hT_out" + n), t - 1)
                        for k in range(KT):
                            last = nc.tensor.transpose(bank(2 * (t % 2), k * P, (1, P)),
                                                       view(arena, HB_AT + (t % 2) * D + k * P, (1, P)), ident[:, :])
                        last.then_inc(sem("hT_ps" + n), 1)
                        if which == 2 and t >= 1:
                            logits(t - 1)
                    if which == 2:
                        logits(tiles - 1).then_inc(sem("lgT_ps" + n), 1)
                        pe.wait_ge(sem("lgT_out" + n), 1)
                        for t in range(tiles):
                            last = nc.tensor.transpose(bank(7, t * EXPERTS, (1, EXPERTS)),
                                                       view(arena, LGT + t * P, (1, P), n=EXPERTS),
                                                       ident[0:EXPERTS, 0:EXPERTS])
                        last.then_inc(sem("lg_ps" + n), 1)
                        pe.wait_ge(sem("aff_ready" + n), 1)
                        for t in range(tiles):
                            last = nc.tensor.transpose(bank(5, t * P, (1, P), n=EXPERTS),
                                                       view(small, LG + t * EXPERTS, (1, EXPERTS)), ident[:, :])
                        last.then_inc(sem("affT_ps" + n), 1)

        def job_stage(n, jobs, waits, prefetch=None, vector_first=None):
            BANKS = 8

            def drained(eng, j):
                eng.wait_ge(sem(("act_out" if j % 2 == 0 else "dve_out") + n), j // 2 + 1)

            with nc.Block() as block:
                if prefetch:
                    @block.sync
                    def _(sp):
                        prefetch(sp)

                @block.tensor
                def _(pe):
                    for s, v in waits:
                        pe.wait_ge(sem(s), v)
                    for j, (mms, _) in enumerate(jobs):
                        if j >= BANKS:
                            drained(pe, j - BANKS)
                        for (at, lhsT, rhs, start, stop) in mms:
                            col, dims, p0, np_ = at
                            last = nc.tensor.matmul(bank(j % BANKS, col, *dims, p=p0, n=np_), lhsT, rhs,
                                                    start=start, stop=stop)
                        last.then_inc(sem("job_done" + n), 1)

                @block.scalar
                def _(act):
                    for j in range(0, len(jobs), 2):
                        act.wait_ge(sem("job_done" + n), j + 1)
                        for dst, col, dims in jobs[j][1]:
                            last = nc.scalar.activation(dst, bank(j % BANKS, col, *dims), ACT.Copy)
                        last.then_inc(sem("act_out" + n), 1)

                @block.vector
                def _(dve):
                    for j in range(1, len(jobs), 2):
                        dve.wait_ge(sem("job_done" + n), j + 1)
                        for dst, col, dims in jobs[j][1]:
                            last = nc.vector.tensor_copy(dst, bank(j % BANKS, col, *dims))
                        last.then_inc(sem("dve_out" + n), 1)

        def even_in_proj():
            def hT(k, t0, w):
                return view(arena, HT_AT + k * TOK + t0, (1, w))

            def w_in(k, c0, w):
                return view(ring, k * EV_IN + c0, (1, w))

            jobs = []
            for g in range(FG):
                for t0, w in ((0, SEQ), (SEQ, CTX)):
                    mms = [((0, ((1, w),), 0, P), w_in(k, g * P, P), hT(k, t0, w), k == 0, k == KT - 1)
                           for k in range(KT)]
                    jobs.append((mms, [(view(arena, FT_AT + g * TOK + t0, (1, w)), 0, ((1, w),))]))
            for t in range(TT):
                for c0, w in ((0, 512), (512, 256)):
                    mms = [((0, ((1, w),), 0, P), hT(k, t * P, P), w_in(k, FW + c0, w), k == 0, k == KT - 1)
                           for k in range(KT)]
                    if c0 == 0:
                        drain = (view(arena, QKV_AT + t * 768, (HD, 2), (2 * HD, 4), (1, HD)),
                                 0, ((4 * HD, 2), (HD, 4), (1, HD)))
                    else:
                        drain = (view(arena, QKV_AT + t * 768 + c0, (1, w)), 0, ((1, w),))
                    jobs.append((mms, [drain]))
            job_stage("ei", jobs, [("evin_in", 16 * KT)], even_gains)

        def even_gains(sp):
            for h in range(QH + KVH):
                g = ev_q_gain if h < QH else ev_k_gain
                sp.dma_start(view(arena, GAIN_AT + h * HD, (1, HD)), g[0].partition_broadcast(P)
                             ).then_inc(sem("gain_in"), 16)
            sp.dma_start(view(ring, 22 * SLOT, (P, XT), (1, P)), rope.rearrange("(t p) n -> p t n", p=P)
                         ).then_inc(sem("gain_in"), 16)

        def even_qk_fourier():
            H = QH + KVH
            UC = 0

            def qk(t):
                return view(arena, QKV_AT + t * 768, (HD, H), (1, HD))

            def qn(t):
                return view(arena, QN_AT + t * QK0, (HD, H), (1, HD))

            def tmp(t):
                return view(arena, TMP_AT + (t % 2) * QK0, (HD, H), (1, HD))

            gain = view(arena, GAIN_AT, (HD, H), (1, HD))
            rows = view(small, QSS, (H, TT), (1, H))

            with nc.Block() as block:
                @block.scalar
                def _(act):
                    for t in range(TT):
                        if t >= 2:
                            act.wait_ge(sem("qsum"), t - 1)
                        nc.scalar.activation(tmp(t), qk(t), ACT.Square).then_inc(sem("qsq"), 1)
                    act.wait_ge(sem("qvar"), 1)
                    nc.scalar.activation(rows, rows, ACT.Sqrt).then_inc(sem("qstd"), 1)
                    for t in range(TT):
                        act.wait_ge(sem("f1_ps"), t + 1)
                        norm = (SEQ * P) ** -0.5 if t < XT else (CTX * P) ** -0.5
                        b0 = 4 + 2 * (t % 2)
                        nc.scalar.activation(view(ring, UC + t * SLOT, (P, FG), (1, P)),
                                             bank(b0, 0, (2 * P, FG), (1, P)), ACT.Copy, scale=norm)
                        nc.scalar.activation(view(ring, UC + t * SLOT + 512, (P, FG), (1, P)),
                                             bank(b0, P, (2 * P, FG), (1, P)), ACT.Copy, scale=-norm
                                             ).then_inc(sem("f1_out"), 1)
                    for j in range(2 * FG):
                        act.wait_ge(sem("f2_ps"), j + 1)
                        t0, w = (0, SEQ) if j % 2 == 0 else (SEQ, CTX)
                        nc.scalar.activation(view(arena, FOUR_AT + (j // 2) * TOK + t0, (1, w)),
                                             bank(4 + j % 4, 0, (1, w)), ACT.Copy).then_inc(sem("f2_out"), 1)
                    for t in range(TT):
                        act.wait_ge(sem("qT_ps"), t + 1)
                        b0 = 2 * (t % 2)
                        nc.scalar.activation(view(arena, QT_AT + t * P, (TOK, 4), (1, P)),
                                             bank(b0, 0, (P, 4), (1, P)), ACT.Copy)
                        nc.scalar.activation(view(arena, KT0_AT + t * P, (1, P)),
                                             bank(b0 + 1, 0, (1, P)), ACT.Copy).then_inc(sem("qT_out"), 1)

                @block.vector
                def _(dve):
                    dve.wait_ge(sem("gain_in"), 16 * 11)
                    g_q = view(arena, GAIN_AT, (1, QH * HD))
                    nc.vector.tensor_scalar(g_q, g_q, HD ** -0.5, None, ALU.mult).then_inc(sem("gain_ready"), 1)
                    for t in range(TT):
                        dve.wait_ge(sem("qsq"), t + 1)
                        nc.vector.tensor_reduce(view(small, QSS + t * H, (1, H)), tmp(t), AX.X, ALU.add
                                                ).then_inc(sem("qsum"), 1)
                    dve.wait_ge(sem("qsum"), TT)
                    nc.vector.tensor_scalar(rows, rows, 1.0 / HD, EPS, ALU.mult, ALU.add).then_inc(sem("qvar"), 1)
                    dve.wait_ge(sem("qstd"), 1)
                    nc.vector.reciprocal(rows, rows).then_inc(sem("qrstd"), 1)
                    dve.wait_ge(sem("qrstd"), 1)
                    dve.wait_ge(sem("gain_ready"), 1)
                    step = 0
                    for t in range(TT):
                        nc.vector.tensor_tensor(qk(t), qk(t), view(small, QSS + t * H, (1, H), (0, HD)), ALU.mult
                                                ).then_inc(sem("qstep"), 1)
                        step += 1
                        dve.wait_ge(sem("qstep"), step)
                        if t >= XT:
                            nc.vector.tensor_tensor(qn(t), qk(t), gain, ALU.mult).then_inc(sem("qn_ready"), 1)
                            continue
                        nc.vector.tensor_tensor(qk(t), qk(t), gain, ALU.mult).then_inc(sem("qgained"), 1)
                        dve.wait_ge(sem("qgained"), t + 1)
                        nc.vector.tensor_tensor(qn(t), qk(t), view(ring, 22 * SLOT + t * P, (0, H), (1, HD)), ALU.mult
                                                ).then_inc(sem("qstep"), 1)
                        step += 1
                        dve.wait_ge(sem("qstep"), step)
                        dve.wait_ge(sem("rot"), 2 * (t + 1))
                        nc.vector.tensor_tensor(qn(t), qn(t), tmp(t), ALU.add).then_inc(sem("qn_ready"), 1)

                @block.gpsimd
                def _(pool):
                    pool.wait_ge(sem("qrstd"), 1)
                    for t in range(XT):
                        pool.wait_ge(sem("qgained"), t + 1)
                        if t >= 2:
                            pool.wait_ge(sem("qn_ready"), t - 1)
                        for half in range(2):
                            nc.gpsimd.tensor_tensor(
                                view(arena, TMP_AT + (t % 2) * QK0 + half * 32, (HD, H), (1, 32)),
                                view(arena, QKV_AT + t * 768 + (32 - half * 32), (HD, H), (1, 32)),
                                view(ring, 22 * SLOT + t * P + HD + half * 32, (0, H), (1, 32)),
                                ALU.mult).then_inc(sem("rot"), 1)

                @block.tensor
                def _(pe):
                    pe.wait_ge(sem("dft_in"), 32)
                    cos_t, sin_t = 10 * SLOT, 12 * SLOT
                    for t in range(TT):
                        if t >= 2:
                            pe.wait_ge(sem("f1_out"), t - 1)
                        for g in range(FG):
                            for s, tab in enumerate((cos_t, sin_t)):
                                last = nc.tensor.matmul(bank(4 + 2 * (t % 2), g * 2 * P + s * P, (1, P)),
                                                        view(arena, FT_AT + g * TOK + t * P, (1, P)),
                                                        view(ring, tab, (4, P)), start=True, stop=True)
                        last.then_inc(sem("f1_ps"), 1)
                    for j in range(2 * FG):
                        g, is_ctx = j // 2, j % 2
                        if j == 0:
                            pe.wait_ge(sem("f1_out"), TT)
                        if j >= 4:
                            pe.wait_ge(sem("f2_out"), j - 3)
                        tiles, w, st = ((0, 1, 2, 3), SEQ, 1) if not is_ctx else ((4, 5), CTX, 2)
                        n_mm = 2 * len(tiles)
                        i = 0
                        for s, tab in enumerate((cos_t, sin_t)):
                            for t in tiles:
                                last = nc.tensor.matmul(bank(4 + j % 4, 0, (1, w)),
                                                        view(ring, UC + t * SLOT + s * 512 + g * P, (1, P)),
                                                        view(ring, tab + (t - tiles[0]) * 512, (st, w)),
                                                        start=(i == 0), stop=(i == n_mm - 1))
                                i += 1
                        last.then_inc(sem("f2_ps"), 1)
                    for t in range(TT):
                        pe.wait_ge(sem("qn_ready"), t + 1)
                        if t >= 2:
                            pe.wait_ge(sem("qT_out"), t - 1)
                        for pr in range(5):
                            last = nc.tensor.transpose(bank(2 * (t % 2), pr * P, (1, P)),
                                                       view(arena, QN_AT + t * QK0 + pr * P, (1, P)), ident[:, :])
                        last.then_inc(sem("qT_ps"), 1)

        ADA1_GROUPS = 2
        ADA1_BIAS, ADA1_GAIN = P0_AT, P0_AT + 1536

        def attention(layer):
            n = f"a{layer}"
            if layer == 0:
                units = [(pr, t) for t in range(TT) for pr in range(4)]
                p_at, pt_at = P0_AT, PT0_AT
                p_w = 640
            else:
                units = [(pr, t) for pr in range(NH // 2) for t in range(XT)]
                p_at, pt_at = P1_AT, PT1_AT
                p_w = 512

            def chunks(t):
                if layer == 1:
                    return [(SEQ, None), (SEQ + P, None), (((t - 1) % XT) * P, None), (t * P, None)]
                keys = [(SEQ, None), (SEQ + P, None)]
                if t < XT:
                    keys.append((t * P, None))
                    if t > 0:
                        keys.append(((t - 1) * P, 0))
                    if t < XT - 1:
                        keys.append(((t + 1) * P, 1))
                return keys

            def wide(u):
                return len(chunks(units[u][1])) > 4

            def sc_bank(u, a):
                return 2 * a if wide(u) else 2 * (u % 2) + a

            def may_overlap(u):
                return not wide(u) and not wide(u - 1)

            def probs(u, a, col=0, *dims):
                return view(arena, p_at + ((u % 2) * 2 + a) * p_w + col, *(dims or ((1, P),)))

            def pt(a, col, w):
                return view(arena, pt_at + a * p_w + col, (1, w))

            def v_tile(key, pr, a):
                if layer == 0:
                    return view(arena, QKV_AT + (key // P) * 768 + QK0 + a * HD, (1, HD))
                return view(ring, (key // P) * SLOT + (2 * pr + a) * HD, (1, HD))

            def qT(pr, t, a):
                at, w = (QT_AT, TOK) if layer == 0 else (QT1_AT, SEQ)
                return view(arena, at + pr * w + t * P, (1, P), p=64 * a, n=64)

            def kT(pr, key, w, a):
                at = KT0_AT if layer == 0 else KT1_AT + pr * TOK
                return view(arena, at + key, (1, w), p=64 * a, n=64)

            ST = SOFT

            def st(u, what, a=0, w=1):
                return view(small, ST + (u % 2) * 16 + what * 2 + a, (1, w))

            MX, NEG, SUM, ES, REC, SHS = 0, 1, 2, 3, 4, 5
            O_BANKS = (7,) if layer == 0 else (6, 7)

            with nc.Block() as block:
                if layer == 0:
                    @block.sync
                    def _(sp):
                        for k in range(ADA1_GROUPS):
                            ada_load(sp, 1, k, k)

                if layer == 1:
                    @block.sync
                    def _(sp):
                        for h in range(NH):
                            if h >= 2:
                                sp.wait_ge(sem("bm_read"), h - 1)
                            sp.dma_start(view(arena, BR1_AT + (h % 2) * 384, (1, 384)), rpb_pad[h]
                                         ).then_inc(sem(f"br_in{h % 2}"), 16)

                    @block.gpsimd
                    def _(pool):
                        pool.wait_ge(sem("na_mask_in"), 16)
                        for h in range(NH):
                            pr, a = h // 2, h % 2
                            pool.wait_ge(sem(f"br_in{h % 2}"), 16 * (h // 2 + 1))
                            if pr >= 2:
                                pool.wait_ge(sem("biased"), 8 * (pr - 1))
                            for v in range(3):
                                last = nc.gpsimd.tensor_tensor(
                                    view(arena, bm_at(pr) + (a * 3 + v) * 256, (64, 4), (8, 8), (1, 8)),
                                    view(arena, BR1_AT + (h % 2) * 384, (8, 4), (RPB_PAD, 8), (1, 8)),
                                    view(ring, 6 * SLOT + v * 256, (64, 4), (8, 8), (1, 8)), ALU.add)
                            last.then_inc(sem("bm_read"), 1)

                @block.tensor
                def _(pe):
                    def scores(u):
                        pr, t = units[u]
                        if u >= 1 and not may_overlap(u):
                            pe.wait_ge(sem("exp_done" + n), 2 * u)
                        elif u >= 2:
                            pe.wait_ge(sem("exp_done" + n), 2 * (u - 1))
                        keys = chunks(t)
                        segs = []
                        for i, (key, mask) in enumerate(keys):
                            if (segs and segs[-1][1] + segs[-1][2] == key and i * P % 512
                                    and segs[-1][3] is None and mask is None):
                                segs[-1][2] += P
                            else:
                                segs.append([i * P, key, P, mask])
                        for col, key, w, mask in segs:
                            for a in range(2):
                                last = nc.tensor.matmul(bank(sc_bank(u, a), col, (1, w)), qT(pr, t, a),
                                                        kT(pr, key, w, a), start=True, stop=mask is None,
                                                        skip_group_check=True)
                            if mask is not None:
                                for a in range(2):
                                    last = nc.tensor.matmul(bank(sc_bank(u, a), col, (1, w)), ident16[:, :],
                                                            view(swa_mask, mask * P, (1, P)), start=False, stop=True,
                                                            skip_group_check=True)
                        last.then_inc(sem("scores" + n), 1)

                    scores(0)
                    scored = 1
                    if may_overlap(1):
                        scores(1)
                        scored = 2
                    for u, (pr, t) in enumerate(units):
                        nk = len(chunks(t))
                        if scored == u + 1 < len(units):
                            scores(u + 1)
                            scored = u + 2
                        for a in range(2):
                            pe.wait_ge(sem("p_ready" + n), 2 * u + a + 1)
                            if u >= 1 and a == 0:
                                pe.wait_ge(sem("pt_act" + n), u)
                                pe.wait_ge(sem("pt_dve" + n), u)
                            for i in range(nk):
                                at = (4 + a, i * P) if i < 4 else (6, a * P)
                                last = nc.tensor.transpose(bank(at[0], at[1], (1, P)), probs(u, a, i * P), ident[:, :])
                            last.then_inc(sem("pt_ps" + n), 1)
                        if scored == u + 2 < len(units) and may_overlap(u + 2):
                            scores(u + 2)
                            scored = u + 3
                        pe.wait_ge(sem("pt_act" + n), u + 1)
                        pe.wait_ge(sem("pt_dve" + n), u + 1)
                        if u >= len(O_BANKS):
                            pe.wait_ge(sem("o_out" + n), u + 1 - len(O_BANKS))
                        for i, (key, _) in enumerate(chunks(t)):
                            for a in range(2):
                                last = nc.tensor.matmul(bank(O_BANKS[u % len(O_BANKS)], 0, (1, P), p=64 * a, n=64),
                                                        v_tile(key, pr, a), pt(a, i * P, P),
                                                        start=(i == 0), stop=(i == nk - 1))
                        last.then_inc(sem("o_ps" + n), 1)

                @block.vector
                def _(dve):
                    steps = [0]

                    def stepped(ins):
                        steps[0] += 1
                        ins.then_inc(sem("dstep" + n), 1)
                        dve.wait_ge(sem("dstep" + n), steps[0])

                    def pt_out(u):
                        w = len(chunks(units[u][1])) * P
                        dve.wait_ge(sem("pt_ps" + n), 2 * u + 2)
                        if u >= 1:
                            dve.wait_ge(sem("o_ps" + n), u)
                        nc.vector.tensor_copy(pt(1, 0, min(w, 512)), bank(5, 0, (1, min(w, 512)))
                                              ).then_inc(sem("pt_dve" + n), 1)

                    for u, (pr, t) in enumerate(units):
                        w = len(chunks(t)) * P
                        dve.wait_ge(sem("scores" + n), u + 1)
                        if layer == 1:
                            if t == 0:
                                dve.wait_ge(sem("bm_read"), 2 * pr + 2)
                            v = 0 if t == 0 else 2 if t == XT - 1 else 1
                            for a in range(2):
                                s = bank(sc_bank(u, a), 256, (1, 256))
                                nc.vector.tensor_tensor(s, s, view(arena, bm_at(pr) + (a * 3 + v) * 256, (1, 256)),
                                                        ALU.add).then_inc(sem("biased"), 1)
                            dve.wait_ge(sem("biased"), 2 * u + 2)
                        for a in range(2):
                            last = nc.vector.tensor_reduce(st(u, MX, a), bank(sc_bank(u, a), 0, (1, w)), AX.X, ALU.max)
                            stepped(last)
                        if layer == 0:
                            sk = view(small, SINK + pr, (4, 2))
                            stepped(nc.vector.tensor_tensor(st(u, MX, 0, 2), st(u, MX, 0, 2), sk, ALU.max))
                            stepped(nc.vector.tensor_tensor(st(u, SHS, 0, 2), sk, st(u, MX, 0, 2), ALU.subtract))
                        nc.vector.tensor_scalar(st(u, NEG, 0, 2), st(u, MX, 0, 2), -1.0, None, ALU.mult
                                                ).then_inc(sem("neg" + n), 1)
                        if u >= 1:
                            pt_out(u - 1)
                        dve.wait_ge(sem("exp_done" + n), 2 * u + 2)
                        if layer == 0:
                            dve.wait_ge(sem("es" + n), u + 1)
                            stepped(nc.vector.tensor_tensor(st(u, SUM, 0, 2), st(u, SUM, 0, 2), st(u, ES, 0, 2),
                                                            ALU.add))
                        stepped(nc.vector.reciprocal(st(u, REC, 0, 2), st(u, SUM, 0, 2)))
                        for a in range(2):
                            pp = probs(u, a, 0, (1, w))
                            nc.vector.tensor_scalar(pp, pp, st(u, REC, a), None, ALU.mult
                                                    ).then_inc(sem("p_ready" + n), 1)
                    pt_out(len(units) - 1)

                @block.scalar
                def _(act):
                    def tail(u):
                        pr, t = units[u]
                        w = len(chunks(t)) * P
                        act.wait_ge(sem("pt_ps" + n), 2 * u + (2 if w > 512 else 1))
                        if u >= 1:
                            act.wait_ge(sem("o_ps" + n), u)
                        last = nc.scalar.activation(pt(0, 0, min(w, 512)), bank(4, 0, (1, min(w, 512))), ACT.Copy)
                        if w > 512:
                            last = nc.scalar.activation(view(arena, pt_at + 512, (p_w, 2), (1, P)),
                                                        bank(6, 0, (P, 2), (1, P)), ACT.Copy)
                        last.then_inc(sem("pt_act" + n), 1)

                    def out_copy(u):
                        pr, t = units[u]
                        act.wait_ge(sem("o_ps" + n), u + 1)
                        if layer == 0:
                            nc.scalar.activation(view(arena, AT0_AT + pr * TOK + t * P, (1, P)),
                                                 bank(O_BANKS[u % len(O_BANKS)], 0, (1, P)), ACT.Copy).then_inc(sem("o_out" + n), 1)
                        else:
                            nc.scalar.activation(view(arena, AT1_AT + pr * SEQ + t * 16, (8, 2), (64, 8), (1, 8)),
                                                 bank(O_BANKS[u % len(O_BANKS)], 0, (64, 2), (8, 8), (1, 8)), ACT.Copy
                                                 ).then_inc(sem("o_out" + n), 1)

                    for u, (pr, t) in enumerate(units):
                        w = len(chunks(t)) * P
                        act.wait_ge(sem("neg" + n), u + 1)
                        if u >= 2:
                            act.wait_ge(sem("pt_ps" + n), 2 * (u - 1))
                        for a in range(2):
                            nc.scalar.activation(probs(u, a, 0, (1, w)), bank(sc_bank(u, a), 0, (1, w)), ACT.Exp,
                                                 bias=st(u, NEG, a), accum_out=st(u, SUM, a)
                                                 ).then_inc(sem("exp_done" + n), 1)
                        if layer == 0:
                            nc.scalar.activation(st(u, ES, 0, 2), st(u, SHS, 0, 2), ACT.Exp).then_inc(sem("es" + n), 1)
                        if u >= 2:
                            out_copy(u - 2)
                        if u >= 1:
                            tail(u - 1)
                    out_copy(len(units) - 2)
                    tail(len(units) - 1)
                    out_copy(len(units) - 1)

        def bm_at(pr):
            return BM1_AT if pr % 2 == 0 else BM1B_AT

        def out_proj(layer, prefetch=None):
            n = f"o{layer}"
            tiles = TT if layer == 0 else XT
            w_slot = 14 if layer == 0 else 8

            def lhsT(k, t):
                if layer == 0:
                    at = FOUR_AT + k * TOK if k < 4 else AT0_AT + (k - 4) * TOK
                    return view(arena, at + t * P, (1, P))
                return view(arena, AT1_AT + k * SEQ + t * P, (1, P))

            jobs = [(t, h) for t in range(tiles) for h in range(2)]
            with_ada = layer == 0
            BANKS = 5 if with_ada else 8
            with nc.Block() as block:
                @block.sync
                def _(sp):
                    for s in range(2 if tiles == TT else 1):
                        sp.dma_start(view(arena, GB_AT + s * D, (1, D)), mod_row(layer, s, G1)
                                     ).then_inc(sem("g_in" + n), 16)
                    load_modulation(sp, layer, 2)
                    if with_ada:
                        ada_bias_load(sp, 1, ADA1_BIAS, ADA1_GAIN)
                        for k in range(ADA1_GROUPS, KT):
                            sp.wait_ge(sem("ada1_used"), k - ADA1_GROUPS + 1)
                            ada_load(sp, 1, k, k % ADA1_GROUPS)
                        ada_save(sp, 1, ADA1_BIAS)
                    if prefetch:
                        prefetch(sp)
                    if with_ada:
                        sp.wait_ge(sem("mods1_out"), 16 * 4)

                @block.scalar
                def _(act):
                    for t in range(tiles):
                        act.wait_ge(sem("added" + n), 2 * t + 2)
                        square_sum(act, f"{layer}2", t)

                @block.tensor
                def _(pe):
                    pe.wait_ge(sem("evout_in" if layer == 0 else "odout_in"), 16 * (12 if layer == 0 else 8))
                    for j, (t, h) in enumerate(jobs):
                        if j >= BANKS:
                            pe.wait_ge(sem("gated" + n), j - BANKS + 1)
                        for k in range(KT):
                            last = nc.tensor.matmul(bank(j % BANKS), lhsT(k, t),
                                                    view(ring, (w_slot + k) * SLOT + h * 512, (1, 512)),
                                                    start=(k == 0), stop=(k == KT - 1))
                        last.then_inc(sem("y_ps" + n), 1)
                        if with_ada and j < KT:
                            ada_product(pe, 1, j, ADA1_GROUPS, 5)

                @block.vector
                def _(dve):
                    dve.wait_ge(sem("g_in" + n), 32 if tiles == TT else 16)
                    for j, (t, h) in enumerate(jobs):
                        dve.wait_ge(sem("y_ps" + n), j + 1)
                        if j >= 4:
                            dve.wait_ge(sem("added" + n), j - 3)
                        nc.vector.tensor_tensor(view(arena, YT_AT + (j % 4) * 512, (1, 512)), bank(j % BANKS),
                                                view(arena, GB_AT + (0 if t < XT else D) + h * 512, (1, 512)),
                                                ALU.mult).then_inc(sem("gated" + n), 1)
                        if with_ada and j == KT:
                            ada_sums(dve, 1, ADA1_BIAS, ADA1_GAIN, 5)

                @block.gpsimd
                def _(pool):
                    for j, (t, h) in enumerate(jobs):
                        pool.wait_ge(sem("gated" + n), j + 1)
                        r = view(resid, t * D + h * 512, (1, 512))
                        nc.gpsimd.tensor_tensor(r, r, view(arena, YT_AT + (j % 4) * 512, (1, 512)), ALU.add
                                                ).then_inc(sem("added" + n), 1)

        IOTA = 12800
        META = IOTA + SEQ
        MT = META + 68
        IDX = MT + 768
        CUR = IDX + 384
        GX = CUR + 8
        XS = GX + 1536
        SX = XS + 1536
        HU = 2048
        SU = HU + 768
        HXT = SU + 768
        YX = HXT + 768
        YC = YX + D
        AFFW = HB_AT
        assert SX + 768 <= ARENA and YC + D <= AB_AT

        def top_k(layer):
            n = f"t{layer}"
            streams = [(0, SEQ, CAPX)] + ([(SEQ, CTX, CAPC)] if layer == 0 else [])
            with nc.Block() as block:
                @block.sync
                def _(sp):
                    sp.dma_start(view(arena, IOTA, (1, SEQ)), iota_in.partition_broadcast(P)
                                 ).then_inc(sem("iota_in" + n), 16)
                    for s in range(len(streams)):
                        sp.dma_start(view(arena, G2_AT + s * D, (1, D)), mod_row(layer, s, G2)
                                     ).then_inc(sem("iota_in" + n), 16)
                    sp.wait_ge(sem("iota_in" + n), 16 + 16 * len(streams))

                @block.vector
                def _(dve):
                    step = [0]

                    def stepped(ins):
                        step[0] += 1
                        ins.then_inc(sem("tk" + n), 1)
                        dve.wait_ge(sem("tk" + n), step[0])

                    E = EXPERTS
                    stepped(nc.vector.memset(view(arena, MT, (1, 768), n=E), 0.0))
                    for s, (t0, w, cap) in enumerate(streams):
                        aff = view(arena, AFFW + t0, (1, w), n=E)
                        reps = P // cap
                        for r in range(cap // 8):
                            val = view(arena, IDX + s * 64 + r * 8, (1, 8), n=E)
                            idx = view(arena, IDX + 192 + s * 64 + r * 8, (1, 8), n=E)
                            stepped(nc.vector.max(val, aff))
                            stepped(nc.vector.max_index(idx.bitcast(U32), val, aff))
                            stepped(nc.vector.match_replace(aff, val, aff, -1.0))
                        raw = view(arena, IDX + 192 + s * 64, (1, cap), n=E)
                        num = view(arena, IDX + 320, (1, cap), n=E)
                        stepped(nc.vector.tensor_copy(num, raw.bitcast(U32)))
                        val = view(arena, IDX + s * 64, (1, cap), n=E)
                        for q in range(reps):
                            stepped(nc.vector.tensor_copy(view(arena, MT + s * P + q * cap, (1, cap), n=E), num))
                            stepped(nc.vector.tensor_copy(view(arena, MT + (2 + s) * P + q * cap, (1, cap), n=E), val))
                            stepped(nc.vector.tensor_scalar(view(arena, MT + (4 + s) * P + q * cap, (1, cap), n=E),
                                                            num, float(reps), float(q), ALU.mult, ALU.add))
                    dve.wait_ge(sem("mt_ps" + n), 1)
                    stepped(nc.vector.tensor_copy(view(arena, META, (4, E), (1, 4)),
                                                  bank(0, 0, (1, E), (E, 4))))
                    stepped(nc.vector.tensor_copy(view(arena, META + 4 * E, (1, 4)), view(arena, META + 4 * E - 4, (1, 4))))
                    stepped(nc.vector.tensor_copy(view(offs, 0, (2, E), (1, 2)), bank(0, 4 * E, (1, E), (E, 2))))
                    stepped(nc.vector.tensor_copy(view(offs, 2 * E, (1, 2)), view(offs, 2 * E - 2, (1, 2))))

                @block.tensor
                def _(pe):
                    n_steps = 1 + sum(3 * (cap // 8) + 1 + 3 * (P // cap) for _, _, cap in streams)
                    pe.wait_ge(sem("tk" + n), n_steps)
                    for j in range(6):
                        last = nc.tensor.transpose(bank(0, j * EXPERTS, (1, EXPERTS)),
                                                   view(arena, MT + j * P, (1, P), n=EXPERTS),
                                                   ident[0:EXPERTS, 0:EXPERTS])
                    last.then_inc(sem("mt_ps" + n), 1)

        WCH = SLOTS // 2

        def expert_src(layer, e, ch):
            w = (exp_w_gate, exp_w_up, exp_w_down)[ch // 4]
            r0 = (ch % 4) * 2 * P
            if isinstance(e, int):
                return w[layer, e, r0:r0 + 2 * P, :].rearrange("(k p) n -> p k n", p=P)
            return w[layer, bass.ds(e, 1), r0:r0 + 2 * P, :].rearrange("e (k p) n -> p (e k) n", p=P)

        def ring_chunk(ch):
            return view(ring, ch * 2 * SLOT, (SLOT, 2), (1, SLOT))

        def load_first(layer, chunks):
            def go(sp):
                for ch in chunks:
                    sp.dma_start(ring_chunk(ch), expert_src(layer, 0, ch)).then_inc(sem(f"w{layer}_{ch}"), 16)
            return go

        def load_odd(sp, blocks):
            for cb in blocks:
                for k4 in range(2):
                    sp.dma_start(view(ring, cb * 4 * SLOT + k4 * 2048, (512, 4), (1, 512)),
                                 od_w_in[0, k4 * 512:(k4 + 1) * 512, cb * 512:(cb + 1) * 512]
                                 .rearrange("(k p) n -> p k n", p=P)).then_inc(sem(f"odin{cb}"), 16)

        def mixture(layer, early):
            n = f"m{layer}"
            has_c = layer == 0
            NC = 2 if has_c else 1
            sc_jobs = [(tt, half) for tt in range(TT if has_c else XT) for half in range(2)]
            SJ = len(sc_jobs)

            def tile_done(t):
                return 2 + (EXPERTS // 2) * SJ + 2 * t + 2

            def buf(at, par, s):
                return view(arena, at + par * 768 + (512 if s else 0), (1, 256 if s else 512))

            def cur(par, what):
                return view(arena, CUR + par * 4 + what, (1, 1))

            with nc.Block() as block:
                @block.sync
                def _(sp):
                    for ch in range(WCH):
                        if ch not in early:
                            sp.dma_start(ring_chunk(ch), expert_src(layer, 0, ch)).then_inc(sem(f"w{layer}_{ch}"), 16)
                    with nc.sync.Fori(0, EXPERTS - 1) as i:
                        for ch in range(WCH):
                            if ch in (7, 11):
                                used, freed = sem(("gu_ps" if ch == 7 else "y_ps") + n), i + 1
                            else:
                                used, freed = sem("w_used" + n), i * 10 + (ch + 1 if ch < 7 else ch)
                            freed = nc.sync.snap(freed)
                            src = expert_src(layer, nc.sync.snap(i + 1), ch)
                            sp.wait_ge(used, freed)
                            sp.dma_start(ring_chunk(ch), src).then_inc(sem(f"w{layer}_{ch}"), 16)
                    if layer == 0:
                        load_modulation(sp, 1, 1)
                        at = (EXPERTS - 1) * 10
                        freed = (("w_used", at + 2), ("w_used", at + 4), ("w_used", at + 6), ("gu_ps", EXPERTS),
                                 ("w_used", at + 9), ("y_ps", EXPERTS))
                        for cb, (used, count) in enumerate(freed):
                            sp.wait_ge(sem(used + n), count)
                            load_odd(sp, (cb,))
                    else:
                        for t in range(XT):
                            sp.wait_ge(sem("sc_add" + n), tile_done(t))
                            sp.dma_start(out[0, t * P:(t + 1) * P, :], view(resid, t * D, (1, D))
                                         ).then_inc(sem("out_done"), 16)
                        sp.wait_ge(sem("out_done"), 16 * XT)

                def gather(e):
                    par = e % 2
                    off = view(offs, e * 2, (1, 1))
                    nc.gpsimd.indirect_dma_start(buf(GX, par, 0), None, h2x.rearrange("t (h d) -> (t h) d", h=2),
                                                 bass.IndirectOffsetOnAxis(ap=off, axis=0)
                                                 ).then_inc(sem(f"gx{par}" + n), 16)
                    if has_c:
                        off = view(offs, e * 2 + 1, (1, 1))
                        nc.gpsimd.indirect_dma_start(buf(GX, par, 1), None, h2c.rearrange("t (q d) -> (t q) d", q=4),
                                                     bass.IndirectOffsetOnAxis(ap=off, axis=0)
                                                     ).then_inc(sem(f"gc{par}" + n), 16)

                @block.gpsimd
                def _(pool):
                    for e in range(EXPERTS + 1):
                        if e >= 2:
                            pool.wait_ge(sem("xs_ps" + n), e - 1)
                        if e >= 2 and has_c:
                            pool.wait_ge(sem("xc_ps" + n), e - 1)
                        gather(e)

                @block.tensor
                def _(pe):
                    def turn_x(par):
                        for j in range(4):
                            last = nc.tensor.transpose(bank(7, j * P, (1, P)), view(arena, GX + par * 768 + j * P, (1, P)),
                                                       ident[:, :])
                        last.then_inc(sem("xs_ps" + n), 1)

                    def turn_c(par):
                        for j in range(2):
                            last = nc.tensor.transpose(bank(2, j * P, (1, P)),
                                                       view(arena, GX + par * 768 + 512 + j * P, (1, P)), ident[:, :])
                        last.then_inc(sem("xc_ps" + n), 1)

                    def xs(par, k):
                        return view(arena, XS + par * 768 + (k % 4) * P + (k // 4) * 64, (1, 64))

                    def xsc(par, k):
                        return view(arena, XS + par * 768 + 512 + (k % 2) * P + (k // 2) * 32, (1, 32))

                    def hx(k):
                        return view(arena, HXT + (k % 4) * P + (k // 4) * 64, (1, 64))

                    def hc(k):
                        return view(arena, HXT + 512 + (k % 2) * P + (k // 2) * 32, (1, 32))

                    def dense(ch, k, lx, lc, bx, bc, cc):
                        w0 = (ch * 2 + k % 2) * SLOT
                        for half in range(2):
                            last = nc.tensor.matmul(bank(bx, 0, (1, 512), p=64 * half, n=64), lx,
                                                    view(ring, w0 + half * 512, (1, 512)),
                                                    start=(k == 0), stop=(k == KT - 1))
                        if has_c:
                            for q in range(4):
                                last = nc.tensor.matmul(bank(bc, cc, (1, 256), p=32 * q, n=32), lc,
                                                        view(ring, w0 + q * 256, (1, 256)),
                                                        start=(k == 0), stop=(k == KT - 1))
                        return last

                    def scatter(pair, job):
                        tt, half = sc_jobs[job]
                        if job == 0:
                            pe.wait_ge(sem("s_ready" + n), pair + 1)
                            pe.wait_ge(sem("y_out" + n), pair * 2 + 1)
                        if tt == XT and half == 0:
                            pe.wait_ge(sem("yc_out" + n), pair * 2 + 1)
                        pe.wait_ge(sem("sc_add" + n), pair * SJ + (job + 1))
                        if tt < XT:
                            lhsT = view(arena, SX + tt * P, (1, P))
                            rhs = view(arena, YX + half * 512, (1, 512))
                        else:
                            lhsT = view(arena, SX + 512 + (tt - XT) * P, (1, P), n=64)
                            rhs = view(arena, YC + half * 512, (1, 512), n=64)
                        nc.tensor.matmul(bank(5 + job % 2), lhsT, rhs, start=True, stop=True
                                         ).then_inc(sem("sc_ps" + n), 1)

                    pe.wait_ge(sem("gx0" + n), 16)
                    if has_c:
                        pe.wait_ge(sem("gc0" + n), 16)
                    turn_x(0)
                    if has_c:
                        turn_c(0)
                    with nc.tensor.Fori(0, EXPERTS // 2) as i:
                        for par in range(2):
                            e = i * 2 + par
                            pe.wait_ge(sem("xs_out" + n), e * NC + NC)
                            for m in range(2):
                                for ch in range(4 * m, 4 * m + 4):
                                    pe.wait_ge(sem(f"w{layer}_{ch}"), e * 16 + 16)
                                    for k in (2 * (ch % 4), 2 * (ch % 4) + 1):
                                        last = dense(ch, k, xs(par, k), xsc(par, k), m, (7, 2)[m], 256 * m)
                                    last.then_inc(sem(("w_used" if ch < 7 else "gu_ps") + n), 1)
                                    if par == 0 and 1 <= ch < 7:
                                        for job in (2 * ch - 2, 2 * ch - 1):
                                            if job < SJ:
                                                scatter(i, job)
                            pe.wait_ge(sem(f"gx{1 - par}" + n), i * 16 + (16 if par == 0 else 32))
                            if has_c:
                                pe.wait_ge(sem("silu" + n), e * NC + NC)
                            turn_x(1 - par)
                            pe.wait_ge(sem("h_ready" + n), e * NC + NC)
                            for j in range(4):
                                last = nc.tensor.transpose(bank(0, j * P, (1, P)), view(arena, HU + j * P, (1, P)),
                                                           ident[:, :])
                            if has_c:
                                for j in range(2):
                                    last = nc.tensor.transpose(bank(1, j * P, (1, P)),
                                                               view(arena, HU + 512 + j * P, (1, P)), ident[:, :])
                            last.then_inc(sem("hT_ps" + n), 1)
                            if has_c:
                                pe.wait_ge(sem(f"gc{1 - par}" + n), i * 16 + (16 if par == 0 else 32))
                                turn_c(1 - par)
                            pe.wait_ge(sem("hT_out" + n), e + 1)
                            if has_c:
                                pe.wait_ge(sem("hT_outc" + n), e + 1)
                            for ch in range(8, 12):
                                pe.wait_ge(sem(f"w{layer}_{ch}"), e * 16 + 16)
                                for k in (2 * (ch % 4), 2 * (ch % 4) + 1):
                                    last = dense(ch, k, hx(k), hc(k), 3, 4, 0)
                                last.then_inc(sem(("w_used" if ch < 11 else "y_ps") + n), 1)
                    for job in range(SJ):
                        scatter(EXPERTS // 2, job)

                @block.scalar
                def _(act):
                    def xs_out(par, e1):
                        act.wait_ge(sem("xs_ps" + n), e1)
                        nc.scalar.activation(buf(XS, par, 0), bank(7), ACT.Copy).then_inc(sem("xs_out" + n), 1)
                        if has_c:
                            act.wait_ge(sem("xc_ps" + n), e1)
                            nc.scalar.activation(buf(XS, par, 1), bank(2, 0, (1, 256)), ACT.Copy
                                                 ).then_inc(sem("xs_out" + n), 1)

                    xs_out(0, 1)
                    with nc.scalar.Fori(0, EXPERTS // 2) as i:
                        for par in range(2):
                            e = i * 2 + par
                            act.wait_ge(sem("w_used" + n), e * 10 + 4)
                            nc.scalar.activation(view(arena, SU, (1, 512)), bank(0), ACT.Silu).then_inc(sem("silu" + n), 1)
                            if has_c:
                                nc.scalar.activation(view(arena, SU + 512, (1, 256)), bank(7, 0, (1, 256)), ACT.Silu
                                                     ).then_inc(sem("silu" + n), 1)
                            act.wait_ge(sem("hT_ps" + n), e + 1)
                            nc.scalar.activation(view(arena, HXT, (1, 512)), bank(0), ACT.Copy).then_inc(sem("hT_out" + n), 1)
                            xs_out(1 - par, e + 2)
                    if layer == 0:
                        for t in range(TT):
                            act.wait_ge(sem("sc_add" + n), tile_done(t))
                            square_sum(act, "11", t)

                @block.vector
                def _(dve):
                    def meta(e, par):
                        nc.vector.tensor_copy(view(arena, CUR + par * 4, (1, 4)), arena[:, bass.ds(e * 4 + META, 4)]
                                              ).then_inc(sem("cur" + n), 1)

                    def adds(pair):
                        for job, (tt, half) in enumerate(sc_jobs):
                            dve.wait_ge(sem("sc_ps" + n), pair * SJ + (job + 1))
                            a = view(resid, tt * D + half * 512, (1, 512))
                            nc.vector.tensor_tensor(a, a, bank(5 + job % 2), ALU.add).then_inc(sem("sc_add" + n), 1)

                    nc.vector.memset(view(arena, YX, (1, D)), 0.0).then_inc(sem("y_out" + n), 1)
                    nc.vector.memset(view(arena, YC, (1, D)), 0.0).then_inc(sem("yc_out" + n), 1)
                    for third, signal in enumerate(("sc_add", "sc_add", "s_ready")):
                        nc.vector.memset(view(arena, SX + third * 256, (1, 256)), 0.0).then_inc(sem(signal + n), 1)
                    dve.wait_ge(sem("s_ready" + n), 1)
                    meta(0, 0)
                    with nc.vector.Fori(0, EXPERTS // 2) as i:
                        for par in range(2):
                            e = i * 2 + par
                            if par == 0:
                                adds(i)
                            else:
                                dve.wait_ge(sem("cur" + n), e + 1)
                                for s in range(NC):
                                    rows, w = (32, 256) if s else (64, 512)
                                    for a in range(2):
                                        last = nc.vector.tensor_scalar(
                                            view(arena, SX + s * 512, (1, w), p=rows * a, n=rows),
                                            view(arena, IOTA, (1, w), p=rows * a, n=rows),
                                            view(arena, CUR + a * 4 + s, (1, 1), p=rows * a, n=rows), None, ALU.is_equal)
                                last.then_inc(sem("s_ready" + n), 1)
                                dve.wait_ge(sem("s_ready" + n), i + 2)
                            dve.wait_ge(sem("silu" + n), e * NC + 1)
                            meta(nc.vector.snap(e + 1), 1 - par)
                            dve.wait_ge(sem("gu_ps" + n), e + 1)
                            nc.vector.tensor_tensor(view(arena, HU, (1, 512)), view(arena, SU, (1, 512)), bank(1), ALU.mult
                                                    ).then_inc(sem("h_ready" + n), 1)
                            if has_c:
                                dve.wait_ge(sem("silu" + n), e * NC + 2)
                                nc.vector.tensor_tensor(view(arena, HU + 512, (1, 256)), view(arena, SU + 512, (1, 256)),
                                                        bank(2, 256, (1, 256)), ALU.mult).then_inc(sem("h_ready" + n), 1)
                                dve.wait_ge(sem("hT_ps" + n), e + 1)
                                nc.vector.tensor_copy(view(arena, HXT + 512, (1, 256)), bank(1, 0, (1, 256))
                                                      ).then_inc(sem("hT_outc" + n), 1)
                            dve.wait_ge(sem("y_ps" + n), e + 1)
                            for half in range(2):
                                last = nc.vector.scalar_tensor_tensor(
                                    view(arena, YX + half * 512, (1, 512), p=64 * par, n=64),
                                    bank(3, 0, (1, 512), p=64 * half, n=64),
                                    view(arena, CUR + par * 4 + 2, (1, 1), p=64 * half, n=64),
                                    view(arena, G2_AT + half * 512, (1, 512), p=64 * half, n=64), ALU.mult, ALU.mult)
                            last.then_inc(sem("y_out" + n), 1)
                            if has_c:
                                for q in range(4):
                                    last = nc.vector.scalar_tensor_tensor(
                                        view(arena, YC + q * 256, (1, 256), p=32 * par, n=32),
                                        bank(4, 0, (1, 256), p=32 * q, n=32),
                                        view(arena, CUR + par * 4 + 3, (1, 1), p=32 * q, n=32),
                                        view(arena, G2_AT + D + q * 256, (1, 256), p=32 * q, n=32), ALU.mult, ALU.mult)
                                last.then_inc(sem("yc_out" + n), 1)
                    adds(EXPERTS // 2)

        def odd_in_proj():
            W1 = 832
            qk_jobs = [(cb, t) for cb in range(4) for t in range(XT if cb < 2 else TT)]
            v_jobs = [(cb, t) for cb in (4, 5) for t in range(TT)]
            jobs = qk_jobs + v_jobs
            NQ = len(qk_jobs)

            def hT_cols(cb, t):
                if t >= XT:
                    return 576 + (t - XT) * P
                return t * P if cb < 2 else t * P + 64

            def tm(j):
                return view(arena, TM1_AT + (j % 4) * 512, (HD, 8), (1, HD))

            def tmf(j):
                return view(arena, TM1_AT + (j % 4) * 512, (1, 512))

            RS = SOFT

            with nc.Block() as block:
                @block.sync
                def _(sp):
                    for s, g in enumerate((od_q_gain, od_k_gain)):
                        sp.dma_start(view(small, MISC + s * HD, (1, HD)), g[0].partition_broadcast(P)
                                     ).then_inc(sem("odgain_in"), 16)
                    sp.wait_ge(sem("od_ps"), 2 * XT + TT)
                    sp.dma_start(view(ring, 6 * SLOT, (1, 768)), na_mask_in).then_inc(sem("na_mask_in"), 16)
                    sp.wait_ge(sem("od_ps"), NQ)
                    for k in range(KT):
                        sp.dma_start(view(ring, (8 + k) * SLOT, (1, D)), od_w_out[0, k * P:(k + 1) * P, :]
                                     ).then_inc(sem("odout_in"), 16)

                @block.tensor
                def _(pe):
                    def project(j):
                        cb, t = jobs[j]
                        pe.wait_ge(sem(f"odin{cb}"), 32)
                        if j >= 4:
                            if j - 4 < NQ:
                                pe.wait_ge(sem("tm_in"), j - 3)
                            else:
                                pe.wait_ge(sem("v_out"), j - 4 - NQ + 1)
                        for k in range(KT):
                            last = nc.tensor.matmul(bank(j % 4), view(arena, HT_AT + k * W1 + hT_cols(cb, t), (1, P)),
                                                    view(ring, cb * 4 * SLOT + k * 512, (1, 512)),
                                                    start=(k == 0), stop=(k == KT - 1))
                        last.then_inc(sem("od_ps"), 1)

                    def turn(j):
                        pe.wait_ge(sem("qk_ready"), j + 1)
                        if j >= 2:
                            pe.wait_ge(sem("odT_out"), j - 1)
                        for i in range(4):
                            last = nc.tensor.transpose(bank(4 + j % 2, i * P, (1, P)),
                                                       view(arena, TM1_AT + (j % 4) * 512 + i * P, (1, P)), ident[:, :])
                        last.then_inc(sem("odT_ps"), 1)

                    for j in range(len(jobs)):
                        project(j)
                        if 2 <= j < NQ + 2:
                            turn(j - 2)

                @block.scalar
                def _(act):
                    def turned(j):
                        cb, t = jobs[j]
                        act.wait_ge(sem("odT_ps"), j + 1)
                        if cb < 2:
                            dst = view(arena, QT1_AT + cb * 4 * SEQ + t * P, (SEQ, 4), (1, P))
                        else:
                            dst = view(arena, KT1_AT + (cb - 2) * 4 * TOK + t * P, (TOK, 4), (1, P))
                        nc.scalar.activation(dst, bank(4 + j % 2, 0, (P, 4), (1, P)), ACT.Copy
                                             ).then_inc(sem("odT_out"), 1)

                    for j in range(len(jobs)):
                        act.wait_ge(sem("od_ps"), j + 1)
                        cb, t = jobs[j]
                        if j < NQ:
                            if j >= 4:
                                act.wait_ge(sem("odT_ps"), j - 3)
                            nc.scalar.activation(tmf(j), bank(j % 4), ACT.Copy).then_inc(sem("tm_in"), 1)
                            if j >= 2:
                                act.wait_ge(sem("odsum"), j - 1)
                            act.wait_ge(sem("tm_in"), j + 1)
                            nc.scalar.activation(view(arena, PT1_AT - 512 + (j % 2) * 512, (1, 512)), tmf(j),
                                                 ACT.Square).then_inc(sem("odsq"), 1)
                            if j >= 1:
                                act.wait_ge(sem("odvar"), j)
                                s = view(small, RS + ((j - 1) % 4) * 8, (1, 8))
                                nc.scalar.activation(s, s, ACT.Sqrt).then_inc(sem("odstd"), 1)
                        else:
                            if j == NQ:
                                act.wait_ge(sem("odvar"), NQ)
                                s = view(small, RS + ((NQ - 1) % 4) * 8, (1, 8))
                                nc.scalar.activation(s, s, ACT.Sqrt).then_inc(sem("odstd"), 1)
                            nc.scalar.activation(view(ring, t * SLOT + (cb - 4) * 512, (1, 512)), bank(j % 4), ACT.Copy
                                                 ).then_inc(sem("v_out"), 1)
                        if 2 <= j < NQ + 2:
                            turned(j - 2)

                @block.vector
                def _(dve):
                    dve.wait_ge(sem("odgain_in"), 32)
                    gq = view(small, MISC, (1, HD))
                    nc.vector.tensor_scalar(gq, gq, HD ** -0.5, None, ALU.mult).then_inc(sem("odgain"), 1)
                    dve.wait_ge(sem("odgain"), 1)

                    def finish(j):
                        s = view(small, RS + (j % 4) * 8, (1, 8))
                        dve.wait_ge(sem("odstd"), j + 1)
                        nc.vector.reciprocal(s, s).then_inc(sem("odrstd"), 1)
                        dve.wait_ge(sem("odrstd"), j + 1)
                        nc.vector.tensor_tensor(tm(j), tm(j), view(small, RS + (j % 4) * 8, (1, 8), (0, HD)), ALU.mult
                                                ).then_inc(sem("odmul"), 1)
                        dve.wait_ge(sem("odmul"), j + 1)
                        g = view(small, MISC + (0 if jobs[j][0] < 2 else HD), (0, 8), (1, HD))
                        nc.vector.tensor_tensor(tm(j), tm(j), g, ALU.mult).then_inc(sem("qk_ready"), 1)

                    for j in range(NQ):
                        s = view(small, RS + (j % 4) * 8, (1, 8))
                        dve.wait_ge(sem("odsq"), j + 1)
                        nc.vector.tensor_reduce(s, view(arena, PT1_AT - 512 + (j % 2) * 512, (HD, 8), (1, HD)), AX.X,
                                                ALU.add).then_inc(sem("odsum"), 1)
                        dve.wait_ge(sem("odsum"), j + 1)
                        nc.vector.tensor_scalar(s, s, 1.0 / HD, EPS, ALU.mult, ALU.add).then_inc(sem("odvar"), 1)
                        if j >= 1:
                            finish(j - 1)
                    finish(NQ - 1)

        stages = [
            lambda: ada_stage(),
            lambda: norm_stage(0, 1, TT, load_even),
            lambda: even_in_proj(),
            lambda: even_qk_fourier(),
            lambda: attention(0),
            lambda: out_proj(0, load_first(0, range(0, 6))),
            lambda: norm_stage(0, 2, TT, load_first(0, range(6, 12))),
            lambda: top_k(0),
            lambda: mixture(0, range(0, 12)),
            lambda: norm_stage(1, 1, TT),
            lambda: odd_in_proj(),
            lambda: attention(1),
            lambda: out_proj(1, load_first(1, range(8, 12))),
            lambda: norm_stage(1, 2, XT, load_first(1, range(0, 8))),
            lambda: top_k(1),
            lambda: mixture(1, range(0, 12)),
        ]
        for number, stage in enumerate(stages[:upto]):
            if number == 9:
                kept = {"ab_in11", "sq_done11"} | {f"odin{cb}" for cb in range(6)}
                nc.clear_and_free_semaphores([sems.pop(name) for name in list(sems) if name not in kept])
                nc.all_engine_barrier()
            stage()
        if taps:
            named = {"resid": resid, "arena": arena, "ring": ring, "small": small, "mods": mods, "h2x": h2x, "offs": offs}
            with nc.Block() as block:
                @block.sync
                def _(sp):
                    for i, (name, dst, col, w, parts) in enumerate(taps):
                        t = named[name]
                        src = t if name in ("mods", "h2x") else view(t, col, (1, w), n=parts)
                        sp.dma_start(dst, src).then_inc(sem("tapped"), 16)
                    sp.wait_ge(sem("tapped"), 16 * len(taps))


def shape_constants():
    n = np.arange(SEQ)
    ang = 2.0 * np.pi * ((n[:, None] * n[None, :]) % SEQ) / SEQ
    dft = np.stack([np.cos(ang), np.sin(ang)]).astype(np.float32)
    inv = np.power(np.float32(10000.0), -np.arange(16, dtype=np.float32) / np.float32(16)).astype(np.float32)
    row, col = (n // GRID_W).astype(np.float32), (n % GRID_W).astype(np.float32)
    a = np.concatenate([row[:, None] * inv, col[:, None] * inv], axis=-1)
    co, si = np.cos(a).astype(np.float32), np.sin(a).astype(np.float32)
    rope = np.concatenate([co, co, -si, si], axis=1).astype(np.float32)
    i, j = np.arange(P)[:, None], np.arange(P)[None, :]
    swa = np.concatenate([np.where(j >= i, 0.0, -1e30), np.where(j <= i, 0.0, -1e30)], axis=1).astype(np.float32)
    na = np.zeros((P, 3, 256), np.float32)
    p, key = np.arange(P), np.arange(256)
    for v, t in enumerate((0, 1, 3)):
        cq = 16 * t + 8 * (p // 64) + p % 8
        ck = 16 * t - 8 + 8 * (key // 64) + key % 8
        start = np.clip(cq - NA_COLS // 2, 0, GRID_W - NA_COLS)
        ok = (ck[None, :] >= start[:, None]) & (ck[None, :] < start[:, None] + NA_COLS)
        na[:, v] = np.where(ok, 0.0, -1e30)
    return {"dft": dft, "rope": rope, "ident": np.eye(P, dtype=np.float32),
            "swa_mask": swa, "na_mask": na.reshape(P, 768), "iota": np.arange(SEQ, dtype=np.float32)}


def layout(inputs):
    a = {k: np.ascontiguousarray(np.asarray(v)) for k, v in inputs.items()}
    a["c"] = a["c"].reshape(D)
    rpb = a.pop("od_rpb")[0]
    wide = np.zeros((NH, RPB_R, RPB_PAD), rpb.dtype)
    wide[:, :, 8:8 + RPB_C] = rpb
    flat = np.concatenate([wide.reshape(NH, -1), np.zeros((NH, RPB_PAD), rpb.dtype)], axis=1)
    p = np.arange(P)
    start = (7 - (p // 8) % 8) * RPB_PAD + 15 - (8 * (p // 64) + p % 8)
    a["rpb_pad"] = np.stack([flat[:, s:s + 8 * RPB_PAD] for s in start], axis=1)
    a.update(shape_constants())
    return a


_INS = ["x", "c", "ctx", "c_ctx", "ada_w", "ada_b", "norm1_g", "norm2_g", "router_w", "exp_w_gate", "exp_w_up",
        "exp_w_down", "ev_w_in", "ev_w_out", "ev_q_gain", "ev_k_gain", "ev_sink", "od_w_in", "od_w_out",
        "od_q_gain", "od_k_gain", "rpb_pad", "dft", "rope", "ident", "swa_mask", "na_mask", "iota"]


def kernel(**inputs):
    import concourse.bacc as bacc
    from concourse.bass_utils import run_bass_kernel_spmd

    a = layout(inputs)
    nc = bacc.Bacc("TRN2", target_bir_lowering=False, num_devices=1)
    arrays, args = {}, []
    for name in _INS:
        arrays[f"in_{name}"] = np.ascontiguousarray(a[name])
        args.append(nc.dram_tensor(f"in_{name}", a[name].shape, mybir.dt.from_np(a[name].dtype),
                                   kind="ExternalInput").ap())
    args.append(nc.dram_tensor("out_x", (1, SEQ, D), F32, kind="ExternalOutput").ap())
    program(nc, *args)
    r = run_bass_kernel_spmd(nc, [arrays], core_ids=[0])
    return r.results[0]["out_x"]
```

```python
from contextlib import ExitStack

import numpy as np

import concourse.bass as bass
from concourse import mybir

F32 = mybir.dt.float32
BF16 = mybir.dt.bfloat16
U32 = mybir.dt.uint32
ACT = mybir.ActivationFunctionType
ALU = mybir.AluOpType
AX = mybir.AxisListType

P = 128
D = 1024
KT = D // P
SEQ, CTX = 512, 256
XT, CT = SEQ // P, CTX // P
TT = XT + CT
TOK = SEQ + CTX
LAYERS = 2
HD = 64
GRID_W = 64
FW = D // 2
FG = FW // P
QH, KVH = 8, 2
QK0 = (QH + KVH) * HD
EV_IN = FW + QK0 + KVH * HD
NH = D // HD
NA_COLS = 16
RPB_R, RPB_C = 2 * 8 - 1, 2 * NA_COLS - 1
RPB_PAD = 48
EXPERTS = 16
CAPX, CAPC = 2 * SEQ // EXPERTS, 2 * CTX // EXPERTS
SLOT = 1024
SLOTS = 24
EPS = 1e-6
SH1, SC1, G1, SH2, SC2, G2 = range(6)

ARENA = 21504
HT_AT = 0
AB_AT = 6656
HB_AT = 10752
FT_AT, QKV_AT = 12800, 15872
QN_AT, TMP_AT, QT_AT, KT0_AT = 0, 3840, 6656, 9728
GAIN_AT = 10496
FOUR_AT = FT_AT
AT0_AT, P0_AT, PT0_AT = 0, 3072, 10496
QT1_AT, TM1_AT, KT1_AT = 6656, 10752, 12800
AT1_AT, BM1_AT, BR1_AT, P1_AT, BM1B_AT, PT1_AT = 0, 4096, 5632, 10752, 18944, 20480
GB_AT, YT_AT = 16384, 18432
AFF_AT = 20480
G2_AT = 0


def program(nc, x, c, ctx, c_ctx, ada_w, ada_b, norm1_g, norm2_g, router_w, exp_w_gate, exp_w_up,
            exp_w_down, ev_w_in, ev_w_out, ev_q_gain, ev_k_gain, ev_sink, od_w_in, od_w_out,
            od_q_gain, od_k_gain, rpb_pad, dft, rope, ident_in, swa_mask_in, na_mask_in,
            iota_in, out):
    stack = ExitStack()
    with stack:
        def sb(name, shape, dt=F32):
            return stack.enter_context(nc.sbuf_tensor(name, shape, dt))

        sems = {}

        def sem(name):
            if name not in sems:
                sems[name] = nc.alloc_semaphore(name=name)
            return sems[name]

        def view(t, col, *dims, p=0, n=P):
            row = t.shape[1] if len(t.shape) == 2 else int(np.prod(t.shape[1:]))
            return bass.AP(t, p * row + col, [[row, n], *[list(d) for d in dims]])

        resid = sb("resid", [P, TT * D])
        ring = sb("ring", [P, SLOTS * SLOT])
        arena = sb("arena", [P, ARENA])
        ident = sb("ident", [P, P])
        ident16 = sb("ident16", [P, P], BF16)
        swa_mask = sb("swa_mask", [P, 2 * P], BF16)
        router = sb("router", [P, KT * EXPERTS])
        small = sb("small", [P, 432])
        offs = sb("offs", [P, 2 * (EXPERTS + 1)], U32)
        ps = stack.enter_context(nc.psum_tensor("ps", [P, 8 * 512], F32))

        def bank(b, col=0, *dims, p=0, n=P):
            return view(ps, b * 512 + col, *(dims or ((1, 512),)), p=p, n=n)

        mods = nc.dram_tensor("mods", [LAYERS * 2, 6 * D], F32, kind="Internal").ap()
        h2x = nc.dram_tensor("h2x", [SEQ, D], F32, kind="Internal").ap()
        h2c = nc.dram_tensor("h2c", [CTX, D], F32, kind="Internal").ap()

        def mod_row(layer, stream, vec):
            return mods[2 * layer + stream, vec * D:(vec + 1) * D].partition_broadcast(P)

        def ring_load(eng, slot, cols, src, done):
            k = src.shape[0] // P
            eng.dma_start(view(ring, slot * SLOT, (cols, k), (1, cols)),
                          src.rearrange("(k p) n -> p k n", p=P)).then_inc(done, 16)

        SS, QSS, SINK, SOFT = 0, 8, 72, 96
        MISC = 300

        ADA_PARTS = {"a": (0, 0, 1, 8, 8, 0, 64),
                     "b": (0, 1, 2, 14, 2, 6, AB_AT),
                     "c": (1, 0, 3, 0, 2, 5, P0_AT)}
        SILU = 0

        def ada_load(sp, part, k):
            layer, b0, nb, slot, groups, _, _ = ADA_PARTS[part]
            if k >= groups:
                sp.wait_ge(sem(f"ada_{part}_used"), k - groups + 1)
            sp.dma_start(view(ring, (slot + (k % groups) * 2 * nb) * SLOT, (1, nb * 2048)),
                         ada_w[layer].rearrange("(p k) n -> k p n", k=KT)[k][:, b0 * 2048:(b0 + nb) * 2048]
                         ).then_inc(sem(f"ada_{part}_in{k % groups}"), 16)

        def ada_bias_load(sp, part):
            layer, b0, nb, _, _, _, at = ADA_PARTS[part]
            for g in range(4):
                sp.dma_start(view(arena, at, (512, nb), (1, 512), p=32 * g, n=2),
                             ada_b[layer].rearrange("(b g n) -> g b n", g=4, n=512)[g][b0:b0 + nb]
                             .partition_broadcast(2)).then_inc(sem(f"bias_{part}_in"), 16)
                src, half = (norm2_g, g) if g < 2 else (norm1_g, g - 2)
                sp.dma_start(view(arena, at + nb * 512, (1, 512), p=32 * g, n=2),
                             src[layer, half * 512:(half + 1) * 512].partition_broadcast(2)
                             ).then_inc(sem(f"bias_{part}_in"), 16)

        def ada_product(pe, part, k):
            _, _, nb, slot, groups, bank0, _ = ADA_PARTS[part]
            pe.wait_ge(sem(f"ada_{part}_in{k % groups}"), 16 * (k // groups + 1))
            for b in range(nb):
                for g in range(4):
                    last = nc.tensor.matmul(bank(bank0 + b, 0, (1, 512), p=32 * g, n=2),
                                            view(router, SILU + k, (KT, 2)),
                                            view(ring, (slot + (k % groups) * 2 * nb) * SLOT + (b * 4 + g) * 512,
                                                 (1, 512)), start=(k == 0), stop=(k == KT - 1))
            last.then_inc(sem(f"ada_{part}_used"), 1)

        def scale_block(part, g):
            _, b0, nb, _, _, _, _ = ADA_PARTS[part]
            b = (2 if g < 2 else 0) - b0
            return b if 0 <= b < nb else None

        def mod_steps(part, g):
            return sum(1 if scale_block(part, i) is None else 2 for i in range(g + 1))

        def ada_sums(dve, part):
            _, _, nb, _, _, bank0, at = ADA_PARTS[part]
            dve.wait_ge(sem(f"bias_{part}_in"), 16 * 8)
            dve.wait_ge(sem(f"ada_{part}_used"), KT)
            for g in range(4):
                mod = view(arena, at, (1, nb * 512), p=32 * g, n=2)
                nc.vector.tensor_tensor(mod, bank(bank0, 0, (1, nb * 512), p=32 * g, n=2), mod, ALU.add
                                        ).then_inc(sem(f"mod_sum_{part}"), 1)
                if scale_block(part, g) is not None:
                    dve.wait_ge(sem(f"mod_sum_{part}"), mod_steps(part, g) - 1)
                    scale = view(arena, at + scale_block(part, g) * 512, (1, 512), p=32 * g, n=2)
                    nc.vector.scalar_tensor_tensor(scale, scale, 1.0, view(arena, at + nb * 512, (1, 512), p=32 * g, n=2),
                                                   ALU.add, ALU.mult).then_inc(sem(f"mod_sum_{part}"), 1)

        def ada_save(sp, part):
            layer, b0, nb, _, _, _, at = ADA_PARTS[part]
            for g in range(4):
                sp.wait_ge(sem(f"mod_sum_{part}"), mod_steps(part, g))
                rows = mods[2 * layer:2 * layer + 2, :].rearrange("s (b g n) -> g s b n", g=4, n=512)[g]
                sp.dma_start(rows[:, b0:b0 + nb],
                             view(arena, at, (512, nb), (1, 512), p=32 * g, n=2)).then_inc(sem(f"mods_{part}_out"), 16)

        def load_even_in(sp, ks):
            for k in ks:
                sp.dma_start(view(ring, k * EV_IN, (1, EV_IN)), ev_w_in[0, k * P:(k + 1) * P, :]
                             ).then_inc(sem("evin_in"), 16)

        EARLY_K = 3
        assert EARLY_K * EV_IN <= ADA_PARTS["a"][3] * SLOT

        def ada_stage():
            CIN, MASK = 0, 4096
            with nc.Block() as block:
                @block.sync
                def _(sp):
                    for s, src in enumerate((c, c_ctx)):
                        sp.dma_start(view(arena, CIN + s * KT, (1, KT)),
                                     src.rearrange("(p k) -> p k", k=KT)).then_inc(sem("c_in"), 16)
                    for k in range(KT):
                        ada_load(sp, "a", k)
                    ada_bias_load(sp, "a")
                    sp.dma_start(view(resid, 0, (D, XT), (1, D)),
                                 x[0].rearrange("(t p) d -> p t d", p=P)).then_inc(sem("x_in"), 16)
                    sp.dma_start(view(resid, XT * D, (D, CT), (1, D)),
                                 ctx[0].rearrange("(t p) d -> p t d", p=P)).then_inc(sem("ctx_in"), 16)
                    sp.dma_start(ident[:, :], ident_in).then_inc(sem("const_in"), 16)
                    sp.dma_start(view(arena, MASK, (1, 2 * P)), swa_mask_in).then_inc(sem("const_in"), 16)
                    sp.dma_start(view(small, SINK, (1, QH)), ev_sink[0].partition_broadcast(P)
                                 ).then_inc(sem("const_in"), 16)
                    ada_save(sp, "a")
                    load_even_in(sp, range(EARLY_K))
                    sp.wait_ge(sem("mods_a_out"), 16 * 4)

                @block.scalar
                def _(act):
                    act.wait_ge(sem("c_in"), 32)
                    nc.scalar.activation(view(router, SILU, (1, 2 * KT)), view(arena, CIN, (1, 2 * KT)),
                                         ACT.Silu).then_inc(sem("silu_c"), 1)
                    square_sums(act, "01", TT, lambda t: act.wait_ge(sem("x_in" if t < XT else "ctx_in"), 16))

                @block.tensor
                def _(pe):
                    pe.wait_ge(sem("silu_c"), 1)
                    for k in range(KT):
                        ada_product(pe, "a", k)

                @block.vector
                def _(dve):
                    ada_sums(dve, "a")
                    dve.wait_ge(sem("const_in"), 48)
                    nc.vector.tensor_copy(ident16[:, :], ident[:, :])
                    nc.vector.tensor_copy(swa_mask[:, :], view(arena, MASK, (1, 2 * P)))
                    mean_square(dve, "01", 1, TT)
                    inverse_rms(dve, "01", 1, TT)

        def load_dft(sp):
            for s in range(2):
                sp.dma_start(view(ring, 10 * SLOT + s * 2048, (512, 4), (1, 512)),
                             dft[s].rearrange("(t p) m -> p t m", p=P)).then_inc(sem("dft_in"), 16)

        def load_even_out(sp):
            for k in range(4):
                sp.dma_start(view(ring, (14 + k) * SLOT, (1, D)), ev_w_out[0, k * P:(k + 1) * P, :]
                             ).then_inc(sem("evout_in"), 16)
            for pr in range(4):
                for a in range(2):
                    r0 = FW + (pr + 4 * a) * HD
                    sp.dma_start(view(ring, (18 + pr) * SLOT, (1, D), p=64 * a, n=64),
                                 ev_w_out[0, r0:r0 + HD, :]).then_inc(sem("evout_in"), 16)

        def ab_at(stream, vec):
            return view(arena, AB_AT + (2 * stream + vec) * D, (1, D))

        def load_modulation(sp, layer, which):
            for s in range(1 if (layer, which) == (1, 2) else 2):
                for v, vec in enumerate((SC1, SH1) if which == 1 else (SC2, SH2)):
                    sp.dma_start(ab_at(s, v), mod_row(layer, s, vec)).then_inc(sem(f"ab{s}_in{layer}{which}"), 16)

        def square_sum(act, n, t):
            if t >= 2:
                act.wait_ge(sem("sq_done" + n), t - 1)
            nc.scalar.activation(view(arena, HB_AT + (t % 2) * D, (1, D)), view(resid, t * D, (1, D)), ACT.Square,
                                 accum_out=view(small, SS + t, (1, 1))).then_inc(sem("sq_done" + n), 1)

        def rms_view(step, tiles):
            return view(small, SS, (1, tiles - 1)) if step == 1 else view(small, SS + tiles - 1, (1, 1))

        def mean_square(dve, n, step, tiles):
            dve.wait_ge(sem("sq_done" + n), tiles - 2 + step)
            nc.vector.tensor_scalar(rms_view(step, tiles), rms_view(step, tiles), 1.0 / D, EPS, ALU.mult, ALU.add
                                    ).then_inc(sem("var_ready" + n), 1)

        def root(act, n, step, tiles):
            act.wait_ge(sem("var_ready" + n), step)
            nc.scalar.activation(rms_view(step, tiles), rms_view(step, tiles), ACT.Sqrt
                                 ).then_inc(sem("std_ready" + n), 1)

        def inverse_rms(dve, n, step, tiles):
            dve.wait_ge(sem("std_ready" + n), step)
            nc.vector.reciprocal(rms_view(step, tiles), rms_view(step, tiles)).then_inc(sem("rstd_ready" + n), 1)

        def square_sums(act, n, tiles, wait_tile):
            for t in range(tiles):
                if t == tiles - 1:
                    root(act, n, 1, tiles)
                wait_tile(t)
                square_sum(act, n, t)

        def norm_stage(layer, which, tiles, prefetch=None):
            n = f"{layer}{which}"
            width = 832 if (layer, which) == (1, 1) else TOK
            blocked = width == 832
            HBUF = 4 if which == 2 else 2

            def saves(buffer):
                return len(range(buffer, tiles, HBUF))

            def hb(t):
                return view(arena, HB_AT + (t % HBUF) * D, (1, D))

            def res(t):
                return view(resid, t * D, (1, D))

            LG = SOFT
            LGT = HB_AT + 4 * D
            with nc.Block() as block:
                @block.sync
                def _(sp):
                    if n == "01":
                        load_modulation(sp, layer, which)
                    if which == 2:
                        for t in range(tiles):
                            sp.wait_ge(sem("h_ready" + n), t + 1)
                            dst = h2x[t * P:(t + 1) * P, :] if t < XT else h2c[(t - XT) * P:(t - XT + 1) * P, :]
                            sp.dma_start(dst, hb(t)).then_inc(sem(f"h_saved{n}{t % HBUF}"), 16)
                    if prefetch:
                        prefetch(sp)
                    if which == 2:
                        for buffer in range(HBUF):
                            sp.wait_ge(sem(f"h_saved{n}{buffer}"), 16 * saves(buffer))

                @block.scalar
                def _(act):
                    root(act, n, 2, tiles)
                    for t in range(tiles):
                        act.wait_ge(sem("hT_ps" + n), t + 1)
                        b0 = 2 * (t % 2)
                        if blocked and t < XT:
                            for r in range(2):
                                for half in range(2):
                                    last = nc.scalar.activation(
                                        view(arena, HT_AT + 4 * half * width + (2 * t + r) * 8,
                                             (width, 4), (64, 8), (1, 8)),
                                        bank(b0 + half, r * 64, (P, 4), (8, 8), (1, 8)), ACT.Copy)
                        else:
                            at = t * P + (64 if blocked else 0)
                            last = nc.scalar.activation(view(arena, HT_AT + at, (width, KT), (1, P)),
                                                        bank(b0, 0, (P, KT), (1, P)), ACT.Copy)
                        last.then_inc(sem("hT_out" + n), 1)
                    if which == 2:
                        act.wait_ge(sem("lg_shift" + n), 1)
                        nc.scalar.activation(view(small, LG, (1, tiles * EXPERTS)), view(small, LG, (1, tiles * EXPERTS)),
                                             ACT.Exp).then_inc(sem("lg_exp" + n), 1)

                @block.vector
                def _(dve):
                    mean_square(dve, n, 2, tiles)
                    if n == "02":
                        nc.vector.memset(view(arena, AFF_AT, (1, SEQ), n=32 + EXPERTS), -1.0
                                         ).then_inc(sem("aff_pad"), 1)
                    for t in range(tiles):
                        stream = 0 if t < XT else 1
                        if t == tiles - 1:
                            inverse_rms(dve, n, 2, tiles)
                        if t in (0, tiles - 1):
                            dve.wait_ge(sem("rstd_ready" + n), 1 if t == 0 else 2)
                        if t in (0, XT):
                            dve.wait_ge(sem(f"ab{stream}_in" + n), 32)
                        if t >= HBUF:
                            dve.wait_ge(sem("hT_ps" + n), t - HBUF + 1)
                            if which == 2:
                                dve.wait_ge(sem(f"h_saved{n}{t % HBUF}"), 16 * (t // HBUF))
                        nc.vector.scalar_tensor_tensor(hb(t), res(t), view(small, SS + t, (1, 1)), ab_at(stream, 0),
                                                       ALU.mult, ALU.mult).then_inc(sem("h_scaled" + n), 1)
                        dve.wait_ge(sem("h_scaled" + n), t + 1)
                        nc.vector.tensor_tensor(hb(t), hb(t), ab_at(stream, 1), ALU.add).then_inc(sem("h_ready" + n), 1)
                    if blocked:
                        dve.wait_ge(sem("hT_out" + n), XT)
                        nc.vector.tensor_copy(view(arena, HT_AT + SEQ, (width, KT), (1, 64)),
                                              view(arena, HT_AT, (width, KT), (1, 64))).then_inc(sem("wrap" + n), 1)
                    if which == 2:
                        lg = view(small, LG, (EXPERTS, tiles), (1, EXPERTS))
                        mx = view(small, MISC, (1, tiles))
                        dve.wait_ge(sem("lgT_ps" + n), 1)
                        nc.vector.tensor_copy(view(arena, LGT, (1, tiles * P), n=EXPERTS),
                                              bank(4, 0, (1, tiles * P), n=EXPERTS)).then_inc(sem("lgT_out" + n), 1)
                        dve.wait_ge(sem("lg_ps" + n), 1)
                        nc.vector.tensor_reduce(mx, bank(7, 0, (EXPERTS, tiles), (1, EXPERTS)), AX.X, ALU.max
                                                ).then_inc(sem("lg_step" + n), 1)
                        dve.wait_ge(sem("lg_step" + n), 1)
                        nc.vector.tensor_tensor(lg, bank(7, 0, (EXPERTS, tiles), (1, EXPERTS)),
                                                view(small, MISC, (1, tiles), (0, EXPERTS)), ALU.subtract
                                                ).then_inc(sem("lg_shift" + n), 1)
                        dve.wait_ge(sem("lg_exp" + n), 1)
                        nc.vector.tensor_reduce(view(small, MISC + 8, (1, tiles)), lg, AX.X, ALU.add
                                                ).then_inc(sem("lg_step" + n), 1)
                        dve.wait_ge(sem("lg_step" + n), 2)
                        nc.vector.reciprocal(view(small, MISC + 16, (1, tiles)), view(small, MISC + 8, (1, tiles))
                                             ).then_inc(sem("lg_step" + n), 1)
                        dve.wait_ge(sem("lg_step" + n), 3)
                        nc.vector.tensor_tensor(lg, lg, view(small, MISC + 16, (1, tiles), (0, EXPERTS)), ALU.mult
                                                ).then_inc(sem("aff_ready" + n), 1)
                        dve.wait_ge(sem("affT_ps" + n), 1)
                        if layer == 0:
                            dve.wait_ge(sem("aff_pad"), 1)
                            nc.vector.tensor_copy(view(arena, AFF_AT, (1, CTX), p=32, n=EXPERTS),
                                                  bank(6, 0, (1, CTX), n=EXPERTS))
                        nc.vector.tensor_copy(view(arena, AFF_AT, (1, SEQ), n=EXPERTS),
                                              bank(5, 0, (1, SEQ), n=EXPERTS)).then_inc(sem("affT" + n), 1)

                @block.tensor
                def _(pe):
                    def logits(t):
                        pe.wait_ge(sem("hT_out" + n), t + 1)
                        for k in range(KT):
                            last = nc.tensor.matmul(bank(4, t * P, (1, P), n=EXPERTS),
                                                    view(router, k * EXPERTS, (1, EXPERTS)),
                                                    view(arena, HT_AT + k * width + t * P, (1, P)),
                                                    start=(k == 0), stop=(k == KT - 1))
                        return last

                    if (layer, which) == (0, 1):
                        pe.wait_ge(sem("const_in"), 48)
                    for t in range(tiles):
                        if t == 0 and which == 2:
                            pe.wait_ge(sem("rt_in" + n), 16)
                        pe.wait_ge(sem("h_ready" + n), t + 1)
                        if t >= 2:
                            pe.wait_ge(sem("hT_out" + n), t - 1)
                        for k in range(KT):
                            last = nc.tensor.transpose(bank(2 * (t % 2), k * P, (1, P)),
                                                       view(arena, HB_AT + (t % HBUF) * D + k * P, (1, P)), ident[:, :])
                        last.then_inc(sem("hT_ps" + n), 1)
                        if which == 2 and t >= 1:
                            logits(t - 1)
                    if which == 2:
                        logits(tiles - 1).then_inc(sem("lgT_ps" + n), 1)
                        pe.wait_ge(sem("lgT_out" + n), 1)
                        for t in range(tiles):
                            last = nc.tensor.transpose(bank(7, t * EXPERTS, (1, EXPERTS)),
                                                       view(arena, LGT + t * P, (1, P), n=EXPERTS),
                                                       ident[0:EXPERTS, 0:EXPERTS])
                        last.then_inc(sem("lg_ps" + n), 1)
                        pe.wait_ge(sem("aff_ready" + n), 1)
                        for t in range(tiles):
                            last = nc.tensor.transpose(bank(5, t * P, (1, P), n=EXPERTS),
                                                       view(small, LG + t * EXPERTS, (1, EXPERTS)), ident[:, :])
                        last.then_inc(sem("affT_ps" + n), 1)

        def job_stage(n, jobs, waits, prefetch=None, ada_from=None):
            BANKS = 8 if ada_from is None else 6

            def drained(eng, j):
                eng.wait_ge(sem(("act_out" if j % 2 == 0 else "dve_out") + n), j // 2 + 1)

            with nc.Block() as block:
                if prefetch:
                    @block.sync
                    def _(sp):
                        prefetch(sp)

                @block.tensor
                def _(pe):
                    for s, v in waits:
                        pe.wait_ge(sem(s), v)
                    for j, (mms, _) in enumerate(jobs):
                        if j >= BANKS:
                            drained(pe, j - BANKS)
                        for (at, lhsT, rhs, start, stop) in mms:
                            col, dims, p0, np_ = at
                            last = nc.tensor.matmul(bank(j % BANKS, col, *dims, p=p0, n=np_), lhsT, rhs,
                                                    start=start, stop=stop)
                        last.then_inc(sem("job_done" + n), 1)
                        if ada_from is not None and 0 <= j - ada_from < 2 * KT and (j - ada_from) % 2 == 0:
                            ada_product(pe, "b", (j - ada_from) // 2)

                @block.scalar
                def _(act):
                    for j in range(0, len(jobs), 2):
                        act.wait_ge(sem("job_done" + n), j + 1)
                        for dst, col, dims in jobs[j][1]:
                            last = nc.scalar.activation(dst, bank(j % BANKS, col, *dims), ACT.Copy)
                        last.then_inc(sem("act_out" + n), 1)

                @block.vector
                def _(dve):
                    for j in range(1, len(jobs), 2):
                        dve.wait_ge(sem("job_done" + n), j + 1)
                        for dst, col, dims in jobs[j][1]:
                            last = nc.vector.tensor_copy(dst, bank(j % BANKS, col, *dims))
                        last.then_inc(sem("dve_out" + n), 1)
                        if ada_from is not None and j == ada_from + 2 * KT - 2:
                            ada_sums(dve, "b")

        def even_in_proj():
            def hT(k, t0, w):
                return view(arena, HT_AT + k * TOK + t0, (1, w))

            def w_in(k, c0, w):
                return view(ring, k * EV_IN + c0, (1, w))

            jobs = []
            for g in range(FG):
                for t0, w in ((0, SEQ), (SEQ, CTX)):
                    mms = [((0, ((1, w),), 0, P), w_in(k, g * P, P), hT(k, t0, w), k == 0, k == KT - 1)
                           for k in range(KT)]
                    jobs.append((mms, [(view(arena, FT_AT + g * TOK + t0, (1, w)), 0, ((1, w),))]))
            for t in range(TT):
                for c0, w in ((0, 512), (512, 256)):
                    mms = [((0, ((1, w),), 0, P), hT(k, t * P, P), w_in(k, FW + c0, w), k == 0, k == KT - 1)
                           for k in range(KT)]
                    if c0 == 0:
                        drain = (view(arena, QKV_AT + t * 768, (HD, 2), (2 * HD, 4), (1, HD)),
                                 0, ((4 * HD, 2), (HD, 4), (1, HD)))
                    else:
                        drain = (view(arena, QKV_AT + t * 768 + c0, (1, w)), 0, ((1, w),))
                    jobs.append((mms, [drain]))
            def loads(sp):
                even_gains(sp)
                for k in range(KT):
                    ada_load(sp, "b", k)
                    if k == 1:
                        load_dft(sp)
                        ada_bias_load(sp, "b")
                ada_save(sp, "b")
                sp.wait_ge(sem("mods_b_out"), 16 * 4)

            job_stage("ei", jobs, [("evin_in", 16 * KT)], loads, ada_from=3)

        def even_gains(sp):
            for h in range(QH + KVH):
                g = ev_q_gain if h < QH else ev_k_gain
                sp.dma_start(view(arena, GAIN_AT + h * HD, (1, HD)), g[0].partition_broadcast(P)
                             ).then_inc(sem("gain_in"), 16)
            sp.dma_start(view(ring, 22 * SLOT, (P, XT), (1, P)), rope.rearrange("(t p) n -> p t n", p=P)
                         ).then_inc(sem("gain_in"), 16)

        def even_qk_fourier():
            H = QH + KVH
            UC = 0

            def qk(t):
                return view(arena, QKV_AT + t * 768, (HD, H), (1, HD))

            def qn(t):
                return view(arena, QN_AT + t * QK0, (HD, H), (1, HD))

            def tmp(t):
                return view(arena, TMP_AT + (t % 2) * QK0, (HD, H), (1, HD))

            gain = view(arena, GAIN_AT, (HD, H), (1, HD))
            rows = view(small, QSS, (H, TT), (1, H))

            with nc.Block() as block:
                @block.scalar
                def _(act):
                    for t in range(TT):
                        if t >= 2:
                            act.wait_ge(sem("qsum"), t - 1)
                        nc.scalar.activation(tmp(t), qk(t), ACT.Square).then_inc(sem("qsq"), 1)
                    act.wait_ge(sem("qvar"), 1)
                    nc.scalar.activation(rows, rows, ACT.Sqrt).then_inc(sem("qstd"), 1)
                    for t in range(TT):
                        act.wait_ge(sem("f1_ps"), t + 1)
                        norm = (SEQ * P) ** -0.5 if t < XT else (CTX * P) ** -0.5
                        b0 = 4 + 2 * (t % 2)
                        nc.scalar.activation(view(ring, UC + t * SLOT, (P, FG), (1, P)),
                                             bank(b0, 0, (2 * P, FG), (1, P)), ACT.Copy, scale=norm)
                        nc.scalar.activation(view(ring, UC + t * SLOT + 512, (P, FG), (1, P)),
                                             bank(b0, P, (2 * P, FG), (1, P)), ACT.Copy, scale=-norm
                                             ).then_inc(sem("f1_out"), 1)
                    for j in range(2 * FG):
                        act.wait_ge(sem("f2_ps"), j + 1)
                        t0, w = (0, SEQ) if j % 2 == 0 else (SEQ, CTX)
                        nc.scalar.activation(view(arena, FOUR_AT + (j // 2) * TOK + t0, (1, w)),
                                             bank(4 + j % 4, 0, (1, w)), ACT.Copy).then_inc(sem("f2_out"), 1)
                    for t in range(TT):
                        act.wait_ge(sem("qT_ps"), t + 1)
                        b0 = 2 * (t % 2)
                        nc.scalar.activation(view(arena, QT_AT + t * P, (TOK, 4), (1, P)),
                                             bank(b0, 0, (P, 4), (1, P)), ACT.Copy)
                        nc.scalar.activation(view(arena, KT0_AT + t * P, (1, P)),
                                             bank(b0 + 1, 0, (1, P)), ACT.Copy).then_inc(sem("qT_out"), 1)

                @block.vector
                def _(dve):
                    dve.wait_ge(sem("gain_in"), 16 * 11)
                    g_q = view(arena, GAIN_AT, (1, QH * HD))
                    nc.vector.tensor_scalar(g_q, g_q, HD ** -0.5, None, ALU.mult).then_inc(sem("gain_ready"), 1)
                    for t in range(TT):
                        dve.wait_ge(sem("qsq"), t + 1)
                        nc.vector.tensor_reduce(view(small, QSS + t * H, (1, H)), tmp(t), AX.X, ALU.add
                                                ).then_inc(sem("qsum"), 1)
                    dve.wait_ge(sem("qsum"), TT)
                    nc.vector.tensor_scalar(rows, rows, 1.0 / HD, EPS, ALU.mult, ALU.add).then_inc(sem("qvar"), 1)
                    dve.wait_ge(sem("qstd"), 1)
                    nc.vector.reciprocal(rows, rows).then_inc(sem("qrstd"), 1)
                    dve.wait_ge(sem("qrstd"), 1)
                    dve.wait_ge(sem("gain_ready"), 1)
                    step = 0
                    for t in range(TT):
                        nc.vector.tensor_tensor(qk(t), qk(t), view(small, QSS + t * H, (1, H), (0, HD)), ALU.mult
                                                ).then_inc(sem("qstep"), 1)
                        step += 1
                        dve.wait_ge(sem("qstep"), step)
                        if t >= XT:
                            nc.vector.tensor_tensor(qn(t), qk(t), gain, ALU.mult).then_inc(sem("qn_ready"), 1)
                            continue
                        nc.vector.tensor_tensor(qk(t), qk(t), gain, ALU.mult).then_inc(sem("qgained"), 1)
                        dve.wait_ge(sem("qgained"), t + 1)
                        nc.vector.tensor_tensor(qn(t), qk(t), view(ring, 22 * SLOT + t * P, (0, H), (1, HD)), ALU.mult
                                                ).then_inc(sem("qstep"), 1)
                        step += 1
                        dve.wait_ge(sem("qstep"), step)
                        dve.wait_ge(sem("rot"), 2 * (t + 1))
                        nc.vector.tensor_tensor(qn(t), qn(t), tmp(t), ALU.add).then_inc(sem("qn_ready"), 1)

                @block.gpsimd
                def _(pool):
                    pool.wait_ge(sem("qrstd"), 1)
                    for t in range(XT):
                        pool.wait_ge(sem("qgained"), t + 1)
                        if t >= 2:
                            pool.wait_ge(sem("qn_ready"), t - 1)
                        for half in range(2):
                            nc.gpsimd.tensor_tensor(
                                view(arena, TMP_AT + (t % 2) * QK0 + half * 32, (HD, H), (1, 32)),
                                view(arena, QKV_AT + t * 768 + (32 - half * 32), (HD, H), (1, 32)),
                                view(ring, 22 * SLOT + t * P + HD + half * 32, (0, H), (1, 32)),
                                ALU.mult).then_inc(sem("rot"), 1)

                @block.tensor
                def _(pe):
                    pe.wait_ge(sem("dft_in"), 32)
                    cos_t, sin_t = 10 * SLOT, 12 * SLOT
                    for t in range(TT):
                        if t >= 2:
                            pe.wait_ge(sem("f1_out"), t - 1)
                        for g in range(FG):
                            for s, tab in enumerate((cos_t, sin_t)):
                                last = nc.tensor.matmul(bank(4 + 2 * (t % 2), g * 2 * P + s * P, (1, P)),
                                                        view(arena, FT_AT + g * TOK + t * P, (1, P)),
                                                        view(ring, tab, (4, P)), start=True, stop=True)
                        last.then_inc(sem("f1_ps"), 1)
                    for j in range(2 * FG):
                        g, is_ctx = j // 2, j % 2
                        if j == 0:
                            pe.wait_ge(sem("f1_out"), TT)
                        if j >= 4:
                            pe.wait_ge(sem("f2_out"), j - 3)
                        tiles, w, st = ((0, 1, 2, 3), SEQ, 1) if not is_ctx else ((4, 5), CTX, 2)
                        n_mm = 2 * len(tiles)
                        i = 0
                        for s, tab in enumerate((cos_t, sin_t)):
                            for t in tiles:
                                last = nc.tensor.matmul(bank(4 + j % 4, 0, (1, w)),
                                                        view(ring, UC + t * SLOT + s * 512 + g * P, (1, P)),
                                                        view(ring, tab + (t - tiles[0]) * 512, (st, w)),
                                                        start=(i == 0), stop=(i == n_mm - 1))
                                i += 1
                        last.then_inc(sem("f2_ps"), 1)
                    for t in range(TT):
                        pe.wait_ge(sem("qn_ready"), t + 1)
                        if t >= 2:
                            pe.wait_ge(sem("qT_out"), t - 1)
                        for pr in range(5):
                            last = nc.tensor.transpose(bank(2 * (t % 2), pr * P, (1, P)),
                                                       view(arena, QN_AT + t * QK0 + pr * P, (1, P)), ident[:, :])
                        last.then_inc(sem("qT_ps"), 1)

        def attention(layer):
            n = f"a{layer}"
            if layer == 0:
                units = [(pr, t) for t in range(TT) for pr in range(4)]
                p_at, pt_at = P0_AT, PT0_AT
                p_w = 640
            else:
                units = [(pr, t) for pr in range(NH // 2) for t in range(XT)]
                p_at, pt_at = P1_AT, PT1_AT
                p_w = 512

            def chunks(t):
                if layer == 1:
                    return [(SEQ, None), (SEQ + P, None), (((t - 1) % XT) * P, None), (t * P, None)]
                keys = [(SEQ, None), (SEQ + P, None)]
                if t < XT:
                    keys.append((t * P, None))
                    if t > 0:
                        keys.append(((t - 1) * P, 0))
                    if t < XT - 1:
                        keys.append(((t + 1) * P, 1))
                return keys

            def wide(u):
                return len(chunks(units[u][1])) > 4

            def sc_bank(u, a):
                return 2 * a if wide(u) else 2 * (u % 2) + a

            def may_overlap(u):
                return not wide(u) and not wide(u - 1)

            def probs(u, a, col=0, *dims):
                return view(arena, p_at + ((u % 2) * 2 + a) * p_w + col, *(dims or ((1, P),)))

            def pt(a, col, w):
                return view(arena, pt_at + a * p_w + col, (1, w))

            def v_tile(key, pr, a):
                if layer == 0:
                    return view(arena, QKV_AT + (key // P) * 768 + QK0 + a * HD, (1, HD))
                return view(ring, (key // P) * SLOT + (2 * pr + a) * HD, (1, HD))

            def qT(pr, t, a):
                at, w = (QT_AT, TOK) if layer == 0 else (QT1_AT, SEQ)
                return view(arena, at + pr * w + t * P, (1, P), p=64 * a, n=64)

            def kT(pr, key, w, a):
                at = KT0_AT if layer == 0 else KT1_AT + pr * TOK
                return view(arena, at + key, (1, w), p=64 * a, n=64)

            ST = SOFT

            def st(u, what, a=0, w=1):
                return view(small, ST + (u % 2) * 16 + what * 2 + a, (1, w))

            MX, NEG, SUM, ES, REC, SHS = 0, 1, 2, 3, 4, 5
            O_BANKS = (7,) if layer == 0 else (6, 7)

            with nc.Block() as block:
                if layer == 0:
                    @block.sync
                    def _(sp):
                        load_even_out(sp)
                        for k in range(2):
                            ada_load(sp, "c", k)

                if layer == 1:
                    @block.sync
                    def _(sp):
                        for h in range(NH):
                            if h >= 2:
                                sp.wait_ge(sem("bm_read"), h - 1)
                            sp.dma_start(view(arena, BR1_AT + (h % 2) * 384, (1, 384)), rpb_pad[h]
                                         ).then_inc(sem(f"br_in{h % 2}"), 16)

                    @block.gpsimd
                    def _(pool):
                        pool.wait_ge(sem("na_mask_in"), 16)
                        for h in range(NH):
                            pr, a = h // 2, h % 2
                            pool.wait_ge(sem(f"br_in{h % 2}"), 16 * (h // 2 + 1))
                            if pr >= 2:
                                pool.wait_ge(sem("biased"), 4 * (pr - 1))
                            for v in range(3):
                                last = nc.gpsimd.tensor_tensor(
                                    view(arena, bm_at(pr) + (a * 3 + v) * 256, (64, 4), (8, 8), (1, 8)),
                                    view(arena, BR1_AT + (h % 2) * 384, (8, 4), (RPB_PAD, 8), (1, 8)),
                                    view(ring, 6 * SLOT + v * 256, (64, 4), (8, 8), (1, 8)), ALU.add)
                            last.then_inc(sem("bm_read"), 1)

                @block.tensor
                def _(pe):
                    def scores(u):
                        pr, t = units[u]
                        if u >= 1 and not may_overlap(u):
                            pe.wait_ge(sem("exp_done" + n), 2 * u)
                        elif u >= 2:
                            pe.wait_ge(sem("exp_done" + n), 2 * (u - 1))
                        keys = chunks(t)
                        segs = []
                        for i, (key, mask) in enumerate(keys):
                            if (segs and segs[-1][1] + segs[-1][2] == key and i * P % 512
                                    and segs[-1][3] is None and mask is None):
                                segs[-1][2] += P
                            else:
                                segs.append([i * P, key, P, mask])
                        for col, key, w, mask in segs:
                            for a in range(2):
                                last = nc.tensor.matmul(bank(sc_bank(u, a), col, (1, w)), qT(pr, t, a),
                                                        kT(pr, key, w, a), start=True, stop=mask is None,
                                                        skip_group_check=True)
                            if mask is not None:
                                for a in range(2):
                                    last = nc.tensor.matmul(bank(sc_bank(u, a), col, (1, w)), ident16[:, :],
                                                            view(swa_mask, mask * P, (1, P)), start=False, stop=True,
                                                            skip_group_check=True)
                        last.then_inc(sem("scores" + n), 1)

                    scores(0)
                    scored = 1
                    if may_overlap(1):
                        scores(1)
                        scored = 2
                    for u, (pr, t) in enumerate(units):
                        nk = len(chunks(t))
                        if scored == u + 1 < len(units):
                            scores(u + 1)
                            scored = u + 2
                        for a in range(2):
                            pe.wait_ge(sem("p_ready" + n), 2 * u + a + 1)
                            if u >= 1 and a == 0:
                                pe.wait_ge(sem("pt_act" + n), u)
                                pe.wait_ge(sem("pt_dve" + n), u)
                            for i in range(nk):
                                at = (4 + a, i * P) if i < 4 else (6, a * P)
                                last = nc.tensor.transpose(bank(at[0], at[1], (1, P)), probs(u, a, i * P), ident[:, :])
                            last.then_inc(sem("pt_ps" + n), 1)
                        if scored == u + 2 < len(units) and may_overlap(u + 2):
                            scores(u + 2)
                            scored = u + 3
                        pe.wait_ge(sem("pt_act" + n), u + 1)
                        pe.wait_ge(sem("pt_dve" + n), u + 1)
                        if u >= len(O_BANKS):
                            pe.wait_ge(sem("o_out" + n), u + 1 - len(O_BANKS))
                        for i, (key, _) in enumerate(chunks(t)):
                            for a in range(2):
                                last = nc.tensor.matmul(bank(O_BANKS[u % len(O_BANKS)], 0, (1, P), p=64 * a, n=64),
                                                        v_tile(key, pr, a), pt(a, i * P, P),
                                                        start=(i == 0), stop=(i == nk - 1))
                        last.then_inc(sem("o_ps" + n), 1)

                @block.vector
                def _(dve):
                    steps = [0]

                    def stepped(ins):
                        steps[0] += 1
                        ins.then_inc(sem("dstep" + n), 1)
                        dve.wait_ge(sem("dstep" + n), steps[0])

                    def pt_out(u):
                        w = len(chunks(units[u][1])) * P
                        dve.wait_ge(sem("pt_ps" + n), 2 * u + 2)
                        if u >= 1:
                            dve.wait_ge(sem("o_ps" + n), u)
                        nc.vector.tensor_copy(pt(1, 0, min(w, 512)), bank(5, 0, (1, min(w, 512)))
                                              ).then_inc(sem("pt_dve" + n), 1)

                    for u, (pr, t) in enumerate(units):
                        w = len(chunks(t)) * P
                        dve.wait_ge(sem("scores" + n), u + 1)
                        if layer == 1:
                            if t == 0:
                                dve.wait_ge(sem("bm_read"), 2 * pr + 2)
                            v = 0 if t == 0 else 2 if t == XT - 1 else 1
                            scr = bank(sc_bank(u, 0), 256, (512, 2), (1, 256))
                            nc.vector.tensor_tensor(scr, scr, view(arena, bm_at(pr) + v * 256, (768, 2), (1, 256)),
                                                    ALU.add).then_inc(sem("biased"), 1)
                            dve.wait_ge(sem("biased"), u + 1)
                        for a in range(2):
                            stepped(nc.vector.tensor_reduce(st(u, MX, a), bank(sc_bank(u, a), 0, (1, w)), AX.X,
                                                            ALU.max))
                            if layer == 0:
                                sk = view(small, SINK + pr + 4 * a, (1, 1))
                                stepped(nc.vector.tensor_tensor(st(u, MX, a), st(u, MX, a), sk, ALU.max))
                                stepped(nc.vector.tensor_tensor(st(u, SHS, a), sk, st(u, MX, a), ALU.subtract))
                            nc.vector.tensor_scalar(st(u, NEG, a), st(u, MX, a), -1.0, None, ALU.mult
                                                    ).then_inc(sem("neg" + n), 1)
                        if u >= 1:
                            pt_out(u - 1)
                        for a in range(2):
                            dve.wait_ge(sem("exp_done" + n), 2 * u + a + 1)
                            if layer == 0:
                                dve.wait_ge(sem("es" + n), 2 * u + a + 1)
                                stepped(nc.vector.tensor_tensor(st(u, SUM, a), st(u, SUM, a), st(u, ES, a), ALU.add))
                            stepped(nc.vector.reciprocal(st(u, REC, a), st(u, SUM, a)))
                            pp = probs(u, a, 0, (1, w))
                            nc.vector.tensor_scalar(pp, pp, st(u, REC, a), None, ALU.mult
                                                    ).then_inc(sem("p_ready" + n), 1)
                    pt_out(len(units) - 1)

                @block.scalar
                def _(act):
                    def tail(u):
                        pr, t = units[u]
                        w = len(chunks(t)) * P
                        act.wait_ge(sem("pt_ps" + n), 2 * u + (2 if w > 512 else 1))
                        if u >= 1:
                            act.wait_ge(sem("o_ps" + n), u)
                        last = nc.scalar.activation(pt(0, 0, min(w, 512)), bank(4, 0, (1, min(w, 512))), ACT.Copy)
                        if w > 512:
                            last = nc.scalar.activation(view(arena, pt_at + 512, (p_w, 2), (1, P)),
                                                        bank(6, 0, (P, 2), (1, P)), ACT.Copy)
                        last.then_inc(sem("pt_act" + n), 1)

                    def out_copy(u):
                        pr, t = units[u]
                        act.wait_ge(sem("o_ps" + n), u + 1)
                        if layer == 0:
                            nc.scalar.activation(view(arena, AT0_AT + pr * TOK + t * P, (1, P)),
                                                 bank(O_BANKS[u % len(O_BANKS)], 0, (1, P)), ACT.Copy
                                                 ).then_inc(sem("o_out" + n), 1)
                        else:
                            nc.scalar.activation(view(arena, AT1_AT + pr * SEQ + t * 16, (8, 2), (64, 8), (1, 8)),
                                                 bank(O_BANKS[u % len(O_BANKS)], 0, (64, 2), (8, 8), (1, 8)), ACT.Copy
                                                 ).then_inc(sem("o_out" + n), 1)

                    for u, (pr, t) in enumerate(units):
                        w = len(chunks(t)) * P
                        if u >= 2:
                            act.wait_ge(sem("pt_ps" + n), 2 * (u - 1))
                        for a in range(2):
                            act.wait_ge(sem("neg" + n), 2 * u + a + 1)
                            if layer == 0:
                                nc.scalar.activation(st(u, ES, a), st(u, SHS, a), ACT.Exp).then_inc(sem("es" + n), 1)
                            nc.scalar.activation(probs(u, a, 0, (1, w)), bank(sc_bank(u, a), 0, (1, w)), ACT.Exp,
                                                 bias=st(u, NEG, a), accum_out=st(u, SUM, a)
                                                 ).then_inc(sem("exp_done" + n), 1)
                        if u >= 2:
                            out_copy(u - 2)
                        if u >= 1:
                            tail(u - 1)
                    out_copy(len(units) - 2)
                    tail(len(units) - 1)
                    out_copy(len(units) - 1)

        def bm_at(pr):
            return BM1_AT if pr % 2 == 0 else BM1B_AT

        def out_proj(layer, prefetch=None):
            n = f"o{layer}"
            tiles = TT if layer == 0 else XT
            w_slot = 14 if layer == 0 else 8

            def lhsT(k, t):
                if layer == 0:
                    at = FOUR_AT + k * TOK if k < 4 else AT0_AT + (k - 4) * TOK
                    return view(arena, at + t * P, (1, P))
                return view(arena, AT1_AT + k * SEQ + t * P, (1, P))

            jobs = [(t, h) for t in range(tiles) for h in range(2)]
            with_ada = layer == 0
            BANKS = 5 if with_ada else 8
            with nc.Block() as block:
                @block.sync
                def _(sp):
                    for s in range(2 if tiles == TT else 1):
                        sp.dma_start(view(arena, GB_AT + s * D, (1, D)), mod_row(layer, s, G1)
                                     ).then_inc(sem("g_in" + n), 16)
                    load_modulation(sp, layer, 2)
                    if with_ada:
                        ada_bias_load(sp, "c")
                        for k in range(2, KT):
                            ada_load(sp, "c", k)
                        ada_save(sp, "c")
                    sp.dma_start(view(router, 0, (EXPERTS, KT), (1, EXPERTS)),
                                 router_w[layer].rearrange("(k p) e -> p k e", p=P)
                                 ).then_inc(sem(f"rt_in{layer}2"), 16)
                    if prefetch:
                        prefetch(sp)
                    if with_ada:
                        sp.wait_ge(sem("mods_c_out"), 16 * 4)

                @block.scalar
                def _(act):
                    square_sums(act, f"{layer}2", tiles, lambda t: act.wait_ge(sem("added" + n), 2 * t + 2))

                @block.tensor
                def _(pe):
                    pe.wait_ge(sem("evout_in" if layer == 0 else "odout_in"), 16 * (12 if layer == 0 else 8))
                    for j, (t, h) in enumerate(jobs):
                        if j >= BANKS:
                            pe.wait_ge(sem("gated" + n), j - BANKS + 1)
                        for k in range(KT):
                            last = nc.tensor.matmul(bank(j % BANKS), lhsT(k, t),
                                                    view(ring, (w_slot + k) * SLOT + h * 512, (1, 512)),
                                                    start=(k == 0), stop=(k == KT - 1))
                        last.then_inc(sem("y_ps" + n), 1)
                        if with_ada and j < KT:
                            ada_product(pe, "c", j)

                @block.vector
                def _(dve):
                    dve.wait_ge(sem("g_in" + n), 32 if tiles == TT else 16)
                    for j, (t, h) in enumerate(jobs):
                        if j == len(jobs) - 1:
                            mean_square(dve, f"{layer}2", 1, tiles)
                            inverse_rms(dve, f"{layer}2", 1, tiles)
                        dve.wait_ge(sem("y_ps" + n), j + 1)
                        if j >= 4:
                            dve.wait_ge(sem("added" + n), j - 3)
                        nc.vector.tensor_tensor(view(arena, YT_AT + (j % 4) * 512, (1, 512)), bank(j % BANKS),
                                                view(arena, GB_AT + (0 if t < XT else D) + h * 512, (1, 512)),
                                                ALU.mult).then_inc(sem("gated" + n), 1)
                        if with_ada and j == KT:
                            ada_sums(dve, "c")

                @block.gpsimd
                def _(pool):
                    for j, (t, h) in enumerate(jobs):
                        pool.wait_ge(sem("gated" + n), j + 1)
                        r = view(resid, t * D + h * 512, (1, 512))
                        nc.gpsimd.tensor_tensor(r, r, view(arena, YT_AT + (j % 4) * 512, (1, 512)), ALU.add
                                                ).then_inc(sem("added" + n), 1)

        IOTA = 12800
        META = IOTA + SEQ
        MT = META + 68
        IDX = MT + 768
        CUR = IDX + 384
        GX = CUR + 8
        XS = GX + 1536
        SX = XS + 1536
        HU = 2048
        SU = HU + 768
        HXT = SU + 768
        YX = HXT + 768
        YC = YX + D
        assert SX + 768 <= AFF_AT and AFF_AT + SEQ <= ARENA and YC + D <= AB_AT

        def top_k(layer):
            n = f"t{layer}"
            streams = [CAPX, CAPC] if layer == 0 else [CAPX]
            with nc.Block() as block:
                @block.sync
                def _(sp):
                    sp.dma_start(view(arena, IOTA, (1, SEQ)), iota_in.partition_broadcast(P)
                                 ).then_inc(sem("iota_in" + n), 16)
                    for s in range(len(streams)):
                        sp.dma_start(view(arena, G2_AT + s * D, (1, D)), mod_row(layer, s, G2)
                                     ).then_inc(sem("iota_in" + n), 16)
                    sp.wait_ge(sem("iota_in" + n), 16 + 16 * len(streams))

                @block.vector
                def _(dve):
                    step = [0]

                    def stepped(ins):
                        step[0] += 1
                        ins.then_inc(sem("tk" + n), 1)
                        dve.wait_ge(sem("tk" + n), step[0])

                    E = EXPERTS
                    stepped(nc.vector.memset(view(arena, MT, (1, 768), n=E), 0.0))
                    rows = 32 + E if layer == 0 else E
                    aff = view(arena, AFF_AT, (1, SEQ), n=rows)
                    for r in range(CAPX // 8):
                        val = view(arena, IDX + r * 8, (1, 8), n=rows)
                        idx = view(arena, IDX + 64 + r * 8, (1, 8), n=rows)
                        stepped(nc.vector.max(val, aff))
                        stepped(nc.vector.max_index(idx.bitcast(U32), val, aff))
                        stepped(nc.vector.match_replace(aff, val, aff, -1.0))
                    stepped(nc.vector.tensor_copy(view(arena, IDX + 128, (1, 64), n=rows),
                                                  view(arena, IDX + 64, (1, 64), n=rows).bitcast(U32)))
                    for s, cap in enumerate(streams):
                        reps = P // cap
                        num = view(arena, IDX + 128, (1, cap), p=32 * s, n=E)
                        val = view(arena, IDX, (1, cap), p=32 * s, n=E)
                        for q in range(reps):
                            stepped(nc.vector.tensor_copy(view(arena, MT + s * P + q * cap, (1, cap), n=E), num))
                            stepped(nc.vector.tensor_copy(view(arena, MT + (2 + s) * P + q * cap, (1, cap), n=E), val))
                            stepped(nc.vector.tensor_scalar(view(arena, MT + (4 + s) * P + q * cap, (1, cap), n=E),
                                                            num, float(reps), float(q), ALU.mult, ALU.add))
                    dve.wait_ge(sem("mt_ps" + n), 1)
                    stepped(nc.vector.tensor_copy(view(arena, META, (4, E), (1, 4)),
                                                  bank(0, 0, (1, E), (E, 4))))
                    stepped(nc.vector.tensor_copy(view(arena, META + 4 * E, (1, 4)), view(arena, META + 4 * E - 4, (1, 4))))
                    stepped(nc.vector.tensor_copy(view(offs, 0, (2, E), (1, 2)), bank(0, 4 * E, (1, E), (E, 2))))
                    stepped(nc.vector.tensor_copy(view(offs, 2 * E, (1, 2)), view(offs, 2 * E - 2, (1, 2))))

                @block.tensor
                def _(pe):
                    n_steps = 1 + 3 * (CAPX // 8) + 1 + sum(3 * (P // cap) for cap in streams)
                    pe.wait_ge(sem("tk" + n), n_steps)
                    for j in range(6):
                        last = nc.tensor.transpose(bank(0, j * EXPERTS, (1, EXPERTS)),
                                                   view(arena, MT + j * P, (1, P), n=EXPERTS),
                                                   ident[0:EXPERTS, 0:EXPERTS])
                    last.then_inc(sem("mt_ps" + n), 1)

        WCH = SLOTS // 2

        def expert_src(layer, e, ch):
            w = (exp_w_gate, exp_w_up, exp_w_down)[ch // 4]
            r0 = (ch % 4) * 2 * P
            if isinstance(e, int):
                return w[layer, e, r0:r0 + 2 * P, :].rearrange("(k p) n -> p k n", p=P)
            return w[layer, bass.ds(e, 1), r0:r0 + 2 * P, :].rearrange("e (k p) n -> p (e k) n", p=P)

        def ring_chunk(ch):
            return view(ring, ch * 2 * SLOT, (SLOT, 2), (1, SLOT))

        def load_first(layer, chunks):
            def go(sp):
                for ch in chunks:
                    sp.dma_start(ring_chunk(ch), expert_src(layer, 0, ch)).then_inc(sem(f"w{layer}_{ch}"), 16)
            return go

        def load_odd(sp, blocks):
            for cb in blocks:
                for k4 in range(2):
                    sp.dma_start(view(ring, cb * 4 * SLOT + k4 * 2048, (512, 4), (1, 512)),
                                 od_w_in[0, k4 * 512:(k4 + 1) * 512, cb * 512:(cb + 1) * 512]
                                 .rearrange("(k p) n -> p k n", p=P)).then_inc(sem(f"odin{cb}"), 16)

        def mixture(layer, early):
            n = f"m{layer}"
            has_c = layer == 0
            NC = 2 if has_c else 1
            sc_jobs = [(tt, half) for tt in range(TT if has_c else XT) for half in range(2)]
            SJ = len(sc_jobs)

            def tile_done(t):
                return 2 + (EXPERTS // 2) * SJ + 2 * t + 2

            def buf(at, par, s):
                return view(arena, at + par * 768 + (512 if s else 0), (1, 256 if s else 512))

            def cur(par, what):
                return view(arena, CUR + par * 4 + what, (1, 1))

            with nc.Block() as block:
                @block.sync
                def _(sp):
                    for ch in range(WCH):
                        if ch not in early:
                            sp.dma_start(ring_chunk(ch), expert_src(layer, 0, ch)).then_inc(sem(f"w{layer}_{ch}"), 16)
                    with nc.sync.Fori(0, EXPERTS - 1) as i:
                        for ch in range(WCH):
                            if ch in (7, 11):
                                used, freed = sem(("gu_ps" if ch == 7 else "y_ps") + n), i + 1
                            else:
                                used, freed = sem("w_used" + n), i * 10 + (ch + 1 if ch < 7 else ch)
                            freed = nc.sync.snap(freed)
                            src = expert_src(layer, nc.sync.snap(i + 1), ch)
                            sp.wait_ge(used, freed)
                            sp.dma_start(ring_chunk(ch), src).then_inc(sem(f"w{layer}_{ch}"), 16)
                    if layer == 0:
                        load_modulation(sp, 1, 1)
                        at = (EXPERTS - 1) * 10
                        freed = (("w_used", at + 2), ("w_used", at + 4), ("w_used", at + 6), ("gu_ps", EXPERTS),
                                 ("w_used", at + 9), ("y_ps", EXPERTS))
                        for cb, (used, count) in enumerate(freed):
                            sp.wait_ge(sem(used + n), count)
                            load_odd(sp, (cb,))
                    else:
                        for t in range(XT):
                            sp.wait_ge(sem("sc_add" + n), tile_done(t))
                            sp.dma_start(out[0, t * P:(t + 1) * P, :], view(resid, t * D, (1, D))
                                         ).then_inc(sem("out_done"), 16)
                        sp.wait_ge(sem("out_done"), 16 * XT)

                def gather(e):
                    par = e % 2
                    off = view(offs, e * 2, (1, 1))
                    nc.gpsimd.indirect_dma_start(buf(GX, par, 0), None, h2x.rearrange("t (h d) -> (t h) d", h=2),
                                                 bass.IndirectOffsetOnAxis(ap=off, axis=0)
                                                 ).then_inc(sem(f"gx{par}" + n), 16)
                    if has_c:
                        off = view(offs, e * 2 + 1, (1, 1))
                        nc.gpsimd.indirect_dma_start(buf(GX, par, 1), None, h2c.rearrange("t (q d) -> (t q) d", q=4),
                                                     bass.IndirectOffsetOnAxis(ap=off, axis=0)
                                                     ).then_inc(sem(f"gc{par}" + n), 16)

                @block.gpsimd
                def _(pool):
                    for e in range(EXPERTS + 1):
                        if e >= 2:
                            pool.wait_ge(sem("xs_ps" + n), e - 1)
                        if e >= 2 and has_c:
                            pool.wait_ge(sem("xc_ps" + n), e - 1)
                        gather(e)

                @block.tensor
                def _(pe):
                    def turn_x(par):
                        for j in range(4):
                            last = nc.tensor.transpose(bank(7, j * P, (1, P)), view(arena, GX + par * 768 + j * P, (1, P)),
                                                       ident[:, :])
                        last.then_inc(sem("xs_ps" + n), 1)

                    def turn_c(par):
                        for j in range(2):
                            last = nc.tensor.transpose(bank(2, j * P, (1, P)),
                                                       view(arena, GX + par * 768 + 512 + j * P, (1, P)), ident[:, :])
                        last.then_inc(sem("xc_ps" + n), 1)

                    def xs(par, k):
                        return view(arena, XS + par * 768 + (k % 4) * P + (k // 4) * 64, (1, 64))

                    def xsc(par, k):
                        return view(arena, XS + par * 768 + 512 + (k % 2) * P + (k // 2) * 32, (1, 32))

                    def hx(k):
                        return view(arena, HXT + (k % 4) * P + (k // 4) * 64, (1, 64))

                    def hc(k):
                        return view(arena, HXT + 512 + (k % 2) * P + (k // 2) * 32, (1, 32))

                    def dense(ch, k, lx, lc, bx, bc, cc):
                        w0 = (ch * 2 + k % 2) * SLOT
                        for half in range(2):
                            last = nc.tensor.matmul(bank(bx, 0, (1, 512), p=64 * half, n=64), lx,
                                                    view(ring, w0 + half * 512, (1, 512)),
                                                    start=(k == 0), stop=(k == KT - 1))
                        if has_c:
                            for q in range(4):
                                last = nc.tensor.matmul(bank(bc, cc, (1, 256), p=32 * q, n=32), lc,
                                                        view(ring, w0 + q * 256, (1, 256)),
                                                        start=(k == 0), stop=(k == KT - 1))
                        return last

                    def scatter(pair, job):
                        tt, half = sc_jobs[job]
                        if job == 0:
                            pe.wait_ge(sem("s_ready" + n), pair + 1)
                            pe.wait_ge(sem("y_out" + n), pair * 2 + 1)
                        if tt == XT and half == 0:
                            pe.wait_ge(sem("yc_out" + n), pair * 2 + 1)
                        pe.wait_ge(sem("sc_add" + n), pair * SJ + (job + 1))
                        if tt < XT:
                            lhsT = view(arena, SX + tt * P, (1, P))
                            rhs = view(arena, YX + half * 512, (1, 512))
                        else:
                            lhsT = view(arena, SX + 512 + (tt - XT) * P, (1, P), n=64)
                            rhs = view(arena, YC + half * 512, (1, 512), n=64)
                        nc.tensor.matmul(bank(5 + job % 2), lhsT, rhs, start=True, stop=True
                                         ).then_inc(sem("sc_ps" + n), 1)

                    pe.wait_ge(sem("gx0" + n), 16)
                    if has_c:
                        pe.wait_ge(sem("gc0" + n), 16)
                    turn_x(0)
                    if has_c:
                        turn_c(0)
                    with nc.tensor.Fori(0, EXPERTS // 2) as i:
                        for par in range(2):
                            e = i * 2 + par
                            pe.wait_ge(sem("xs_out" + n), e * NC + NC)
                            for m in range(2):
                                for ch in range(4 * m, 4 * m + 4):
                                    pe.wait_ge(sem(f"w{layer}_{ch}"), e * 16 + 16)
                                    for k in (2 * (ch % 4), 2 * (ch % 4) + 1):
                                        last = dense(ch, k, xs(par, k), xsc(par, k), m, (7, 2)[m], 256 * m)
                                    last.then_inc(sem(("w_used" if ch < 7 else "gu_ps") + n), 1)
                                    if par == 0 and 1 <= ch < 7:
                                        for job in (2 * ch - 2, 2 * ch - 1):
                                            if job < SJ:
                                                scatter(i, job)
                            pe.wait_ge(sem(f"gx{1 - par}" + n), i * 16 + (16 if par == 0 else 32))
                            if has_c:
                                pe.wait_ge(sem("silu" + n), e * NC + NC)
                            turn_x(1 - par)
                            pe.wait_ge(sem("h_ready" + n), e * NC + NC)
                            for j in range(4):
                                last = nc.tensor.transpose(bank(0, j * P, (1, P)), view(arena, HU + j * P, (1, P)),
                                                           ident[:, :])
                            if has_c:
                                for j in range(2):
                                    last = nc.tensor.transpose(bank(1, j * P, (1, P)),
                                                               view(arena, HU + 512 + j * P, (1, P)), ident[:, :])
                            last.then_inc(sem("hT_ps" + n), 1)
                            if has_c:
                                pe.wait_ge(sem(f"gc{1 - par}" + n), i * 16 + (16 if par == 0 else 32))
                                turn_c(1 - par)
                            pe.wait_ge(sem("hT_out" + n), e + 1)
                            if has_c:
                                pe.wait_ge(sem("hT_outc" + n), e + 1)
                            for ch in range(8, 12):
                                pe.wait_ge(sem(f"w{layer}_{ch}"), e * 16 + 16)
                                for k in (2 * (ch % 4), 2 * (ch % 4) + 1):
                                    last = dense(ch, k, hx(k), hc(k), 3, 4, 0)
                                last.then_inc(sem(("w_used" if ch < 11 else "y_ps") + n), 1)
                    for job in range(SJ):
                        scatter(EXPERTS // 2, job)

                @block.scalar
                def _(act):
                    def xs_out(par, e1):
                        act.wait_ge(sem("xs_ps" + n), e1)
                        nc.scalar.activation(buf(XS, par, 0), bank(7), ACT.Copy).then_inc(sem("xs_out" + n), 1)
                        if has_c:
                            act.wait_ge(sem("xc_ps" + n), e1)
                            nc.scalar.activation(buf(XS, par, 1), bank(2, 0, (1, 256)), ACT.Copy
                                                 ).then_inc(sem("xs_out" + n), 1)

                    xs_out(0, 1)
                    with nc.scalar.Fori(0, EXPERTS // 2) as i:
                        for par in range(2):
                            e = i * 2 + par
                            act.wait_ge(sem("w_used" + n), e * 10 + 4)
                            nc.scalar.activation(view(arena, SU, (1, 512)), bank(0), ACT.Silu).then_inc(sem("silu" + n), 1)
                            if has_c:
                                nc.scalar.activation(view(arena, SU + 512, (1, 256)), bank(7, 0, (1, 256)), ACT.Silu
                                                     ).then_inc(sem("silu" + n), 1)
                            act.wait_ge(sem("hT_ps" + n), e + 1)
                            nc.scalar.activation(view(arena, HXT, (1, 512)), bank(0), ACT.Copy).then_inc(sem("hT_out" + n), 1)
                            xs_out(1 - par, e + 2)
                    if layer == 0:
                        square_sums(act, "11", TT, lambda t: act.wait_ge(sem("sc_add" + n), tile_done(t)))

                @block.vector
                def _(dve):
                    def meta(e, par):
                        nc.vector.tensor_copy(view(arena, CUR + par * 4, (1, 4)), arena[:, bass.ds(e * 4 + META, 4)]
                                              ).then_inc(sem("cur" + n), 1)

                    def adds(pair, jobs=range(SJ)):
                        for job in jobs:
                            tt, half = sc_jobs[job]
                            dve.wait_ge(sem("sc_ps" + n), pair * SJ + (job + 1))
                            a = view(resid, tt * D + half * 512, (1, 512))
                            nc.vector.tensor_tensor(a, a, bank(5 + job % 2), ALU.add).then_inc(sem("sc_add" + n), 1)

                    nc.vector.memset(view(arena, YX, (1, D)), 0.0).then_inc(sem("y_out" + n), 1)
                    nc.vector.memset(view(arena, YC, (1, D)), 0.0).then_inc(sem("yc_out" + n), 1)
                    for third, signal in enumerate(("sc_add", "sc_add", "s_ready")):
                        nc.vector.memset(view(arena, SX + third * 256, (1, 256)), 0.0).then_inc(sem(signal + n), 1)
                    dve.wait_ge(sem("s_ready" + n), 1)
                    meta(0, 0)
                    with nc.vector.Fori(0, EXPERTS // 2) as i:
                        for par in range(2):
                            e = i * 2 + par
                            if par == 0:
                                adds(i)
                            else:
                                dve.wait_ge(sem("cur" + n), e + 1)
                                for s in range(NC):
                                    rows, w = (32, 256) if s else (64, 512)
                                    for a in range(2):
                                        last = nc.vector.tensor_scalar(
                                            view(arena, SX + s * 512, (1, w), p=rows * a, n=rows),
                                            view(arena, IOTA, (1, w), p=rows * a, n=rows),
                                            view(arena, CUR + a * 4 + s, (1, 1), p=rows * a, n=rows), None, ALU.is_equal)
                                last.then_inc(sem("s_ready" + n), 1)
                                dve.wait_ge(sem("s_ready" + n), i + 2)
                            dve.wait_ge(sem("silu" + n), e * NC + 1)
                            meta(nc.vector.snap(e + 1), 1 - par)
                            dve.wait_ge(sem("gu_ps" + n), e + 1)
                            nc.vector.tensor_tensor(view(arena, HU, (1, 512)), view(arena, SU, (1, 512)), bank(1), ALU.mult
                                                    ).then_inc(sem("h_ready" + n), 1)
                            if has_c:
                                dve.wait_ge(sem("silu" + n), e * NC + 2)
                                nc.vector.tensor_tensor(view(arena, HU + 512, (1, 256)), view(arena, SU + 512, (1, 256)),
                                                        bank(2, 256, (1, 256)), ALU.mult).then_inc(sem("h_ready" + n), 1)
                                dve.wait_ge(sem("hT_ps" + n), e + 1)
                                nc.vector.tensor_copy(view(arena, HXT + 512, (1, 256)), bank(1, 0, (1, 256))
                                                      ).then_inc(sem("hT_outc" + n), 1)
                            dve.wait_ge(sem("y_ps" + n), e + 1)
                            for half in range(2):
                                last = nc.vector.scalar_tensor_tensor(
                                    view(arena, YX + half * 512, (1, 512), p=64 * par, n=64),
                                    bank(3, 0, (1, 512), p=64 * half, n=64),
                                    view(arena, CUR + par * 4 + 2, (1, 1), p=64 * half, n=64),
                                    view(arena, G2_AT + half * 512, (1, 512), p=64 * half, n=64), ALU.mult, ALU.mult)
                            last.then_inc(sem("y_out" + n), 1)
                            if has_c:
                                for q in range(4):
                                    last = nc.vector.scalar_tensor_tensor(
                                        view(arena, YC + q * 256, (1, 256), p=32 * par, n=32),
                                        bank(4, 0, (1, 256), p=32 * q, n=32),
                                        view(arena, CUR + par * 4 + 3, (1, 1), p=32 * q, n=32),
                                        view(arena, G2_AT + D + q * 256, (1, 256), p=32 * q, n=32), ALU.mult, ALU.mult)
                                last.then_inc(sem("yc_out" + n), 1)
                    adds(EXPERTS // 2, range(SJ - 1))
                    if layer == 0:
                        mean_square(dve, "11", 1, TT)
                        inverse_rms(dve, "11", 1, TT)
                    adds(EXPERTS // 2, range(SJ - 1, SJ))

        def odd_in_proj():
            W1 = 832
            qk_jobs = [(cb, t) for cb in range(4) for t in range(XT if cb < 2 else TT)]
            v_jobs = [(cb, t) for cb in (4, 5) for t in range(TT)]
            jobs = qk_jobs + v_jobs
            NQ = len(qk_jobs)

            def hT_cols(cb, t):
                if t >= XT:
                    return 576 + (t - XT) * P
                return t * P if cb < 2 else t * P + 64

            def tm(j):
                return view(arena, TM1_AT + (j % 4) * 512, (HD, 8), (1, HD))

            def tmf(j):
                return view(arena, TM1_AT + (j % 4) * 512, (1, 512))

            RS = SOFT

            with nc.Block() as block:
                @block.sync
                def _(sp):
                    for s, g in enumerate((od_q_gain, od_k_gain)):
                        sp.dma_start(view(small, MISC + s * HD, (1, HD)), g[0].partition_broadcast(P)
                                     ).then_inc(sem("odgain_in"), 16)
                    sp.wait_ge(sem("od_ps"), 2 * XT + TT)
                    sp.dma_start(view(ring, 6 * SLOT, (1, 768)), na_mask_in).then_inc(sem("na_mask_in"), 16)
                    sp.wait_ge(sem("od_ps"), NQ)
                    for k in range(KT):
                        sp.dma_start(view(ring, (8 + k) * SLOT, (1, D)), od_w_out[0, k * P:(k + 1) * P, :]
                                     ).then_inc(sem("odout_in"), 16)

                @block.tensor
                def _(pe):
                    def project(j):
                        cb, t = jobs[j]
                        pe.wait_ge(sem(f"odin{cb}"), 32)
                        if j >= 4:
                            if j - 4 < NQ:
                                pe.wait_ge(sem("tm_in"), j - 3)
                            else:
                                pe.wait_ge(sem("v_out"), j - 4 - NQ + 1)
                        for k in range(KT):
                            last = nc.tensor.matmul(bank(j % 4), view(arena, HT_AT + k * W1 + hT_cols(cb, t), (1, P)),
                                                    view(ring, cb * 4 * SLOT + k * 512, (1, 512)),
                                                    start=(k == 0), stop=(k == KT - 1))
                        last.then_inc(sem("od_ps"), 1)

                    def turn(j):
                        pe.wait_ge(sem("qk_ready"), j + 1)
                        if j >= 2:
                            pe.wait_ge(sem("odT_out"), j - 1)
                        for i in range(4):
                            last = nc.tensor.transpose(bank(4 + j % 2, i * P, (1, P)),
                                                       view(arena, TM1_AT + (j % 4) * 512 + i * P, (1, P)), ident[:, :])
                        last.then_inc(sem("odT_ps"), 1)

                    for j in range(len(jobs)):
                        project(j)
                        if 2 <= j < NQ + 2:
                            turn(j - 2)

                @block.scalar
                def _(act):
                    def turned(j):
                        cb, t = jobs[j]
                        act.wait_ge(sem("odT_ps"), j + 1)
                        if cb < 2:
                            dst = view(arena, QT1_AT + cb * 4 * SEQ + t * P, (SEQ, 4), (1, P))
                        else:
                            dst = view(arena, KT1_AT + (cb - 2) * 4 * TOK + t * P, (TOK, 4), (1, P))
                        nc.scalar.activation(dst, bank(4 + j % 2, 0, (P, 4), (1, P)), ACT.Copy
                                             ).then_inc(sem("odT_out"), 1)

                    for j in range(len(jobs)):
                        act.wait_ge(sem("od_ps"), j + 1)
                        cb, t = jobs[j]
                        if j < NQ:
                            if j >= 4:
                                act.wait_ge(sem("odT_ps"), j - 3)
                            nc.scalar.activation(tmf(j), bank(j % 4), ACT.Copy).then_inc(sem("tm_in"), 1)
                            if j >= 2:
                                act.wait_ge(sem("odsum"), j - 1)
                            act.wait_ge(sem("tm_in"), j + 1)
                            nc.scalar.activation(view(arena, PT1_AT - 512 + (j % 2) * 512, (1, 512)), tmf(j),
                                                 ACT.Square).then_inc(sem("odsq"), 1)
                            if j >= 1:
                                act.wait_ge(sem("odvar"), j)
                                s = view(small, RS + ((j - 1) % 4) * 8, (1, 8))
                                nc.scalar.activation(s, s, ACT.Sqrt).then_inc(sem("odstd"), 1)
                        else:
                            if j == NQ:
                                act.wait_ge(sem("odvar"), NQ)
                                s = view(small, RS + ((NQ - 1) % 4) * 8, (1, 8))
                                nc.scalar.activation(s, s, ACT.Sqrt).then_inc(sem("odstd"), 1)
                            nc.scalar.activation(view(ring, t * SLOT + (cb - 4) * 512, (1, 512)), bank(j % 4), ACT.Copy
                                                 ).then_inc(sem("v_out"), 1)
                        if 2 <= j < NQ + 2:
                            turned(j - 2)

                @block.vector
                def _(dve):
                    dve.wait_ge(sem("odgain_in"), 32)
                    gq = view(small, MISC, (1, HD))
                    nc.vector.tensor_scalar(gq, gq, HD ** -0.5, None, ALU.mult).then_inc(sem("odgain"), 1)
                    dve.wait_ge(sem("odgain"), 1)

                    def finish(j):
                        s = view(small, RS + (j % 4) * 8, (1, 8))
                        dve.wait_ge(sem("odstd"), j + 1)
                        nc.vector.reciprocal(s, s).then_inc(sem("odrstd"), 1)
                        dve.wait_ge(sem("odrstd"), j + 1)
                        nc.vector.tensor_tensor(tm(j), tm(j), view(small, RS + (j % 4) * 8, (1, 8), (0, HD)), ALU.mult
                                                ).then_inc(sem("odmul"), 1)
                        dve.wait_ge(sem("odmul"), j + 1)
                        g = view(small, MISC + (0 if jobs[j][0] < 2 else HD), (0, 8), (1, HD))
                        nc.vector.tensor_tensor(tm(j), tm(j), g, ALU.mult).then_inc(sem("qk_ready"), 1)

                    for j in range(NQ):
                        s = view(small, RS + (j % 4) * 8, (1, 8))
                        dve.wait_ge(sem("odsq"), j + 1)
                        nc.vector.tensor_reduce(s, view(arena, PT1_AT - 512 + (j % 2) * 512, (HD, 8), (1, HD)), AX.X,
                                                ALU.add).then_inc(sem("odsum"), 1)
                        dve.wait_ge(sem("odsum"), j + 1)
                        nc.vector.tensor_scalar(s, s, 1.0 / HD, EPS, ALU.mult, ALU.add).then_inc(sem("odvar"), 1)
                        if j >= 1:
                            finish(j - 1)
                    finish(NQ - 1)

        stages = [
            lambda: ada_stage(),
            lambda: norm_stage(0, 1, TT, lambda sp: load_even_in(sp, range(EARLY_K, KT))),
            lambda: even_in_proj(),
            lambda: even_qk_fourier(),
            lambda: attention(0),
            lambda: out_proj(0, load_first(0, range(0, 6))),
            lambda: norm_stage(0, 2, TT, load_first(0, range(6, 12))),
            lambda: top_k(0),
            lambda: mixture(0, range(0, 12)),
            lambda: norm_stage(1, 1, TT),
            lambda: odd_in_proj(),
            lambda: attention(1),
            lambda: out_proj(1, load_first(1, range(8, 12))),
            lambda: norm_stage(1, 2, XT, load_first(1, range(0, 8))),
            lambda: top_k(1),
            lambda: mixture(1, range(0, 12)),
        ]
        for number, stage in enumerate(stages):
            if number == 9:
                kept = {"ab0_in11", "ab1_in11", "sq_done11", "var_ready11", "std_ready11", "rstd_ready11"} | {f"odin{cb}" for cb in range(6)}
                nc.clear_and_free_semaphores([sems.pop(name) for name in list(sems) if name not in kept])
                nc.all_engine_barrier()
            stage()


def shape_constants():
    n = np.arange(SEQ)
    ang = 2.0 * np.pi * ((n[:, None] * n[None, :]) % SEQ) / SEQ
    dft = np.stack([np.cos(ang), np.sin(ang)]).astype(np.float32)
    inv = np.power(np.float32(10000.0), -np.arange(16, dtype=np.float32) / np.float32(16)).astype(np.float32)
    row, col = (n // GRID_W).astype(np.float32), (n % GRID_W).astype(np.float32)
    a = np.concatenate([row[:, None] * inv, col[:, None] * inv], axis=-1)
    co, si = np.cos(a).astype(np.float32), np.sin(a).astype(np.float32)
    rope = np.concatenate([co, co, -si, si], axis=1).astype(np.float32)
    i, j = np.arange(P)[:, None], np.arange(P)[None, :]
    swa = np.concatenate([np.where(j >= i, 0.0, -1e30), np.where(j <= i, 0.0, -1e30)], axis=1).astype(np.float32)
    na = np.zeros((P, 3, 256), np.float32)
    p, key = np.arange(P), np.arange(256)
    for v, t in enumerate((0, 1, 3)):
        cq = 16 * t + 8 * (p // 64) + p % 8
        ck = 16 * t - 8 + 8 * (key // 64) + key % 8
        start = np.clip(cq - NA_COLS // 2, 0, GRID_W - NA_COLS)
        ok = (ck[None, :] >= start[:, None]) & (ck[None, :] < start[:, None] + NA_COLS)
        na[:, v] = np.where(ok, 0.0, -1e30)
    return {"dft": dft, "rope": rope, "ident": np.eye(P, dtype=np.float32), "swa_mask": swa,
            "na_mask": na.reshape(P, 768), "iota": np.arange(SEQ, dtype=np.float32)}


def layout(inputs):
    a = {k: np.ascontiguousarray(np.asarray(v)) for k, v in inputs.items()}
    a["c"] = a["c"].reshape(D)
    rpb = a.pop("od_rpb")[0]
    wide = np.zeros((NH, RPB_R, RPB_PAD), rpb.dtype)
    wide[:, :, 8:8 + RPB_C] = rpb
    flat = np.concatenate([wide.reshape(NH, -1), np.zeros((NH, RPB_PAD), rpb.dtype)], axis=1)
    p = np.arange(P)
    start = (7 - (p // 8) % 8) * RPB_PAD + 15 - (8 * (p // 64) + p % 8)
    a["rpb_pad"] = np.stack([flat[:, s:s + 8 * RPB_PAD] for s in start], axis=1)
    a.update(shape_constants())
    return a


_INS = ["x", "c", "ctx", "c_ctx", "ada_w", "ada_b", "norm1_g", "norm2_g", "router_w", "exp_w_gate", "exp_w_up",
        "exp_w_down", "ev_w_in", "ev_w_out", "ev_q_gain", "ev_k_gain", "ev_sink", "od_w_in", "od_w_out",
        "od_q_gain", "od_k_gain", "rpb_pad", "dft", "rope", "ident", "swa_mask", "na_mask", "iota"]


def kernel(**inputs):
    import concourse.bacc as bacc
    from concourse.bass_utils import run_bass_kernel_spmd

    a = layout(inputs)
    nc = bacc.Bacc("TRN2", target_bir_lowering=False, num_devices=1)
    arrays, args = {}, []
    for name in _INS:
        arrays[f"in_{name}"] = np.ascontiguousarray(a[name])
        args.append(nc.dram_tensor(f"in_{name}", a[name].shape, mybir.dt.from_np(a[name].dtype),
                                   kind="ExternalInput").ap())
    args.append(nc.dram_tensor("out_x", (1, SEQ, D), F32, kind="ExternalOutput").ap())
    program(nc, *args)
    r = run_bass_kernel_spmd(nc, [arrays], core_ids=[0])
    return r.results[0]["out_x"]
```
